# Optimizing a Trainium2 kernel written in Bass

```python
import functools
import jax, jax.numpy as jnp
from jax import lax
import numpy as np

D_MODEL = 1024
BATCH = 1
SEQ = 128
DEPTH = 1
DEC_BATCH = 1
DEC_SEQ = 512
PAST_LEN = 256

GRID_W = 64
MIX_WIDTH = D_MODEL
ATTN_WIDTH = MIX_WIDTH // 2
N_HEADS = 8
HEAD_DIM = ATTN_WIDTH // N_HEADS
SGU_WIDTH = MIX_WIDTH - ATTN_WIDTH
SGU_GROUPS = 4
SGU_GROUP_DIM = SGU_WIDTH // SGU_GROUPS
CHUNK = 128
WIN_H_MAX = 8
WIN_W = 16
Q_BLOCK = 128
IN_WIDTH = 3 * ATTN_WIDTH + 2 * SGU_WIDTH
N_EXPERTS = 16
N_EXPERT_GROUPS = 4
EXPERTS_PER_GROUP = N_EXPERTS // N_EXPERT_GROUPS
TOP_K = 2
D_EXPERT = 256
EPS = 1e-6
NEG = -1e30

kernel_name = "hybrid_natten_sgu_moe_diffusion_step"

def _rms_norm(x, w):
    xf = x.astype(jnp.float32)
    y = xf * lax.rsqrt(jnp.mean(xf * xf, axis=-1, keepdims=True) + EPS)
    return (y * w.astype(jnp.float32)).astype(x.dtype)

def _layer_norm(x, w, b):
    xf = x.astype(jnp.float32)
    mu = jnp.mean(xf, axis=-1, keepdims=True)
    var = jnp.mean(jnp.square(xf - mu), axis=-1, keepdims=True)
    y = (xf - mu) * lax.rsqrt(var + EPS)
    return (y * w.astype(jnp.float32) + b.astype(jnp.float32)).astype(x.dtype)

def _adaln(cond, w_ada, b_ada):
    m = jax.nn.silu(cond) @ w_ada + b_ada
    return jnp.split(m, 6, axis=-1)

def _context_attention(q, k, v):
    B, L, H, Dh = q.shape
    nb = L // Q_BLOCK
    qb = q.reshape(B, nb, Q_BLOCK, H, Dh).transpose(1, 0, 2, 3, 4)
    scale = HEAD_DIM ** -0.5

    def block(qi):
        s = jnp.einsum('bqhd,bkhd->bhqk', qi, k).astype(jnp.float32) * scale
        p = jax.nn.softmax(s, axis=-1).astype(v.dtype)
        return jnp.einsum('bhqk,bkhd->bqhd', p, v)

    o = lax.map(block, qb)
    return o.transpose(1, 0, 2, 3, 4).reshape(B, L, H * Dh)

def _neighbourhood_attention(q, k, v, k_ctx, v_ctx, rpb):
    B, L, H, Dh = q.shape
    rows = L // GRID_W
    win_h = min(WIN_H_MAX, rows)
    scale = HEAD_DIM ** -0.5
    qg = q.reshape(B, rows, GRID_W, H, Dh).transpose(1, 0, 2, 3, 4)
    kg = k.reshape(B, rows, GRID_W, H, Dh)
    vg = v.reshape(B, rows, GRID_W, H, Dh)
    cols = jnp.arange(GRID_W)
    col_start = jnp.clip(cols - WIN_W // 2, 0, GRID_W - WIN_W)
    col_mask = (cols[None, :] >= col_start[:, None]) & (cols[None, :] < col_start[:, None] + WIN_W)
    col_idx = jnp.clip(cols[None, :] - cols[:, None] + WIN_W - 1, 0, 2 * WIN_W - 2)
    rpb_c = rpb.astype(jnp.float32)[:, :, col_idx]
    row_start = jnp.clip(jnp.arange(rows) - win_h // 2, 0, rows - win_h)

    def row_block(args):
        q_r, r = args
        rs = row_start[r]
        k_band = lax.dynamic_slice_in_dim(kg, rs, win_h, axis=1)
        v_band = lax.dynamic_slice_in_dim(vg, rs, win_h, axis=1)
        row_idx = rs + jnp.arange(win_h) - r + WIN_H_MAX - 1
        bias = rpb_c[:, row_idx].transpose(0, 2, 1, 3)
        s_win = jnp.einsum('bqhd,bjkhd->bhqjk', q_r, k_band).astype(jnp.float32) * scale + bias[None]
        s_win = jnp.where(col_mask[:, None, :], s_win, NEG)
        s_ctx = jnp.einsum('bqhd,bchd->bhqc', q_r, k_ctx).astype(jnp.float32) * scale
        n_win = win_h * GRID_W
        s = jnp.concatenate([s_win.reshape(B, H, GRID_W, n_win), s_ctx], axis=-1)
        p = jax.nn.softmax(s, axis=-1).astype(v.dtype)
        p_win = p[..., :n_win].reshape(B, H, GRID_W, win_h, GRID_W)
        p_ctx = p[..., n_win:]
        return (jnp.einsum('bhqjk,bjkhd->bqhd', p_win, v_band)
                + jnp.einsum('bhqc,bchd->bqhd', p_ctx, v_ctx))

    o = lax.map(row_block, (qg, jnp.arange(rows)))
    return o.transpose(1, 0, 2, 3, 4).reshape(B, L, H * Dh)

def _spatial_gating(gu, gv, w_s, b_s, ln_w, ln_b):
    B, L, _ = gu.shape
    nc = L // CHUNK
    u = jax.nn.gelu(gu).reshape(B, nc, CHUNK, SGU_GROUPS, SGU_GROUP_DIM)
    vv = _layer_norm(jax.nn.gelu(gv).reshape(B, nc, CHUNK, SGU_GROUPS, SGU_GROUP_DIM), ln_w, ln_b)
    sv = jnp.einsum('gpq,bnqgc->bnpgc', w_s, vv) + b_s.T[:, :, None]
    return (u * sv).reshape(B, L, SGU_WIDTH)

def _moe(h, w_router, b_router, w1, w3, w2):
    B, L, D = h.shape
    t = h.reshape(B * L, D)
    s = jax.nn.sigmoid((t @ w_router).astype(jnp.float32))
    sel = s + b_router.astype(jnp.float32)
    g_score = lax.top_k(sel.reshape(-1, N_EXPERT_GROUPS, EXPERTS_PER_GROUP), 2)[0].sum(-1)
    best = jnp.argmax(g_score, axis=-1)
    e_mask = (jnp.arange(N_EXPERTS)[None, :] // EXPERTS_PER_GROUP) == best[:, None]
    _, idx = lax.top_k(jnp.where(e_mask, sel, NEG), TOP_K)
    w_sel = jnp.take_along_axis(s, idx, axis=-1)
    w_sel = w_sel / jnp.sum(w_sel, axis=-1, keepdims=True)
    gates = jnp.sum(jax.nn.one_hot(idx, N_EXPERTS, dtype=jnp.float32) * w_sel[..., None], axis=1)
    hid = jax.nn.silu(jnp.einsum('td,edf->tef', t, w1)) * jnp.einsum('td,edf->tef', t, w3)
    hid = hid * gates.astype(hid.dtype)[..., None]
    return jnp.einsum('tef,efd->td', hid, w2).reshape(B, L, D)

def _trunk_layer(x, cond, attend, lp, w_router, b_router):
    (w_ada, b_ada, norm1_w, norm2_w, w_in, q_norm_w, k_norm_w,
     w_sgu, b_sgu, sgu_ln_w, sgu_ln_b, w_out, w1, w3, w2) = lp
    sh1, sc1, g1, sh2, sc2, g2 = _adaln(cond, w_ada, b_ada)
    B, L, _ = x.shape
    h = _rms_norm(x, norm1_w) * (1 + sc1) + sh1
    p = h @ w_in
    q, k, v, gu, gv = jnp.split(
        p, [ATTN_WIDTH, 2 * ATTN_WIDTH, 3 * ATTN_WIDTH, 3 * ATTN_WIDTH + SGU_WIDTH], axis=-1)
    q = _rms_norm(q.reshape(B, L, N_HEADS, HEAD_DIM), q_norm_w)
    k = _rms_norm(k.reshape(B, L, N_HEADS, HEAD_DIM), k_norm_w)
    v = v.reshape(B, L, N_HEADS, HEAD_DIM)
    a = attend(q, k, v)
    sg = _spatial_gating(gu, gv, w_sgu, b_sgu, sgu_ln_w, sgu_ln_b)
    x = x + g1 * (jnp.concatenate([a, sg], axis=-1) @ w_out)
    h2 = _rms_norm(x, norm2_w) * (1 + sc2) + sh2
    x = x + g2 * _moe(h2, w_router, b_router, w1, w3, w2)
    return x, k, v

def setup_inputs(seed: int = 0) -> dict:
    key = jax.random.key(seed)
    ks = jax.random.split(key, 26)
    f32 = jnp.float32

    def nrm(k, shape, scale):
        return jax.random.normal(k, shape, f32) * scale

    D = D_MODEL
    kv_shape = (DEC_BATCH, DEPTH, PAST_LEN, N_HEADS, HEAD_DIM)
    return {
        "x_prompt": nrm(ks[0], (BATCH, SEQ, D), 1.0),
        "x_sample": nrm(ks[1], (DEC_BATCH, DEC_SEQ, D), 1.0),
        "cache_k": nrm(ks[2], kv_shape, 1.0),
        "cache_v": nrm(ks[3], kv_shape, 1.0),
        "c": nrm(ks[4], (DEC_BATCH, D), 1.0),
        "c_ctx": nrm(ks[5], (D,), 1.0),
        "w_ada": nrm(ks[6], (DEPTH, D, 6 * D), 0.5 * D ** -0.5),
        "b_ada": nrm(ks[7], (DEPTH, 6 * D), 0.02),
        "norm1_w": 1.0 + nrm(ks[8], (DEPTH, D), 0.02),
        "norm2_w": 1.0 + nrm(ks[9], (DEPTH, D), 0.02),
        "w_in": nrm(ks[10], (DEPTH, D, IN_WIDTH), D ** -0.5),
        "q_norm_w": 1.0 + nrm(ks[11], (DEPTH, HEAD_DIM), 0.02),
        "k_norm_w": 1.0 + nrm(ks[12], (DEPTH, HEAD_DIM), 0.02),
        "rpb": nrm(ks[13], (DEPTH, N_HEADS, 2 * WIN_H_MAX - 1, 2 * WIN_W - 1), 0.1),
        "w_sgu": nrm(ks[14], (DEPTH, SGU_GROUPS, CHUNK, CHUNK), CHUNK ** -0.5),
        "b_sgu": 1.0 + nrm(ks[15], (DEPTH, SGU_GROUPS, CHUNK), 0.1),
        "sgu_ln_w": 1.0 + nrm(ks[16], (DEPTH, SGU_GROUPS, SGU_GROUP_DIM), 0.02),
        "sgu_ln_b": nrm(ks[17], (DEPTH, SGU_GROUPS, SGU_GROUP_DIM), 0.02),
        "w_out": nrm(ks[18], (DEPTH, MIX_WIDTH, D), MIX_WIDTH ** -0.5),
        "w_router": nrm(ks[19], (D, N_EXPERTS), D ** -0.5),
        "b_router": nrm(ks[20], (N_EXPERTS,), 0.01),
        "w1": nrm(ks[21], (DEPTH, N_EXPERTS, D, D_EXPERT), D ** -0.5),
        "w3": nrm(ks[22], (DEPTH, N_EXPERTS, D, D_EXPERT), D ** -0.5),
        "w2": nrm(ks[23], (DEPTH, N_EXPERTS, D_EXPERT, D), D_EXPERT ** -0.5),
    }

def reference(x_prompt, x_sample, cache_k, cache_v, c, c_ctx, w_ada, b_ada, norm1_w, norm2_w,
              w_in, q_norm_w, k_norm_w, rpb, w_sgu, b_sgu, sgu_ln_w, sgu_ln_b, w_out,
              w_router, b_router, w1, w3, w2):
    xp = x_prompt
    xs = x_sample
    c_lat = c[:, None, :]
    ks, vs = [], []
    for l in range(DEPTH):
        lp = (w_ada[l], b_ada[l], norm1_w[l], norm2_w[l], w_in[l], q_norm_w[l], k_norm_w[l],
              w_sgu[l], b_sgu[l], sgu_ln_w[l], sgu_ln_b[l], w_out[l], w1[l], w3[l], w2[l])
        xp, k_l, v_l = _trunk_layer(xp, c_ctx, _context_attention, lp, w_router, b_router)
        ks.append(k_l)
        vs.append(v_l)
        attend = functools.partial(_neighbourhood_attention, k_ctx=cache_k[:, l],
                                   v_ctx=cache_v[:, l], rpb=rpb[l])
        xs, _, _ = _trunk_layer(xs, c_lat, attend, lp, w_router, b_router)
    new_k = jnp.stack(ks, axis=1)
    new_v = jnp.stack(vs, axis=1)
    return (xp, xs, new_k, new_v)


_drawn_inputs = setup_inputs


def setup_inputs(seed=0):
    import zlib

    import numpy as np

    out = dict(_drawn_inputs(seed))
    spreads = {}
    factors = {'cache_k': 2.786,
     'norm1_w': 3.099,
     'q_norm_w': 29.331,
     'k_norm_w': 9.838,
     'rpb': 26.789,
     'sgu_ln_w': 22.547,
     'sgu_ln_b': 23.019,
     'norm2_w': 8.0,
     'b_sgu': 4.397,
     'b_router': 5.76}
    for name, (base, spread) in spreads.items():
        noise = np.random.default_rng([zlib.crc32(name.encode()), seed]).standard_normal(out[name].shape)
        drawn = base * np.exp(spread * noise) if base else spread * noise
        out[name] = __import__('jax').numpy.asarray(drawn.astype(out[name].dtype))
    for name, factor in factors.items():
        out[name] = (out[name] * factor).astype(out[name].dtype)
    return out
```

```python
from contextlib import ExitStack

import concourse.bass as bass
from concourse import mybir

F32 = mybir.dt.float32
U32 = mybir.dt.uint32
I32 = mybir.dt.int32
ALU = mybir.AluOpType
ACT = mybir.ActivationFunctionType
X = mybir.AxisListType.X

P = 128
D = 1024
KD = D // P
GRID_W, GRID_H = 64, 8
HEADS, HD = 8, 64
AW = HEADS * HD
GROUPS = 4
TILES = 5
TOK = TILES * P
CTX, LAT = 0, 1
COLS = P // GRID_H
CACHE = 256
WIN_W, HALF_W = 16, 8
RPB_W = 2 * WIN_W - 1
RPB_H = 2 * GRID_H - 1
RPB_PAD = 16
RUN = (GRID_H - 1) * RPB_W + 3 * COLS
EXPERTS, EG, EPG = 16, 4, 4
DE = 256
MAX_BLOCKS = 26
MIN_BLOCKS = 2 * TOK // P
NEG = -1e30
EPS = 1e-6
CHUNK = KD * 512
RING = 4

INNER, LEFT_EDGE, RIGHT_EDGE = 0, 3, 5


def build(nc, t_in, t_out):
    (x_prompt, x_sample, cache_kt, cache_v, c, c_ctx, w_ada, b_ada, norm1_w, norm2_w, w_in, q_norm_w,
     k_norm_w, rpb_runs, w_sgu_t, b_sgu, ln_w, ln_b, w_out, w_router, b_router, w1, w3, w2) = t_in
    y_prompt, y_sample, new_k, new_v = t_out
    ctx = ExitStack()
    with ctx:
        def sb(name, shape, dt=F32):
            return ctx.enter_context(nc.sbuf_tensor(name, shape, dt))

        def sem(name):
            return ctx.enter_context(nc.semaphore(name))

        ada_rows = nc.dram_tensor("ada_rows", (6, 2, D), F32, kind="Internal").ap()
        h2_rows = nc.dram_tensor("h2_rows", (TOK, D), F32, kind="Internal").ap()
        slot_out = nc.dram_tensor("slot_out", (MAX_BLOCKS * P, D), F32, kind="Internal").ap()

        big = sb("big", [P, RING * CHUNK + KD * TOK])
        ring = [big[:, s * CHUNK:(s + 1) * CHUNK].rearrange("p (k n) -> p k n", k=KD) for s in range(RING)]
        catT = big[:, RING * CHUNK:].rearrange("p (k n) -> p k n", k=KD)
        hT_rows = catT[:, :, 0:4 * P]
        w13 = ring[0:2]
        w2s = [big[:, (2 * CHUNK + s * 2 * D):(2 * CHUNK + (s + 1) * 2 * D)].rearrange("p (k n) -> p k n", k=2)
               for s in range(2)]
        y_in = [[big[:, (4 * i + 2 * j) * D:(4 * i + 2 * j + 1) * D] for j in range(2)] for i in range(2)]
        y_fin = [big[:, (4 * i + 1) * D:(4 * i + 2) * D] for i in range(2)]

        hu = sb("hu", [P, KD * TOK + GROUPS * TOK])
        hT = hu[:, 0:KD * TOK].rearrange("p (k n) -> p k n", k=KD)
        uT = hu[:, KD * TOK:].rearrange("p (g n) -> p g n", g=GROUPS)
        bm = hu[:, 0:HEADS * 7 * P].rearrange("p (h v n) -> p h v n", h=HEADS, v=7)
        bc = hu[:, 0:6 * D].rearrange("p (v c n) -> p v c n", v=3, c=2)

        vvr = sb("vvr", [P, TILES * AW])
        vv = vvr[:, :].rearrange("p (t n) -> p t n", t=TILES)
        slab = vvr[:, 0:HEADS * RUN].rearrange("p (h n) -> p h n", h=HEADS)
        hg = [vvr[:, s * D:(s + 1) * D] for s in range(2)]

        qk = sb("qk", [P, 5 * D])
        x_sb = qk[:, :].rearrange("p (t n) -> p t n", t=TILES)
        qT = qk[:, 0:4 * TOK].rearrange("p (k n) -> p k n", k=4)
        kT = qk[:, 4 * TOK:8 * TOK].rearrange("p (k n) -> p k n", k=4)

        vr = sb("vr", [P, TILES * AW])
        v_sb = vr[:, :].rearrange("p (t n) -> p t n", t=TILES)
        h2 = [vr[:, s * D:(s + 1) * D] for s in range(2)]
        hgT = vr[:, 0:D].rearrange("p (k n) -> p k n", k=KD)
        sil = vr[:, D:D + DE]
        hid = [vr[:, D + (1 + s) * DE:D + (2 + s) * DE] for s in range(2)]
        hidT = vr[:, D + 3 * DE:D + 4 * DE].rearrange("p (k n) -> p k n", k=2)

        cc = sb("cc", [P, 4 * CACHE + 2 * AW])
        ckT = cc[:, 0:4 * CACHE].rearrange("p (k n) -> p k n", k=4)
        cv = cc[:, 4 * CACHE:].rearrange("p (t n) -> p t n", t=2)
        g1b = cc[:, :].rearrange("p (c n) -> p c n", c=2)

        xt = sb("xt", [P, 2 * D])
        junk = xt[:, 0:D]
        masks = xt[:, D:D + 7 * P].rearrange("p (v n) -> p v n", v=7)
        probs = [xt[:, s * 640:(s + 1) * 640] for s in range(2)]
        win = [xt[:, 1280 + s * 384:1280 + (s + 1) * 384] for s in range(2)]

        po = sb("po", [P, 2 * D])
        bias_row = po[0:2, 0:D]
        n2_row = po[0:2, D:2 * D]
        pT = [po[:, s * 640:(s + 1) * 640].rearrange("p (j n) -> p j n", j=5) for s in range(2)]
        o_row = po[:, 1280:1280 + AW]
        h2T = po[:, 0:D].rearrange("p (k n) -> p k n", k=KD)

        rs = sb("rs", [P, 4 * 512])
        raw = [rs[:, s * 512:(s + 1) * 512] for s in range(2)]
        sq = [rs[:, (2 + s) * 512:(3 + s) * 512] for s in range(2)]
        y_sb = rs[:, 0:D]
        wr_sb = sb("wr_sb", [P, KD, EXPERTS])
        ada_row = sb("ada_row", [2, D])
        norms = sb("norms", [P, 6 * 512])
        qw, kw, lnw, lnb, bsg, wsT = [norms[:, s * 512:(s + 1) * 512] for s in range(6)]
        ident = sb("ident", [P, P])
        before = sb("before", [P, P])
        ones = sb("ones", [P, P])
        zero = sb("zero", [P, 256])
        small = sb("small", [P, 400])
        at = [0]

        def cut(n, shape=None, dt=F32):
            a = small[:, at[0]:at[0] + n]
            at[0] += n
            a = a if dt == F32 else a.bitcast(dt)
            return a if shape is None else a.rearrange(shape[0], **shape[1])

        cond = cut(16, ("p (c k) -> p c k", dict(c=2)))
        silT = cut(16, ("p (k c) -> p k c", dict(c=2)))
        bcol = cut(16, ("p (v k) -> p v k", dict(v=2)))
        n1w = cut(8)
        colB = cut(16, ("p (k c) -> p k c", dict(c=2)))
        colA = cut(16, ("p (k c) -> p k c", dict(c=2)))
        xss, xms, xr = cut(5), cut(5), cut(5)
        mean, ssq, msq, rsq = cut(4), [cut(8) for _ in range(2)], [cut(8) for _ in range(2)], [cut(8) for _ in range(2)]
        mhalf = cut(8)
        m_win, m_ctx, nmax = [cut(2) for _ in range(3)]
        sums = cut(32, ("p (b h c) -> p b h c", dict(b=2, c=2)))
        rsum = cut(8)
        tokid = cut(5)
        brt = cut(16)
        gates = cut(10, ("p (k t) -> p k t", dict(k=2)))
        slot_u = cut(10, None, U32)
        gidx = cut(28, None, U32)
        ebi = cut(28, None, I32)
        held = cut(3)
        idx1 = [cut(1, None, U32) for _ in range(2)]
        r_at = [0]

        def rcut(n):
            a = norms[:, r_at[0]:r_at[0] + n]
            r_at[0] += n
            return a

        banks = [ctx.enter_context(nc.psum_tensor(f"bank{i}", [P, 512], F32)) for i in range(8)]

        cond_in, small_in, x_in, norms_in, cache_in, slab_in = [sem(n) for n in (
            "cond_in", "small_in", "x_in", "norms_in", "cache_in", "slab_in")]
        ring_in = [sem(f"ring_in{s}") for s in range(RING)]
        zero_ready, slots_zeroed, bias_ready = sem("zero_ready"), sem("slots_zeroed"), sem("bias_ready")
        by_row, ones_ready, n2_in, consts_ready, rstd_ready, norm_rstd_ready, n_rstd2 = [sem(n) for n in (
            "by_row", "ones_ready", "n2_in", "consts_ready", "rstd_ready", "norm_rstd_ready", "n_rstd2")]
        silu_ready, ada_done, ada_copied, col_done, cols_ready = [sem(n) for n in (
            "silu_ready", "ada_done", "ada_copied", "col_done", "cols_ready")]
        ss_ready, ms_ready, xn_ready, xT_done, hT_ready = [sem(n) for n in (
            "ss_ready", "ms_ready", "xn_ready", "xT_done", "hT_ready")]
        proj_done, proj_out, raw_ready, raw_normed, nT_done, nT_copied, normed_ms = [sem(n) for n in (
            "proj_done", "proj_out", "raw_ready", "raw_normed", "nT_done", "nT_copied", "normed_ms")]
        new_out, sgu_done, sgu_out, row_in, row_ready, row_out = [sem(n) for n in (
            "new_out", "sgu_done", "sgu_out", "row_in", "row_ready", "row_out")]
        bm_ready, scored, win_ready, nmax_ready, exp_done, pT_done, pT_dve, pT_act = [sem(n) for n in (
            "bm_ready", "scored", "win_ready", "nmax_ready", "exp_done", "pT_done", "pT_dve", "pT_act")]
        pv_done, o_ready, aT_done, aT_copied = [sem(n) for n in ("pv_done", "o_ready", "aT_done", "aT_copied")]
        x_again, g1_in, bc_in, wout_done, x1_ready, ss2_ready, ms2_ready, h2_ready, h2_stored = [sem(n) for n in (
            "x_again", "g1_in", "bc_in", "wout_done", "x1_ready", "ss2_ready", "ms2_ready", "h2_ready", "h2_stored")]
        h2_out = [sem(f"h2_out{s}") for s in range(2)]
        h2T_done, h2T_act, h2T_dve, z_done, s_ready, m_ready, ranks_done, hot_ready, inv_done, table_ready = [
            sem(n) for n in ("h2T_done", "h2T_act", "h2T_dve", "z_done", "s_ready", "m_ready", "ranks_done",
                             "hot_ready", "inv_done", "table_ready")]
        w13_in = [sem(f"w13_in{s}") for s in range(2)]
        w2_in = [sem(f"w2_in{s}") for s in range(2)]
        hg_in = [sem(f"hg_in{s}") for s in range(2)]
        hgT_done, hgT_act, hgT_dve, w13_done, silu_done, hid_ready, hidT_done, hidT_ready = [sem(n) for n in (
            "hgT_done", "hgT_act", "hgT_dve", "w13_done", "silu_done", "hid_ready", "hidT_done", "hidT_ready")]
        y_done, y_act, y_dve, y_stored, idx_ready = [sem(n) for n in (
            "y_done", "y_act", "y_dve", "y_stored", "idx_ready")]
        back_in = [sem(f"back_in{s}") for s in range(2)]
        fin_ready, fin_mid = sem("fin_ready"), sem("fin_mid")
        fin_out = [sem(f"fin_out{s}") for s in range(2)]
        dve_step, pool_step, act_step = [sem(n) for n in ("dve_step", "pool_step", "act_step")]

        chunks = [("ada", j) for j in range(4)] + [("in", j) for j in (0, 1, 2, 4, 3)] \
            + [("ada", j) for j in range(4, 12)] + [("out", j) for j in range(2)]
        chunk_at = {key: n for n, key in enumerate(chunks)}
        ada_v = w_ada.rearrange("(p k) n -> p k n", k=KD)
        in_v = w_in.rearrange("(p k) n -> p k n", k=KD)
        out_v = w_out.rearrange("(k p) n -> p k n", k=KD)

        def tile_rows(prompt, sample, t):
            return prompt if t == 0 else sample[(t - 1) * P:t * P]

        proj = [(0, "q", t) for t in range(TILES)] + [(1, "k", t) for t in range(TILES)] \
            + [(2, "v", t) for t in range(TILES)] + [(4, "gv", t) for t in range(TILES)] \
            + [(3, "gu", (g, w)) for g in range(GROUPS) for w in (CTX, LAT)]
        rows = [n for n, p in enumerate(proj) if p[1] in ("q", "k", "gv")]
        row_no = {n: i for i, n in enumerate(rows)}

        def positions(ap, t):
            if t == 0:
                return ap[:, :, 0:P].rearrange("p k (r c) -> p k r c", r=2)
            v = ap[:, :, P:].rearrange("p k (c r) -> p k r c", r=GRID_H)
            return v[:, :, 2 * (t - 1):2 * t, :]

        steps = [(t, h) for t in range(TILES) for h in range(HEADS)]

        def span(t):
            i = t - 1
            lo, hi = max(i - 1, 0), min(i + 1, 3)
            return lo, hi - lo + 1, (LEFT_EDGE if i == 0 else RIGHT_EDGE if i == 3 else INNER)

        def key_tiles(t):
            return 1 if t == 0 else span(t)[1] + 2

        def used(key):
            kind, j = key
            if kind == "ada":
                return ada_done, j + 1
            if kind == "in":
                return proj_done, max(n for n, p in enumerate(proj) if p[0] == j) + 1
            return wout_done, 2 * TILES - 1 + j

        TE = TILES * EXPERTS
        scores_s = rcut(TE)
        sel, msel, tmp, hot1, hot2, both, rank = [rcut(TE) for _ in range(7)]
        pair = rcut(TILES * EG * 6)
        gsc, ghot, gtmp, gdesc = [rcut(TILES * EG) for _ in range(4)]
        desc = rcut(EXPERTS)
        t5a, t5b = rcut(TILES), rcut(TILES)
        gate_s = rcut(10)
        nb, bend, bstart = [rcut(EXPERTS) for _ in range(3)]
        blk_edge = rcut(27)
        slotf, blkf, inf = rcut(10), rcut(10), rcut(10)
        iota_b = rcut(28)
        iota_p = rcut(P)
        ebf = rcut(28)
        cmp_e = rcut(28 * EXPERTS)
        hot_b = rcut(10 * 28)
        assert r_at[0] <= 6 * 512
        cmp_b = cmp_e[:, 0:10 * 27]
        hot_s = rs[:, 0:10 * P]

        block = ctx.enter_context(nc.Block())

        @block.sync
        def _(sp):
            for n, (kind, j) in enumerate(chunks):
                if n >= RING:
                    sp.wait_ge(*used(chunks[n - RING]))
                src = {"ada": ada_v, "in": in_v, "out": out_v}[kind]
                sp.dma_start(ring[n % RING], src[:, :, 512 * j:512 * (j + 1)]).then_inc(ring_in[n % RING], 16)
            sp.wait_ge(zero_ready, 1)
            fill = slot_out[MIN_BLOCKS * P:].rearrange("(p b) (v n) -> p (b v) n", p=P, n=256)
            sp.dma_start(fill, zero[:].unsqueeze(1).to_broadcast((P, fill.shape[1], 256))).then_inc(slots_zeroed, 16)
            for t in range(TILES):
                sp.wait_ge(h2_ready, t + 1)
                sp.dma_start(h2_rows[t * P:(t + 1) * P], h2[t % 2]).then_inc(h2_out[t % 2], 16)
            sp.wait_ge(table_ready, 1)
            sp.wait_ge(wout_done, 2 * TILES)
            more = sp.value_load(ebi[0:1, 27:28], min_val=4, max_val=MAX_BLOCKS // 2 - 1)

            def load(p, b):
                e = sp.value_load(ebi[0:1, bass.ds(b, 1)], min_val=0, max_val=EXPERTS - 1)
                for src, off in ((w1, 0), (w3, DE)):
                    sp.dma_start(w13[p][:, :, off:off + DE], src[bass.ds(e, 1)].rearrange(
                        "e (p k) f -> p (e k) f", k=KD)).then_inc(w13_in[p], 16)
                return e

            def load2(p, e):
                sp.dma_start(w2s[p], w2[bass.ds(e, 1)].rearrange("e (p k) n -> p (e k) n", k=2)).then_inc(w2_in[p], 16)

            load2(0, load(0, 0))
            load2(1, load(1, 1))
            with sp.Fori(0, more) as i:
                for p in range(2):
                    sp.wait_ge(w13_done, 2 * i + p + 1)
                    e = load(p, 2 * i + p + 2)
                    sp.wait_ge(y_done, 2 * i + p + 1)
                    load2(p, e)

        @block.gpsimd
        def _(pool):
            steps_done = [0]

            def link(ins):
                steps_done[0] += 1
                ins.then_inc(pool_step, 1)
                pool.wait_ge(pool_step, steps_done[0])

            with nc.allow_non_contiguous_dma(reason="columns of the conditioning"):
                pool.dma_start(cond[:, 0, :], c_ctx.rearrange("(p k) -> p k", k=KD)).then_inc(cond_in, 16)
                pool.dma_start(cond[:, 1, :], c.rearrange("(p k) -> p k", k=KD)).then_inc(cond_in, 16)
                pool.dma_start(x_sb[:, 0, :], x_prompt).then_inc(x_in, 16)
                pool.dma_start(x_sb[:, 1:, :], x_sample.rearrange("(t p) d -> p t d", p=P)).then_inc(x_in, 16)
                pool.dma_start(bcol, b_ada[0:2 * D].rearrange("(v p k) -> p v k", p=P, k=KD)).then_inc(small_in, 16)
                pool.dma_start(n1w, norm1_w.rearrange("(p k) -> p k", k=KD)).then_inc(small_in, 16)
            nc.gpsimd.memset(zero[:], 0.0).then_inc(zero_ready, 1)
            nc.gpsimd.memset(ones[:], 1.0).then_inc(ones_ready, 1)
            pool.wait_ge(ones_ready, 1)
            nc.gpsimd.memset(mhalf, -0.5).then_inc(consts_ready, 1)
            nc.gpsimd.affine_select(out=ident[:], in_=ones[:], pattern=[[-1, P]], compare_op=ALU.is_equal,
                                    fill=0.0, base=0, channel_multiplier=1).then_inc(consts_ready, 1)
            nc.gpsimd.affine_select(out=before[:], in_=ones[:], pattern=[[1, P]], compare_op=ALU.is_gt,
                                    fill=0.0, base=0, channel_multiplier=-1).then_inc(consts_ready, 1)
            pool.wait_ge(consts_ready, 3)
            pool.wait_ge(ms_ready, 1)
            nc.gpsimd.tensor_tensor(xr, xms, mhalf[:, 0:5], ALU.pow).then_inc(rstd_ready, 1)
            pool.dma_start(qw.rearrange("p (h d) -> p h d", h=HEADS),
                           q_norm_w.partition_broadcast(P).unsqueeze(1).to_broadcast((P, HEADS, HD))).then_inc(norms_in, 16)
            pool.dma_start(kw.rearrange("p (h d) -> p h d", h=HEADS),
                           k_norm_w.partition_broadcast(P).unsqueeze(1).to_broadcast((P, HEADS, HD))).then_inc(norms_in, 16)
            pool.dma_start(lnw, ln_w.partition_broadcast(P)).then_inc(norms_in, 16)
            pool.dma_start(lnb, ln_b.partition_broadcast(P)).then_inc(norms_in, 16)
            pool.dma_start(bsg, b_sgu.partition_broadcast(P)).then_inc(norms_in, 16)
            pool.dma_start(wsT, w_sgu_t).then_inc(norms_in, 16)
            pool.dma_start(ckT, cache_kt).then_inc(cache_in, 16)
            pool.dma_start(cv, cache_v.rearrange("(t p) d -> p t d", p=P)).then_inc(cache_in, 16)
            pool.dma_start(wr_sb[:], w_router.rearrange("(p k) n -> p k n", k=KD)).then_inc(cache_in, 16)
            pool.dma_start(brt, b_router.partition_broadcast(P)).then_inc(cache_in, 16)
            pool.dma_start(bias_row, b_ada[2 * D:3 * D].partition_broadcast(2)).then_inc(row_in, 16)
            pool.dma_start(n2_row, norm2_w.partition_broadcast(2)).then_inc(n2_in, 16)
            for half in range(2):
                ks = slice(4 * half, 4 * half + 4)
                pool.wait_ge(hT_ready, 12 + 4 * half)
                nc.gpsimd.tensor_copy(hT_rows[:, ks, :].rearrange("p k (r c) -> p k r c", c=GRID_W),
                                      hT[:, ks, P:].rearrange("p k (c r) -> p k r c", r=GRID_H)).then_inc(by_row, 1)
            for i, n in enumerate(rows):
                w = 4 if proj[n][1] == "gv" else HEADS
                pool.wait_ge(normed_ms, i + 1)
                nc.gpsimd.tensor_tensor(rsq[i % 2][:, 0:w], msq[i % 2][:, 0:w], mhalf[:, 0:w],
                                        ALU.pow).then_inc(norm_rstd_ready, 1)
            for v in range(3, 6):
                pool.wait_ge(ada_copied, 2 * v)
                pool.dma_start(bias_row, b_ada[v * D:(v + 1) * D].partition_broadcast(2)).then_inc(row_in, 16)
            pool.wait_ge(sgu_done, TILES)
            pool.dma_start(slab, rpb_runs).then_inc(slab_in, 16)
            pool.wait_ge(slab_in, 16)
            pool.wait_ge(sgu_out, TILES)
            def mask(piece, rel, side, src):
                first = GRID_H * COLS * rel
                link(nc.gpsimd.affine_select(
                    out=masks[:, piece, :], in_=src, pattern=[[side * GRID_H, COLS], [0, GRID_H]],
                    compare_op=ALU.is_ge, fill=NEG,
                    base=(first + GRID_H * HALF_W + GRID_H - 1) if side > 0 else GRID_H * (HALF_W - 1) - first,
                    channel_multiplier=-side))

            mask(RIGHT_EDGE, -1, 1, zero[:, 0:P])
            mask(LEFT_EDGE, 0, 1, zero[:, 0:P])
            mask(RIGHT_EDGE + 1, 0, -1, zero[:, 0:P])
            mask(LEFT_EDGE + 1, 1, -1, zero[:, 0:P])
            mask(INNER, -1, 1, zero[:, 0:P])
            mask(INNER + 1, 0, -1, masks[:, LEFT_EDGE, :])
            mask(INNER + 2, 1, -1, zero[:, 0:P])
            for piece, rel in ((0, -1), (1, 0), (2, 1), (3, 0), (4, 1), (5, -1), (6, 0)):
                keys = bass.AP(slab.tensor, slab.offset + COLS * (rel + 1),
                               [slab.ap[0], slab.ap[1], (1, COLS), (RPB_W, GRID_H)])
                nc.gpsimd.tensor_tensor(
                    bm[:, :, piece, :].rearrange("p h (c r) -> p h c r", r=GRID_H), keys,
                    masks[:, piece, :].rearrange("p (c r) -> p c r", r=GRID_H).unsqueeze(1).to_broadcast(
                        (P, HEADS, COLS, GRID_H)), ALU.add).then_inc(bias_ready, 1)
            for out, step, base, per_row in ((desc, -1, EXPERTS, 0), (iota_b, 1, 0, 0), (iota_p, 1, 0, 0),
                                             (blk_edge, P, P, 0), (tokid, P, 0, 1)):
                nc.gpsimd.iota(out, pattern=[[step, out.shape[1]]], base=base, channel_multiplier=per_row,
                               allow_small_or_imprecise_dtypes=True).then_inc(bm_ready, 1)
            pool.wait_ge(row_out, 16 * 4)
            pool.wait_ge(scored, len(steps))
            pool.wait_ge(pv_done, len(steps))
            for cnd in range(2):
                pool.dma_start(g1b[:, cnd, :], ada_rows[2, cnd].partition_broadcast(P)).then_inc(g1_in, 16)
            for t in range(TILES):
                pool.dma_start(x_sb[:, t, :], tile_rows(x_prompt, x_sample, t)).then_inc(x_again, 16)
            pool.wait_ge(win_ready, len(steps) - HEADS)
            for cnd in range(2):
                for v in range(3):
                    pool.dma_start(bc[:, v, cnd, :], ada_rows[3 + v, cnd].partition_broadcast(P)).then_inc(bc_in, 16)
            for t in range(TILES):
                pool.wait_ge(ms2_ready, t + 1)
                nc.gpsimd.tensor_tensor(xr[:, t:t + 1], xms[:, t:t + 1], mhalf[:, 0:1], ALU.pow).then_inc(n_rstd2, 1)
            pool.wait_ge(h2_out[0], 16 * 3)
            pool.wait_ge(h2_out[1], 16 * 2)
            pool.wait_ge(table_ready, 1)
            more = pool.value_load(ebi[0:1, 27:28], min_val=4, max_val=MAX_BLOCKS // 2 - 1)

            def hold(i):
                nc.gpsimd.tensor_tensor(held[:, i:i + 1], mhalf[:, 0:1], mhalf[:, 0:1], ALU.mult)

            def gather(b, p):
                nc.gpsimd.tensor_copy(idx1[p], gidx[:, bass.ds(b, 1)]).then_inc(idx_ready, 1)
                pool.wait_ge(idx_ready, b + 1)
                hold(p)
                nc.gpsimd.indirect_dma_start(out=hg[p], out_offset=None, in_=h2_rows,
                                             in_offset=bass.IndirectOffsetOnAxis(ap=idx1[p], axis=0)
                                             ).then_inc(hg_in[p], 16)

            gather(0, 0)
            gather(1, 1)
            with pool.Fori(0, more) as i:
                for p in range(2):
                    pool.wait_ge(hgT_done, 2 * i + p + 1)
                    gather(2 * i + p + 2, p)
            pool.wait_ge(y_stored, 32 * more + 48)
            hold(2)
            for t in range(TILES):
                if t >= 2:
                    pool.wait_ge(fin_mid, t - 1)
                for j in range(2):
                    nc.gpsimd.indirect_dma_start(
                        out=y_in[t % 2][j], out_offset=None, in_=slot_out,
                        in_offset=bass.IndirectOffsetOnAxis(ap=slot_u[:, 2 * t + j:2 * t + j + 1], axis=0)
                    ).then_inc(back_in[t % 2], 16)

        @block.scalar
        def _(act):
            act.wait_ge(cond_in, 32)
            nc.scalar.activation(silT.rearrange("p k c -> p c k"), cond, ACT.Silu).then_inc(silu_ready, 1)
            act.wait_ge(x_in, 32)
            for t in range(TILES):
                if t:
                    act.wait_ge(ss_ready, t)
                nc.scalar.activation(junk, x_sb[:, t, :], ACT.Square, accum_out=xss[:, t:t + 1]).then_inc(ss_ready, 1)
            act.wait_ge(cols_ready, 2)
            for half in range(2):
                act.wait_ge(xT_done, half + 1)
                for k in range(4 * half, 4 * half + 4):
                    nc.scalar.activation(hT[:, k, 0:P], banks[half][:, (k % 4) * P:(k % 4 + 1) * P], ACT.Identity,
                                         scale=colA[:, k, CTX:CTX + 1], bias=colB[:, k, CTX:CTX + 1]).then_inc(hT_ready, 1)
            for k in range(KD):
                act.wait_ge(xT_done, k + 3)
                nc.scalar.activation(hT[:, k, P:], banks[(k + 2) % 4][:], ACT.Identity,
                                     scale=colA[:, k, LAT:LAT + 1], bias=colB[:, k, LAT:LAT + 1]).then_inc(hT_ready, 1)
            for n, (_, kind, t) in enumerate(proj):
                out = banks[n % 4]
                act.wait_ge(proj_done, n + 1)
                i = row_no.get(n)
                if i is not None and i >= 2:
                    act.wait_ge(raw_normed, i - 1)
                    if proj[rows[i - 2]][1] in ("q", "k"):
                        act.wait_ge(nT_done, i - 1)
                    if proj[rows[i - 2]] == (1, "k", 0):
                        act.wait_ge(new_out, 16)
                if kind in ("q", "k"):
                    nc.scalar.activation(sq[i % 2], out[:], ACT.Square).then_inc(raw_ready, 1)
                    nc.scalar.activation(raw[i % 2], out[:], ACT.Copy).then_inc(proj_out, 1)
                elif kind == "v":
                    nc.scalar.activation(v_sb[:, t, :], out[:], ACT.Copy).then_inc(proj_out, 1)
                elif kind == "gv":
                    nc.scalar.activation(raw[i % 2], out[:], ACT.Gelu_apprx_tanh).then_inc(proj_out, 1)
                else:
                    g, w = t
                    lo, hi = (0, P) if w == CTX else (P, TOK)
                    nc.scalar.activation(uT[:, g, lo:hi], out[:, 0:hi - lo], ACT.Gelu_apprx_tanh).then_inc(proj_out, 1)
                if kind == "k" and t == 1:
                    act.wait_ge(raw_normed, TILES + 1)
                    act.dma_start(new_k, raw[TILES % 2]).then_inc(new_out, 16)
                if kind == "v" and t == 0:
                    act.wait_ge(proj_out, n + 1)
                    act.dma_start(new_v, v_sb[:, 0, :]).then_inc(new_out, 16)
            for v in range(4):
                act.wait_ge(ada_copied, 2 * v + 6)
                if v == 2:
                    act.wait_ge(row_ready, 1)
                act.dma_start(ada_rows[2 + v], ada_row[:, :]).then_inc(row_out, 16)
            def softmax(n):
                t, h = steps[n]
                bank = 2 * (n % 2)
                nk = key_tiles(t)
                act.wait_ge(nmax_ready, n + 1)
                if n >= 2:
                    act.wait_ge(pT_done, n - 1)
                if h == 0 and t >= 2:
                    act.wait_ge(o_ready, t - 1)
                w = 0
                if t:
                    w = span(t)[1] * P
                    nc.scalar.activation(probs[n % 2][:, 0:w], win[n % 2][:, 0:w], ACT.Exp, bias=nmax[:, n % 2:n % 2 + 1],
                                         accum_out=sums[:, t % 2, h, 0:1]).then_inc(act_step, 1)
                    src = banks[bank + 1][:, 0:CACHE]
                else:
                    src = banks[bank + 1][:, 0:P]
                nc.scalar.activation(probs[n % 2][:, w:nk * P], src, ACT.Exp, bias=nmax[:, n % 2:n % 2 + 1],
                                     accum_out=sums[:, t % 2, h, 1:2]).then_inc(exp_done, 1)

            def copy_pT(n):
                t, h = steps[n]
                k4 = min(key_tiles(t), 3)
                act.wait_ge(pT_done, n + 1)
                if n >= 2:
                    act.wait_ge(pv_done, n - 1)
                nc.scalar.activation(pT[n % 2][:, 0:k4, :], banks[4][:, 0:k4 * P].rearrange("p (j n) -> p j n", n=P),
                                     ACT.Copy).then_inc(pT_act, 1)

            for n in range(len(steps) + 1):
                if n < len(steps):
                    softmax(n)
                if n >= 1:
                    copy_pT(n - 1)
            for t in range(TILES):
                act.wait_ge(x1_ready, 2 * (t + 1))
                nc.scalar.activation(junk, x_sb[:, t, :], ACT.Square, accum_out=xss[:, t:t + 1]).then_inc(ss2_ready, 1)
                act.wait_ge(ss2_ready, t + 1)
                act.wait_ge(h2T_done, t + 1)
                if t:
                    act.wait_ge(z_done, t)
                nc.scalar.activation(h2T[:, 0:4, :], banks[4][:].rearrange("p (j n) -> p j n", n=P),
                                     ACT.Copy).then_inc(h2T_act, 1)
            act.wait_ge(z_done, TILES)
            nc.scalar.activation(scores_s, banks[6][:, 0:TILES * EXPERTS], ACT.Sigmoid).then_inc(s_ready, 1)
            act.wait_ge(table_ready, 1)
            more = act.value_load(ebi[0:1, 27:28], min_val=4, max_val=MAX_BLOCKS // 2 - 1)

            def copy_hgT(b):
                act.wait_ge(hgT_done, b + 1)
                act.wait_ge(w13_done, b)
                nc.scalar.activation(hgT[:, 0:4, :], banks[4][:].rearrange("p (j n) -> p j n", n=P),
                                     ACT.Copy).then_inc(hgT_act, 1)

            def silu(b, p):
                act.wait_ge(w13_done, b + 1)
                act.wait_ge(hid_ready, b + 1)
                nc.scalar.activation(sil, banks[6 + p][:, 0:DE], ACT.Silu).then_inc(silu_done, 1)

            def store(b):
                act.wait_ge(y_done, b + 1)
                act.wait_ge(y_stored, 16 * (b + 1))
                nc.scalar.activation(y_sb[:, 0:512], banks[0][:], ACT.Copy).then_inc(y_act, 1)
                act.wait_ge(y_act, b + 1)
                act.wait_ge(y_dve, b + 1)
                act.dma_start(slot_out[bass.ds(b * P, P)], y_sb).then_inc(y_stored, 16)

            act.nop().then_inc(y_stored, 16)
            act.wait_ge(slots_zeroed, 16)
            act.wait_ge(hgT_done, 1)
            nc.scalar.activation(hgT[:, 0:4, :], banks[4][:].rearrange("p (j n) -> p j n", n=P),
                                 ACT.Copy).then_inc(hgT_act, 1)
            act.wait_ge(w13_done, 1)
            nc.scalar.activation(sil, banks[6][:, 0:DE], ACT.Silu).then_inc(silu_done, 1)
            copy_hgT(1)
            with act.Fori(0, more) as i:
                for p in (1, 0):
                    b = 2 * i + 2 - p
                    silu(b, p)
                    copy_hgT(b + 1)
                    store(2 * i + 1 - p)
            silu(2 * more + 1, 1)
            store(2 * more)
            store(2 * more + 1)
            for t in range(TILES):
                act.wait_ge(fin_ready, t + 1)
                act.dma_start(tile_rows(y_prompt, y_sample, t), y_fin[t % 2]).then_inc(fin_out[t % 2], 16)
            act.wait_ge(fin_out[0], 16 * 3)
            act.wait_ge(fin_out[1], 16 * 2)
            act.wait_ge(new_out, 32)

        @block.vector
        def _(dve):
            done = [0]

            def link(ins):
                done[0] += 1
                ins.then_inc(dve_step, 1)
                dve.wait_ge(dve_step, done[0])

            V = nc.vector
            dve.wait_ge(ss_ready, TILES)
            V.tensor_scalar(xms, xss, 1.0 / D, EPS, ALU.mult, ALU.add).then_inc(ms_ready, 1)
            dve.wait_ge(rstd_ready, 1)
            for t in range(TILES):
                V.tensor_scalar(x_sb[:, t, :], x_sb[:, t, :], xr[:, t:t + 1], None, ALU.mult).then_inc(xn_ready, 1)
            dve.wait_ge(small_in, 32)
            for v in range(2):
                for half in range(2):
                    dve.wait_ge(ada_done, 2 * v + half + 1)
                    if v and not half:
                        dve.wait_ge(col_done, v)
                    V.tensor_copy(ada_row[:, half * 512:(half + 1) * 512],
                                  banks[6 + half][0:2, :]).then_inc(ada_copied, 1)
                dve.wait_ge(col_done, v + 1)
                col = banks[5][:, 0:16].rearrange("p (k c) -> p k c", c=2)
                b = bcol[:, v, :].unsqueeze(2).to_broadcast((P, KD, 2))
                if v == 0:
                    V.tensor_tensor(colB, col, b, ALU.add).then_inc(cols_ready, 1)
                else:
                    link(V.tensor_tensor(colA, col, b, ALU.add))
                    link(V.tensor_scalar(colA, colA, 1.0, None, ALU.add))
                    V.tensor_tensor(colA, colA, n1w.unsqueeze(2).to_broadcast((P, KD, 2)), ALU.mult).then_inc(cols_ready, 1)
            dve.wait_ge(norms_in, 96)
            link(V.tensor_scalar(qw, qw, HD ** -0.5, None, ALU.mult))

            def norm_head(i):
                n = rows[i]
                kind = proj[n][1]
                r = raw[i % 2]
                dve.wait_ge(proj_out, n + 1)
                if kind == "gv":
                    g = r.rearrange("p (g n) -> p g n", g=GROUPS)
                    s = sq[i % 2].rearrange("p (g n) -> p g n", g=GROUPS)
                    link(V.tensor_reduce(mean, g, X, ALU.add))
                    link(V.tensor_scalar(mean, mean, -1.0 / P, None, ALU.mult))
                    link(V.tensor_tensor(g, g, mean.unsqueeze(2).to_broadcast((P, GROUPS, P)), ALU.add))
                    link(V.tensor_tensor(s, g, g, ALU.mult))
                    link(V.tensor_reduce(ssq[i % 2][:, 0:4], s, X, ALU.add))
                    V.tensor_scalar(msq[i % 2][:, 0:4], ssq[i % 2][:, 0:4], 1.0 / P, EPS, ALU.mult,
                                    ALU.add).then_inc(normed_ms, 1)
                else:
                    dve.wait_ge(raw_ready, i + 1)
                    link(V.tensor_reduce(ssq[i % 2], sq[i % 2].rearrange("p (h d) -> p h d", h=HEADS), X, ALU.add))
                    V.tensor_scalar(msq[i % 2], ssq[i % 2], 1.0 / HD, EPS, ALU.mult, ALU.add).then_inc(normed_ms, 1)

            def norm_tail(i):
                n = rows[i]
                _, kind, t = proj[n]
                r = raw[i % 2]
                dve.wait_ge(norm_rstd_ready, i + 1)
                g = GROUPS if kind == "gv" else HEADS
                rv = r.rearrange("p (g n) -> p g n", g=g)
                link(V.tensor_tensor(rv, rv, rsq[i % 2][:, 0:g].unsqueeze(2).to_broadcast((P, g, 512 // g)), ALU.mult))
                if kind == "gv":
                    link(V.tensor_tensor(r, r, lnw, ALU.mult))
                    V.tensor_tensor(vv[:, t, :], r, lnb, ALU.add).then_inc(raw_normed, 1)
                else:
                    V.tensor_tensor(r, r, qw if kind == "q" else kw, ALU.mult).then_inc(raw_normed, 1)

            def copy_nT(i):
                _, kind, t = proj[rows[i]]
                dve.wait_ge(nT_done, i + 1)
                V.tensor_copy((qT if kind == "q" else kT)[:, :, t * P:(t + 1) * P],
                              banks[4 + i % 2][:].rearrange("p (j n) -> p j n", n=P)).then_inc(nT_copied, 1)

            for i in range(len(rows)):
                norm_head(i)
                norm_tail(i)
                if 1 <= i <= 2 * TILES:
                    copy_nT(i - 1)
            dve.wait_ge(proj_out, len(proj))
            for t in range(TILES):
                dve.wait_ge(sgu_done, t + 1)
                s = sq[t % 2].rearrange("p (g n) -> p g n", g=GROUPS)
                link(V.tensor_tensor(s, banks[4 + t % 2][:].rearrange("p (g n) -> p g n", g=GROUPS),
                                     bsg.rearrange("p (g n) -> p g n", g=GROUPS), ALU.add))
                u = positions(uT, t)
                o = positions(catT[:, 4:8, :], t)
                for g in range(GROUPS):
                    ins = V.tensor_tensor(o[:, g], s[:, g].rearrange("p (r c) -> p r c", r=2), u[:, g], ALU.mult)
                ins.then_inc(sgu_out, 1)
            for v in range(2, 6):
                dve.wait_ge(row_in, 16 * (v - 1))
                dve.wait_ge(n2_in, 16)
                if v > 2:
                    dve.wait_ge(row_out, 16 * (v - 2))
                for half in range(2):
                    s = slice(half * 512, (half + 1) * 512)
                    dve.wait_ge(ada_done, 2 * v + half + 1)
                    ins = V.tensor_tensor(ada_row[:, s], banks[6 + half][0:2, :], bias_row[:, s], ALU.add)
                    ins.then_inc(ada_copied, 1)
                dve.wait_ge(ada_copied, 2 * v + 2)
                if v == 4:
                    link(V.tensor_scalar(ada_row[:, :], ada_row[:, :], 1.0, None, ALU.add))
                    V.tensor_tensor(ada_row[:, :], ada_row[:, :], n2_row, ALU.mult).then_inc(row_ready, 1)

            def largest(n):
                t, h = steps[n]
                bank = 2 * (n % 2)
                p = n % 2
                dve.wait_ge(scored, n + 1)
                if t == 0:
                    link(V.tensor_reduce(m_ctx[:, p:p + 1], banks[bank + 1][:, 0:P], X, ALU.max))
                    V.tensor_scalar(nmax[:, p:p + 1], m_ctx[:, p:p + 1], -1.0, None, ALU.mult).then_inc(nmax_ready, 1)
                    return
                _, nt, piece = span(t)
                V.tensor_tensor_reduce(out=win[p][:, 0:nt * P], in0=banks[bank][:, 0:nt * P],
                                       in1=bm[:, h, piece:piece + nt, :].rearrange("p v n -> p (v n)"),
                                       scale=1.0, scalar=-3e38, op0=ALU.add, op1=ALU.max,
                                       accum_out=m_win[:, p:p + 1]).then_inc(win_ready, 1)
                link(V.tensor_reduce(m_ctx[:, p:p + 1], banks[bank + 1][:, 0:CACHE], X, ALU.max))
                dve.wait_ge(win_ready, n - HEADS + 1)
                V.tensor_scalar(nmax[:, p:p + 1], m_ctx[:, p:p + 1], m_win[:, p:p + 1], -1.0, ALU.max,
                                ALU.mult).then_inc(nmax_ready, 1)

            def copy_pT(n):
                t, h = steps[n]
                nk = key_tiles(t)
                dve.wait_ge(pT_done, n + 1)
                if nk > 3:
                    if n >= 2:
                        dve.wait_ge(pv_done, n - 1)
                    V.tensor_copy(pT[n % 2][:, 3:nk, :], banks[5][:, 0:(nk - 3) * P].rearrange(
                        "p (j n) -> p j n", n=P)).then_inc(pT_dve, 1)

            def normalise(t):
                dve.wait_ge(exp_done, HEADS * (t + 1))
                if t:
                    dve.wait_ge(act_step, HEADS * t)
                    link(V.tensor_tensor(rsum, sums[:, t % 2, :, 0], sums[:, t % 2, :, 1], ALU.add))
                    link(V.reciprocal(rsum, rsum))
                else:
                    link(V.reciprocal(rsum, sums[:, 0, :, 1]))
                dve.wait_ge(pv_done, HEADS * (t + 1))
                if t:
                    dve.wait_ge(aT_done, t)
                V.tensor_tensor(o_row.rearrange("p (h d) -> p h d", h=HEADS),
                                banks[6 + t % 2][:].rearrange("p (h d) -> p h d", h=HEADS),
                                rsum.unsqueeze(2).to_broadcast((P, HEADS, HD)), ALU.mult).then_inc(o_ready, 1)
                dve.wait_ge(aT_done, t + 1)
                V.tensor_copy(catT[:, 0:4, t * P:(t + 1) * P],
                              banks[4][:].rearrange("p (j n) -> p j n", n=P)).then_inc(aT_copied, 1)

            dve.wait_ge(bias_ready, 7)
            for n in range(len(steps) + 1):
                if n < len(steps):
                    largest(n)
                if n >= 1:
                    copy_pT(n - 1)
                    if steps[n - 1][1] == HEADS - 1:
                        normalise(steps[n - 1][0])
            dve.wait_ge(g1_in, 32)
            dve.wait_ge(new_out, 32)

            def second_norm(t):
                cnd = LAT if t else CTX
                dve.wait_ge(ss2_ready, t + 1)
                V.tensor_scalar(xms[:, t:t + 1], xss[:, t:t + 1], 1.0 / D, EPS, ALU.mult, ALU.add).then_inc(ms2_ready, 1)
                dve.wait_ge(n_rstd2, t + 1)
                if t >= 2:
                    dve.wait_ge(h2T_done, t - 1)
                    dve.wait_ge(h2_out[t % 2], 16 * (t // 2))
                link(V.scalar_tensor_tensor(h2[t % 2], x_sb[:, t, :], xr[:, t:t + 1], bc[:, 1, cnd, :],
                                            ALU.mult, ALU.mult))
                V.tensor_tensor(h2[t % 2], h2[t % 2], bc[:, 0, cnd, :], ALU.add).then_inc(h2_ready, 1)
                dve.wait_ge(h2T_done, t + 1)
                if t:
                    dve.wait_ge(z_done, t)
                V.tensor_copy(h2T[:, 4:8, :], banks[5][:].rearrange("p (j n) -> p j n", n=P)).then_inc(h2T_dve, 1)

            for t in range(TILES):
                cnd = LAT if t else CTX
                dve.wait_ge(x_again, 16 * TILES)
                for half in range(2):
                    s = slice(half * 512, (half + 1) * 512)
                    dve.wait_ge(wout_done, 2 * t + half + 1)
                    link(V.tensor_tensor(sq[half], banks[(2 * t + half) % 4][:], g1b[:, cnd, s], ALU.mult))
                    V.tensor_tensor(x_sb[:, t, s], x_sb[:, t, s], sq[half], ALU.add).then_inc(x1_ready, 1)
                if t == 0:
                    dve.wait_ge(bc_in, 96)
                second_norm(t)

            def b3(a, n, w):
                return a.rearrange("p (t e) -> p t e", t=n)

            def wide(a, n, w):
                return a.unsqueeze(2).to_broadcast((P, n, w))

            dve.wait_ge(s_ready, 1)
            dve.wait_ge(bm_ready, 5)
            link(V.tensor_tensor(b3(sel, TILES, 16), b3(scores_s, TILES, 16),
                                 brt.unsqueeze(1).to_broadcast((P, TILES, EXPERTS)), ALU.add))
            s4 = sel.rearrange("p (g e) -> p g e", e=EPG)
            p6 = pair.rearrange("p (g e) -> p g e", e=6)
            V.tensor_tensor(p6[:, :, 0:3], s4[:, :, 0:3], s4[:, :, 1:4], ALU.add)
            V.tensor_tensor(p6[:, :, 3:5], s4[:, :, 0:2], s4[:, :, 2:4], ALU.add)
            link(V.tensor_tensor(p6[:, :, 5:6], s4[:, :, 0:1], s4[:, :, 3:4], ALU.add))
            link(V.tensor_reduce(gsc, p6, X, ALU.max))

            def first_largest(hot, val, n, t1, best, order):
                v3, h3, o3 = b3(val, TILES, n), b3(hot, TILES, n), b3(t1, TILES, n)
                link(V.tensor_reduce(best, v3, X, ALU.max))
                link(V.tensor_tensor(o3, v3, wide(best, TILES, n), ALU.is_ge))
                link(V.tensor_tensor(o3, o3, order.unsqueeze(1).to_broadcast((P, TILES, n)), ALU.mult))
                link(V.tensor_reduce(best, o3, X, ALU.max))
                link(V.tensor_tensor(h3, o3, wide(best, TILES, n), ALU.is_equal))

            first_largest(ghot, gsc, EG, gtmp, t5a, desc[:, EXPERTS - EG:])
            m4 = msel.rearrange("p (g e) -> p g e", e=EPG)
            link(V.tensor_tensor(m4, s4, wide(ghot, TILES * EG, EPG), ALU.mult))
            link(V.tensor_scalar(gtmp, ghot, 1.0, -NEG, ALU.subtract, ALU.mult))
            link(V.tensor_tensor(m4, m4, wide(gtmp, TILES * EG, EPG), ALU.add))
            first_largest(hot1, msel, EXPERTS, tmp, t5a, desc)
            link(V.scalar_tensor_tensor(msel, hot1, 3 * NEG, msel, ALU.mult, ALU.add))
            first_largest(hot2, msel, EXPERTS, tmp, t5a, desc)
            V.tensor_tensor(both, hot1, hot2, ALU.add).then_inc(m_ready, 1)
            for j, hot in enumerate((hot1, hot2)):
                link(V.tensor_tensor(tmp, scores_s, hot, ALU.mult))
                link(V.tensor_reduce(gate_s[:, 5 * j:5 * j + 5], b3(tmp, TILES, 16), X, ALU.add))
            link(V.tensor_tensor(t5a, gate_s[:, 0:5], gate_s[:, 5:10], ALU.add))
            link(V.reciprocal(t5b, t5a))
            link(V.tensor_tensor(gates, gate_s.rearrange("p (k t) -> p k t", k=2),
                                 t5b.unsqueeze(1).to_broadcast((P, 2, TILES)), ALU.mult))
            dve.wait_ge(ranks_done, 1)
            count = banks[7][:, TE:TE + EXPERTS]
            link(V.tensor_scalar(nb, count, 0.0, None, ALU.is_gt))
            for j in range(1, TILES):
                link(V.scalar_tensor_tensor(nb, count, float(j * P), nb, ALU.is_gt, ALU.add))
            link(V.tensor_tensor_scan(bend, ones[:, 0:EXPERTS], nb, 0.0, ALU.mult, ALU.add))
            link(V.tensor_tensor(bstart, bend, nb, ALU.subtract))
            link(V.tensor_scalar(bstart, bstart, float(P), None, ALU.mult))
            link(V.tensor_tensor(b3(rank, TILES, 16), b3(banks[7][:, 0:TE], TILES, 16),
                                 bstart.unsqueeze(1).to_broadcast((P, TILES, EXPERTS)), ALU.add))
            sl = slotf.rearrange("p (t k) -> p t k", k=2)
            for j, hot in enumerate((hot1, hot2)):
                link(V.tensor_tensor(tmp, rank, hot, ALU.mult))
                link(V.tensor_reduce(sl[:, :, j], b3(tmp, TILES, 16), X, ALU.add))
            link(V.tensor_copy(slot_u, slotf))
            link(V.tensor_tensor(cmp_b.rearrange("p (s b) -> p s b", s=10), wide(slotf, 10, 27),
                                 blk_edge.unsqueeze(1).to_broadcast((P, 10, 27)), ALU.is_ge))
            link(V.tensor_reduce(blkf, cmp_b.rearrange("p (s b) -> p s b", s=10), X, ALU.add))
            link(V.scalar_tensor_tensor(inf, blkf, -float(P), slotf, ALU.mult, ALU.add))
            link(V.tensor_tensor(hot_s.rearrange("p (s n) -> p s n", s=10), wide(inf, 10, P),
                                 iota_p.unsqueeze(1).to_broadcast((P, 10, P)), ALU.is_equal))
            hb = hot_b.rearrange("p (t k b) -> p t k b", t=TILES, k=2)
            link(V.tensor_tensor(hot_b.rearrange("p (s b) -> p s b", s=10), wide(blkf, 10, 28),
                                 iota_b.unsqueeze(1).to_broadcast((P, 10, 28)), ALU.is_equal))
            V.tensor_tensor(hot_b.rearrange("p (t b) -> p t b", t=TILES), hot_b.rearrange("p (t b) -> p t b", t=TILES),
                            wide(tokid, TILES, 56), ALU.mult).then_inc(hot_ready, 1)
            link(V.tensor_tensor(cmp_e.rearrange("p (b e) -> p b e", e=EXPERTS), wide(iota_b, 28, EXPERTS),
                                 bend.unsqueeze(1).to_broadcast((P, 28, EXPERTS)), ALU.is_ge))
            link(V.tensor_reduce(ebf, cmp_e.rearrange("p (b e) -> p b e", e=EXPERTS), X, ALU.add))
            link(V.tensor_scalar(ebf, ebf, float(EXPERTS - 1), None, ALU.min))
            link(V.tensor_tensor(cmp_e[:, 0:13], iota_b[:, 0:26].rearrange("p (i k) -> p i k", k=2)[:, :, 0],
                                 bend[:, 15:16].to_broadcast((P, 13)), ALU.is_lt))
            link(V.tensor_reduce(ebf[:, 27:28], cmp_e[:, 0:13], X, ALU.add))
            link(V.tensor_scalar(ebf[:, 27:28], ebf[:, 27:28], -1.0, None, ALU.add))
            link(V.tensor_copy(ebi, ebf))
            dve.wait_ge(inv_done, 1)
            V.tensor_copy(gidx, banks[7][:, 128:156]).then_inc(table_ready, 1)
            dve.wait_ge(table_ready, 1)
            more = dve.value_load(ebi[0:1, 27:28], min_val=4, max_val=MAX_BLOCKS // 2 - 1)

            def copy_hgT(b):
                dve.wait_ge(hgT_done, b + 1)
                if not (isinstance(b, int) and b == 0):
                    dve.wait_ge(w13_done, b)
                V.tensor_copy(hgT[:, 4:8, :], banks[5][:].rearrange("p (j n) -> p j n", n=P)).then_inc(hgT_dve, 1)

            def hidden(b, p):
                dve.wait_ge(silu_done, b + 1)
                V.tensor_tensor(hid[p], banks[6 + p][:, DE:2 * DE], sil, ALU.mult).then_inc(hid_ready, 1)

            def copy_hidT(b):
                dve.wait_ge(hidT_done, b + 1)
                V.tensor_copy(hidT, banks[3][:, 0:2 * P].rearrange("p (j n) -> p j n", n=P)).then_inc(hidT_ready, 1)

            def copy_y(b):
                dve.wait_ge(y_done, b + 1)
                dve.wait_ge(y_stored, 16 * (b + 1))
                V.tensor_copy(y_sb[:, 512:1024], banks[1][:]).then_inc(y_dve, 1)

            V.engine_nop().then_inc(hid_ready, 1)
            copy_hgT(0)
            hidden(0, 0)
            copy_hgT(1)
            with dve.Fori(0, more) as i:
                for p in (1, 0):
                    b = 2 * i + 2 - p
                    hidden(b, p)
                    copy_hgT(b + 1)
                    copy_hidT(2 * i + 1 - p)
                    copy_y(2 * i + 1 - p)
            hidden(2 * more + 1, 1)
            for b in (2 * more, 2 * more + 1):
                copy_hidT(b)
                copy_y(b)
            for t in range(TILES):
                cnd = LAT if t else CTX
                a, b = y_in[t % 2]
                f = y_fin[t % 2]
                dve.wait_ge(back_in[t % 2], 32 * (t // 2 + 1))
                if t >= 2:
                    dve.wait_ge(fin_out[t % 2], 16 * (t // 2))
                link(V.tensor_scalar(f, a, gates[:, 0, t:t + 1], None, ALU.mult))
                ins = V.scalar_tensor_tensor(f, b, gates[:, 1, t:t + 1], f, ALU.mult, ALU.add)
                ins.then_inc(fin_mid, 1)
                dve.wait_ge(fin_mid, t + 1)
                link(V.tensor_tensor(f, f, bc[:, 2, cnd, :], ALU.mult))
                V.tensor_tensor(f, f, x_sb[:, t, :], ALU.add).then_inc(fin_ready, 1)

        @block.tensor
        def _(pe):
            T = nc.tensor

            def arrived(key):
                n = chunk_at[key]
                pe.wait_ge(ring_in[n % RING], 16 * (n // RING + 1))
                return ring[n % RING]

            def ada(j, s):
                w = arrived(("ada", j))
                bank = banks[6 + j % 2]
                if j >= 2:
                    pe.wait_ge(ada_copied, j - 1)
                for k in range(KD):
                    ins = T.matmul(bank[0:2, :], s[:, k, :], w[:, k, :], start=(k == 0), stop=(k == KD - 1))
                ins.then_inc(ada_done, 1)

            pe.wait_ge(consts_ready, 3)
            pe.wait_ge(ones_ready, 1)
            pe.wait_ge(silu_ready, 1)
            for v in range(2):
                for half in range(2):
                    ada(2 * v + half, silT)
                pe.wait_ge(ada_copied, 2 * v + 2)
                if v:
                    pe.wait_ge(cols_ready, v)
                for k in range(KD):
                    ins = T.transpose(banks[5][:, 2 * k:2 * k + 2], ada_row[:, :].rearrange(
                        "c (p k) -> c k p", k=KD)[:, k, :], ident[0:2, 0:2])
                ins.then_inc(col_done, 1)
            pe.wait_ge(xn_ready, TILES)
            xv = x_sb.rearrange("p t (c k) -> p t k c", k=KD)
            for half in range(2):
                for k in range(4 * half, 4 * half + 4):
                    ins = T.transpose(banks[half][:, (k % 4) * P:(k % 4 + 1) * P], xv[:, 0, k, :], ident[:])
                ins.then_inc(xT_done, 1)
            for k in range(KD):
                if k >= 2:
                    pe.wait_ge(hT_ready, 4 * (k - 1) if k < 4 else 8 + k - 3)
                for t in range(1, TILES):
                    ins = T.transpose(banks[(k + 2) % 4][:, (t - 1) * P:t * P], xv[:, t, k, :], ident[:])
                ins.then_inc(xT_done, 1)
            def norm_T(i):
                pe.wait_ge(raw_normed, i + 1)
                if i >= 2:
                    pe.wait_ge(nT_copied, i - 1)
                for j in range(4):
                    ins = T.transpose(banks[4 + i % 2][:, j * P:(j + 1) * P], raw[i % 2][:, j * P:(j + 1) * P], ident[:])
                ins.then_inc(nT_done, 1)

            pe.wait_ge(hT_ready, 16)
            for n, (col, kind, t) in enumerate(proj):
                w = arrived(("in", col))
                bank = banks[n % 4]
                if n >= 4:
                    pe.wait_ge(proj_out, n - 3)
                if kind == "gv" and t == 1:
                    pe.wait_ge(by_row, 2)
                for k in range(KD):
                    if kind == "gu":
                        g, part = t
                        lo, hi = (0, P) if part == CTX else (P, TOK)
                        ins = T.matmul(bank[:, 0:hi - lo], w[:, k, g * P:(g + 1) * P], hT[:, k, lo:hi],
                                       start=(k == 0), stop=(k == KD - 1))
                    else:
                        if kind == "gv" and t:
                            lhs = hT_rows[:, k, (t - 1) * P:t * P]
                        else:
                            lhs = hT[:, k, t * P:(t + 1) * P]
                        ins = T.matmul(bank[:], lhs, w[:, k, :], start=(k == 0), stop=(k == KD - 1))
                ins.then_inc(proj_done, 1)
                if 1 <= n <= 2 * TILES:
                    norm_T(n - 1)
            pe.wait_ge(raw_normed, 3 * TILES)
            pe.wait_ge(norms_in, 96)
            pe.wait_ge(nT_copied, 2 * TILES)
            for t in range(TILES):
                if t >= 2:
                    pe.wait_ge(sgu_out, t - 1)
                for g in range(GROUPS):
                    ins = T.matmul(banks[4 + t % 2][:, g * P:(g + 1) * P], vv[:, t, g * P:(g + 1) * P],
                                   wsT[:, g * P:(g + 1) * P], start=True, stop=True)
                ins.then_inc(sgu_done, 1)
            for j in range(4, 12):
                ada(j, silT)

            def scores(n):
                t, h = steps[n]
                hp, lo = h // 2, HD * (h % 2)
                bank = 2 * (n % 2)
                if n >= 2:
                    pe.wait_ge(exp_done, n - 1)
                q = qT[lo:lo + HD, hp, t * P:(t + 1) * P]
                if t == 0:
                    T.matmul(banks[bank + 1][:, 0:P], q, kT[lo:lo + HD, hp, 0:P], start=True,
                             stop=True).then_inc(scored, 1)
                    return
                first, nt, _ = span(t)
                T.matmul(banks[bank][:, 0:nt * P], q, kT[lo:lo + HD, hp, (1 + first) * P:(1 + first + nt) * P],
                         start=True, stop=True)
                T.matmul(banks[bank + 1][:, 0:CACHE], q, ckT[lo:lo + HD, hp, :], start=True,
                         stop=True).then_inc(scored, 1)

            def prob_T(n):
                t, h = steps[n]
                pe.wait_ge(exp_done, n + 1)
                if t:
                    pe.wait_ge(act_step, n - HEADS + 1)
                if n >= 1:
                    pe.wait_ge(pT_act, n)
                    if dve_copies(n - 1):
                        pe.wait_ge(pT_dve, dve_copies(n - 1))
                if h == 0 and t:
                    pe.wait_ge(aT_copied, t)
                for j in range(key_tiles(t)):
                    bank, at_ = (4, j) if j < 3 else (5, j - 3)
                    ins = T.transpose(banks[bank][:, at_ * P:(at_ + 1) * P], probs[n % 2][:, j * P:(j + 1) * P], ident[:])
                ins.then_inc(pT_done, 1)

            def dve_copies(n):
                return sum(key_tiles(steps[m][0]) > 3 for m in range(n + 1))

            def values(n):
                t, h = steps[n]
                pe.wait_ge(pT_act, n + 1)
                if dve_copies(n):
                    pe.wait_ge(pT_dve, dve_copies(n))
                if h == 0 and t >= 2:
                    pe.wait_ge(o_ready, t - 1)
                lo = h * HD
                nk = key_tiles(t)
                for j in range(nk):
                    if t == 0:
                        v = v_sb[:, 0, lo:lo + HD]
                    elif j < nk - 2:
                        v = v_sb[:, 1 + span(t)[0] + j, lo:lo + HD]
                    else:
                        v = cv[:, j - (nk - 2), lo:lo + HD]
                    ins = T.matmul(banks[6 + t % 2][:, lo:lo + HD], pT[n % 2][:, j, :], v, start=(j == 0),
                                   stop=(j == nk - 1))
                ins.then_inc(pv_done, 1)

            def att_T(t):
                pe.wait_ge(o_ready, t + 1)
                for j in range(4):
                    ins = T.transpose(banks[4][:, j * P:(j + 1) * P], o_row[:, j * P:(j + 1) * P], ident[:])
                ins.then_inc(aT_done, 1)

            pe.wait_ge(cache_in, 64)
            pe.wait_ge(sgu_out, TILES)
            pe.wait_ge(ada_copied, 12)
            scores(0)
            for n in range(len(steps)):
                if n + 1 < len(steps):
                    scores(n + 1)
                prob_T(n)
                values(n)
                if steps[n][1] == HEADS - 1:
                    att_T(steps[n][0])
            pe.wait_ge(exp_done, len(steps))
            pe.wait_ge(aT_copied, TILES)

            def router(t):
                pe.wait_ge(h2_ready, t + 1)
                if t:
                    pe.wait_ge(h2T_act, t)
                    pe.wait_ge(h2T_dve, t)
                hrow = h2[t % 2].rearrange("p (c k) -> p k c", k=KD)
                for k in range(KD):
                    ins = T.transpose(banks[4 + k // 4][:, (k % 4) * P:(k % 4 + 1) * P], hrow[:, k, :], ident[:])
                ins.then_inc(h2T_done, 1)
                pe.wait_ge(h2T_act, t + 1)
                pe.wait_ge(h2T_dve, t + 1)
                for k in range(KD):
                    ins = T.matmul(banks[6][:, t * EXPERTS:(t + 1) * EXPERTS], h2T[:, k, :], wr_sb[:, k, :],
                                   start=(k == 0), stop=(k == KD - 1))
                ins.then_inc(z_done, 1)

            arrived(("out", 0))
            arrived(("out", 1))
            for t in range(TILES):
                for half in range(2):
                    n = 2 * t + half
                    w = arrived(("out", half))
                    if n >= 4:
                        pe.wait_ge(x1_ready, n - 3)
                    for k in range(KD):
                        ins = T.matmul(banks[n % 4][:], catT[:, k, t * P:(t + 1) * P], w[:, k, :],
                                       start=(k == 0), stop=(k == KD - 1))
                    ins.then_inc(wout_done, 1)
                if t:
                    router(t - 1)
            router(TILES - 1)
            pe.wait_ge(m_ready, 1)
            for t in range(TILES):
                r = banks[7][:, t * EXPERTS:(t + 1) * EXPERTS]
                T.matmul(r, before[:], both[:, t * EXPERTS:(t + 1) * EXPERTS], start=True, stop=(t == 0))
                for u in range(t):
                    T.matmul(r, ones[:], both[:, u * EXPERTS:(u + 1) * EXPERTS], start=False, stop=(u == t - 1))
            for u in range(TILES):
                ins = T.matmul(banks[7][:, TE:TE + EXPERTS], ones[:], both[:, u * EXPERTS:(u + 1) * EXPERTS],
                               start=(u == 0), stop=(u == TILES - 1))
            ins.then_inc(ranks_done, 1)
            pe.wait_ge(hot_ready, 1)
            for s in range(10):
                ins = T.matmul(banks[7][:, 128:156], hot_s[:, s * P:(s + 1) * P], hot_b[:, s * 28:(s + 1) * 28],
                               start=(s == 0), stop=(s == 9))
            ins.then_inc(inv_done, 1)
            pe.wait_ge(table_ready, 1)
            more = pe.value_load(ebi[0:1, 27:28], min_val=4, max_val=MAX_BLOCKS // 2 - 1)

            def token_T(b, p, half):
                pe.wait_ge(hg_in[p], 16 * (half + 1))
                if not (isinstance(b, int) and b == 0):
                    pe.wait_ge(hgT_act, b)
                    pe.wait_ge(hgT_dve, b)
                hrow = hg[p].rearrange("p (c k) -> p k c", k=KD)
                for k in range(KD):
                    ins = T.transpose(banks[4 + k // 4][:, (k % 4) * P:(k % 4 + 1) * P], hrow[:, k, :], ident[:])
                ins.then_inc(hgT_done, 1)

            def up(b, p, half):
                pe.wait_ge(hgT_act, b + 1)
                pe.wait_ge(hgT_dve, b + 1)
                pe.wait_ge(w13_in[p], 32 * (half + 1))
                if not (isinstance(b, int) and b == 0):
                    pe.wait_ge(hid_ready, b)
                for k in range(KD):
                    ins = T.matmul(banks[6 + p][:], hgT[:, k, :], w13[p][:, k, :], start=(k == 0), stop=(k == KD - 1))
                ins.then_inc(w13_done, 1)

            def down(b, p, half):
                pe.wait_ge(hid_ready, b + 2)
                hrow = hid[p].rearrange("p (c k) -> p k c", k=2)
                for k in range(2):
                    ins = T.transpose(banks[3][:, k * P:(k + 1) * P], hrow[:, k, :], ident[:])
                ins.then_inc(hidT_done, 1)
                pe.wait_ge(hidT_ready, b + 1)
                pe.wait_ge(w2_in[p], 16 * (half + 1))
                if not (isinstance(b, int) and b == 0):
                    pe.wait_ge(y_act, b)
                    pe.wait_ge(y_dve, b)
                for n in range(2):
                    for k in range(2):
                        ins = T.matmul(banks[n][:], hidT[:, k, :], w2s[p][:, k, n * 512:(n + 1) * 512],
                                       start=(k == 0), stop=(k == 1))
                ins.then_inc(y_done, 1)

            token_T(0, 0, 0)
            up(0, 0, 0)
            token_T(1, 1, 0)
            with pe.Fori(0, more) as i:
                up(2 * i + 1, 1, i)
                token_T(2 * i + 2, 0, i + 1)
                down(2 * i, 0, i)
                up(2 * i + 2, 0, i + 1)
                token_T(2 * i + 3, 1, i + 1)
                down(2 * i + 1, 1, i)
            up(2 * more + 1, 1, more)
            down(2 * more, 0, more)
            down(2 * more + 1, 1, more)


_INS = ("x_prompt", "x_sample", "cache_kt", "cache_v", "c", "c_ctx", "w_ada", "b_ada", "norm1_w", "norm2_w", "w_in",
        "q_norm_w", "k_norm_w", "rpb_runs", "w_sgu_t", "b_sgu", "ln_w", "ln_b", "w_out", "w_router", "b_router", "w1",
        "w3", "w2")
_OUTS = (("y_prompt", (P, D)), ("y_sample", (4 * P, D)), ("new_k", (P, AW)), ("new_v", (P, AW)))


def kernel(x_prompt, x_sample, cache_k, cache_v, c, c_ctx, w_ada, b_ada, norm1_w, norm2_w, w_in, q_norm_w, k_norm_w,
           rpb, w_sgu, b_sgu, sgu_ln_w, sgu_ln_b, w_out, w_router, b_router, w1, w3, w2):
    import concourse.bacc as bacc
    import numpy as np
    from concourse.bass_utils import run_bass_kernel_spmd

    def a(x, *shape):
        return np.ascontiguousarray(np.asarray(x).reshape(shape))

    rpb_flat = np.zeros(2 * RPB_PAD + np.asarray(rpb).size, np.asarray(rpb).dtype)
    rpb_flat[RPB_PAD:-RPB_PAD] = np.asarray(rpb).ravel()
    rpb_runs = np.empty((P, HEADS, RUN), rpb_flat.dtype)
    for p in range(P):
        for h in range(HEADS):
            at = RPB_PAD + (h * RPB_H + GRID_H - 1 - p % GRID_H) * RPB_W - p // GRID_H - 1
            rpb_runs[p, h] = rpb_flat[at:at + RUN]
    arrays = {
        "x_prompt": a(x_prompt, P, D),
        "x_sample": np.ascontiguousarray(a(x_sample, GRID_H, GRID_W, D).transpose(1, 0, 2)).reshape(4 * P, D),
        "cache_kt": np.ascontiguousarray(a(cache_k, CACHE, 4, P).transpose(2, 1, 0)),
        "cache_v": a(cache_v, CACHE, AW), "c": a(c, D), "c_ctx": a(c_ctx, D), "w_ada": a(w_ada, D, 6 * D),
        "b_ada": a(b_ada, 6 * D), "norm1_w": a(norm1_w, D), "norm2_w": a(norm2_w, D), "w_in": a(w_in, D, 5 * AW),
        "q_norm_w": a(q_norm_w, HD), "k_norm_w": a(k_norm_w, HD), "rpb_runs": rpb_runs,
        "w_sgu_t": np.ascontiguousarray(a(w_sgu, GROUPS, P, P).transpose(2, 0, 1)).reshape(P, GROUPS * P),
        "b_sgu": a(b_sgu, GROUPS * P), "ln_w": a(sgu_ln_w, AW), "ln_b": a(sgu_ln_b, AW), "w_out": a(w_out, D, D),
        "w_router": a(w_router, D, EXPERTS), "b_router": a(b_router, EXPERTS), "w1": a(w1, EXPERTS, D, DE),
        "w3": a(w3, EXPERTS, D, DE), "w2": a(w2, EXPERTS, DE, D),
    }
    nc = bacc.Bacc("TRN2", target_bir_lowering=False, num_devices=1)
    ins = [nc.dram_tensor(n, arrays[n].shape, mybir.dt.from_np(arrays[n].dtype), kind="ExternalInput").ap()
           for n in _INS]
    outs = [nc.dram_tensor(n, shape, F32, kind="ExternalOutput").ap() for n, shape in _OUTS]
    build(nc, ins, outs)
    r = run_bass_kernel_spmd(nc, [arrays], core_ids=[0]).results[0]
    y_sample = r["y_sample"].reshape(GRID_W, GRID_H, D).transpose(1, 0, 2).reshape(1, 4 * P, D)
    return (r["y_prompt"].reshape(1, P, D), np.ascontiguousarray(y_sample), r["new_k"].reshape(1, 1, P, HEADS, HD),
            r["new_v"].reshape(1, 1, P, HEADS, HD))
```

```python
from contextlib import ExitStack

import concourse.bass as bass
from concourse import mybir

F32 = mybir.dt.float32
BF16 = mybir.dt.bfloat16
F16 = mybir.dt.float16
U32 = mybir.dt.uint32
I32 = mybir.dt.int32
ALU = mybir.AluOpType
ACT = mybir.ActivationFunctionType
X = mybir.AxisListType.X

P = 128
D = 1024
KD = D // P
GRID_W, GRID_H = 64, 8
HEADS, HD = 8, 64
AW = HEADS * HD
GROUPS = 4
TILES = 5
TOK = TILES * P
CTX, LAT = 0, 1
COLS = P // GRID_H
CACHE = 256
WIN_W, HALF_W = 16, 8
RPB_W = 2 * WIN_W - 1
RPB_H = 2 * GRID_H - 1
RPB_PAD = 16
RUN = (GRID_H - 1) * RPB_W + 3 * COLS
EXPERTS, EG, EPG = 16, 4, 4
DE = 256
MAX_BLOCKS = EXPERTS + 10
SHARED = EXPERTS // 2 - 1
NEG = -1e30
EPS = 1e-6
CHUNK = KD * 512
RING = 4

INNER, LEFT_EDGE, RIGHT_EDGE = 0, 3, 5


def build(nc, t_in, t_out):
    (x_prompt, x_sample, cache_kt, cache_v, c, c_ctx, w_ada, b_ada, norm1_w, norm2_w, w_in, q_norm_w,
     k_norm_w, rpb_runs, w_sgu_t, b_sgu, ln_w, ln_b, w_out, w_router, b_router, w1, w3, w2) = t_in
    y_prompt, y_sample, new_k, new_v = t_out
    ctx = ExitStack()
    with ctx:
        def sb(name, shape, dt=F32):
            return ctx.enter_context(nc.sbuf_tensor(name, shape, dt))

        def sem(name):
            return ctx.enter_context(nc.semaphore(name))

        ada_rows = nc.dram_tensor("ada_rows", (6, 2, D), F32, kind="Internal").ap()
        h2_rows = nc.dram_tensor("h2_rows", (TOK, D), F32, kind="Internal").ap()
        slot_out = nc.dram_tensor("slot_out", (MAX_BLOCKS * P, D), F32, kind="Internal").ap()

        big = sb("big", [P, RING * CHUNK + KD * TOK])
        ring = [big[:, s * CHUNK:(s + 1) * CHUNK].rearrange("p (k n) -> p k n", k=KD) for s in range(RING)]
        catT = big[:, RING * CHUNK:].rearrange("p (k n) -> p k n", k=KD)
        hT_rows = catT[:, :, 0:4 * P]
        w13 = [ring[3], ring[0]]
        w2s = [big[:, (CHUNK + s * 2 * D):(CHUNK + (s + 1) * 2 * D)].rearrange("p (k n) -> p k n", k=2)
               for s in range(2)]
        y_in = [[big[:, (4 * i + 2 * j) * D:(4 * i + 2 * j + 1) * D] for j in range(2)] for i in range(2)]
        y_fin = [big[:, (4 * i + 1) * D:(4 * i + 2) * D] for i in range(2)]

        hu = sb("hu", [P, KD * TOK + GROUPS * TOK])
        hT = hu[:, 0:KD * TOK].rearrange("p (k n) -> p k n", k=KD)
        uT = hu[:, KD * TOK:].rearrange("p (g n) -> p g n", g=GROUPS)
        bm = hu[:, 0:HEADS * 7 * P].rearrange("p (h v n) -> p h v n", h=HEADS, v=7)
        bc = hu[:, 0:6 * D].rearrange("p (v c n) -> p v c n", v=3, c=2)

        vvr = sb("vvr", [P, TILES * AW])
        vv = vvr[:, :].rearrange("p (t n) -> p t n", t=TILES)
        slab = vvr[:, 0:HEADS * RUN].rearrange("p (h n) -> p h n", h=HEADS)
        hg = [vvr[:, s * D:(s + 1) * D] for s in range(2)]

        qk = sb("qk", [P, 5 * D])
        x_sb = qk[:, :].rearrange("p (t n) -> p t n", t=TILES)
        qT = qk[:, 0:4 * TOK].rearrange("p (k n) -> p k n", k=4)
        kT = qk[:, 4 * TOK:8 * TOK].rearrange("p (k n) -> p k n", k=4)

        vr = sb("vr", [P, TILES * AW])
        v_sb = vr[:, :].rearrange("p (t n) -> p t n", t=TILES)
        h2 = [vr[:, s * D:(s + 1) * D] for s in range(2)]
        hgT = vr[:, 0:D].rearrange("p (k n) -> p k n", k=KD)
        sil = vr[:, D:D + DE]
        hid = [vr[:, D + (1 + s) * DE:D + (2 + s) * DE] for s in range(2)]
        hidT = vr[:, D + 3 * DE:D + 4 * DE].rearrange("p (k n) -> p k n", k=2)

        cc = sb("cc", [P, 4 * CACHE + 2 * AW])
        ckT = cc[:, 0:4 * CACHE].rearrange("p (k n) -> p k n", k=4)
        cv = cc[:, 4 * CACHE:].rearrange("p (t n) -> p t n", t=2)
        g1b = cc[:, :].rearrange("p (c n) -> p c n", c=2)

        xt = sb("xt", [P, 2 * D])
        junk = xt[:, 0:D]
        probs = [xt[:, s * 640:(s + 1) * 640] for s in range(2)]
        win = [xt[:, 1280 + s * 384:1280 + (s + 1) * 384] for s in range(2)]

        po = sb("po", [P, 2 * D])
        pT = [po[:, s * 640:(s + 1) * 640].rearrange("p (j n) -> p j n", j=5) for s in range(2)]
        o_row = po[:, 1280:1280 + AW]
        masks = {m: catT[:, i, 4 * P:] for i, m in enumerate(("left", "right", "from", "upto"))}
        masks["both"] = po[:, 1280 + AW:1280 + AW + P]
        h2T = po[:, 0:D].rearrange("p (k n) -> p k n", k=KD)

        rs = sb("rs", [P, 4 * 512])
        raw = [rs[:, s * 512:(s + 1) * 512] for s in range(2)]
        sq = [rs[:, (2 + s) * 512:(3 + s) * 512] for s in range(2)]
        bias_row = rs[0:2, 0:D]
        n2_row = rs[0:2, D:2 * D]
        y_sb = rs[:, 0:D]
        wr_sb = sb("wr_sb", [P, KD, EXPERTS])
        ada_row = sb("ada_row", [2, D])
        norms = sb("norms", [P, 6 * 512])
        qw, kw, lnw, lnb, bsg, wsT = [norms[:, s * 512:(s + 1) * 512] for s in range(6)]
        ident = sb("ident", [P, P])
        ones = sb("ones", [P, P])
        before = sb("before", [P, P], BF16)
        ones_b = sb("ones_b", [P, P], BF16)
        zero = sb("zero", [P, 256])
        small = sb("small", [P, 400])
        at = [0]

        def cut(n, shape=None, dt=F32):
            a = small[:, at[0]:at[0] + n]
            at[0] += n
            a = a if dt == F32 else a.bitcast(dt)
            return a if shape is None else a.rearrange(shape[0], **shape[1])

        cond = cut(16, ("p (c k) -> p c k", dict(c=2)))
        silT = cut(16, ("p (k c) -> p k c", dict(c=2)))
        bcol = cut(16, ("p (v k) -> p v k", dict(v=2)))
        n1w = cut(8)
        colB = cut(16, ("p (k c) -> p k c", dict(c=2)))
        colA = cut(16, ("p (k c) -> p k c", dict(c=2)))
        xss, xms, xr = cut(5), cut(5), cut(5)
        mean, ssq, msq, rsq = cut(4), [cut(8) for _ in range(2)], [cut(8) for _ in range(2)], [cut(8) for _ in range(2)]
        mhalf = cut(8)
        m_win, m_ctx, nmax = [cut(2) for _ in range(3)]
        sums = cut(32, ("p (b h c) -> p b h c", dict(b=2, c=2)))
        rsum = cut(8)
        tokid = cut(5)
        brt = cut(16)
        gates = cut(10, ("p (k t) -> p k t", dict(k=2)))
        slot_u = cut(10, None, U32)
        gidx = cut(28, None, U32)
        ebi = cut(28, None, I32)
        held = cut(3)
        warm = cut(2)
        both = cut((TILES + 1) * EXPERTS // 2).bitcast(BF16)
        idx1 = [cut(1, None, U32) for _ in range(2)]
        r_at = [0]

        def rcut(n):
            a = norms[:, r_at[0]:r_at[0] + n]
            r_at[0] += n
            return a

        banks = [ctx.enter_context(nc.psum_tensor(f"bank{i}", [P, 512], F32)) for i in range(8)]

        cond_in, small_in, x_in, norms_in, cache_in, slab_in = [sem(n) for n in (
            "cond_in", "small_in", "x_in", "norms_in", "cache_in", "slab_in")]
        ring_in = [sem(f"ring_in{s}") for s in range(RING)]
        zero_ready, slots_zeroed, bias_ready = sem("zero_ready"), sem("slots_zeroed"), sem("bias_ready")
        by_row, ones_ready, n2_in, consts_ready, rstd_ready, norm_rstd_ready, n_rstd2 = [sem(n) for n in (
            "by_row", "ones_ready", "n2_in", "consts_ready", "rstd_ready", "norm_rstd_ready", "n_rstd2")]
        silu_ready, ada_done, ada_copied, col_done, cols_ready = [sem(n) for n in (
            "silu_ready", "ada_done", "ada_copied", "col_done", "cols_ready")]
        ss_ready, ms_ready, xn_ready, xT_done, hT_ready = [sem(n) for n in (
            "ss_ready", "ms_ready", "xn_ready", "xT_done", "hT_ready")]
        proj_done, proj_out, raw_ready, raw_normed, nT_done, nT_copied, normed_ms = [sem(n) for n in (
            "proj_done", "proj_out", "raw_ready", "raw_normed", "nT_done", "nT_copied", "normed_ms")]
        new_out, sgu_done, sgu_out, row_in, row_ready, row_out = [sem(n) for n in (
            "new_out", "sgu_done", "sgu_out", "row_in", "row_ready", "row_out")]
        bm_ready, scored, win_ready, nmax_ready, exp_done, pT_done, pT_dve, pT_act = [sem(n) for n in (
            "bm_ready", "scored", "win_ready", "nmax_ready", "exp_done", "pT_done", "pT_dve", "pT_act")]
        pv_done, o_ready, aT_done, aT_copied = [sem(n) for n in ("pv_done", "o_ready", "aT_done", "aT_copied")]
        x_again, g1_in, bc_in, wout_done, x1_ready, ss2_ready, ms2_ready, h2_ready, h2_stored = [sem(n) for n in (
            "x_again", "g1_in", "bc_in", "wout_done", "x1_ready", "ss2_ready", "ms2_ready", "h2_ready", "h2_stored")]
        h2_out = [sem(f"h2_out{s}") for s in range(2)]
        h2T_done, h2T_act, h2T_dve, z_done, s_ready, m_ready, ranks_done, hot_ready, inv_done, table_ready = [
            sem(n) for n in ("h2T_done", "h2T_act", "h2T_dve", "z_done", "s_ready", "m_ready", "ranks_done",
                             "hot_ready", "inv_done", "table_ready")]
        hot_b_ready = sem("hot_b_ready")
        w13_in = [sem(f"w13_in{s}") for s in range(2)]
        w2_in = [sem(f"w2_in{s}") for s in range(2)]
        hg_in = [sem(f"hg_in{s}") for s in range(2)]
        hgT_done, hgT_act, hgT_dve, w13_done, silu_done, hid_ready, hidT_done, hidT_ready = [sem(n) for n in (
            "hgT_done", "hgT_act", "hgT_dve", "w13_done", "silu_done", "hid_ready", "hidT_done", "hidT_ready")]
        y_done, y_act, y_dve, y_stored, idx_ready = [sem(n) for n in (
            "y_done", "y_act", "y_dve", "y_stored", "idx_ready")]
        back_in = [sem(f"back_in{s}") for s in range(2)]
        fin_ready, fin_mid = sem("fin_ready"), sem("fin_mid")
        fin_out = [sem(f"fin_out{s}") for s in range(2)]
        dve_step, pool_step, act_step = [sem(n) for n in ("dve_step", "pool_step", "act_step")]

        chunks = [("ada", j) for j in range(4)] + [("in", j) for j in (0, 1, 2, 4, 3)] \
            + [("ada", j) for j in range(4, 12)] + [("out", j) for j in range(2)]
        chunk_at = {key: n for n, key in enumerate(chunks)}
        ada_v = w_ada.rearrange("(p k) n -> p k n", k=KD)
        in_v = w_in.rearrange("(p k) n -> p k n", k=KD)
        out_v = w_out.rearrange("(k p) n -> p k n", k=KD)

        def tile_rows(prompt, sample, t):
            return prompt if t == 0 else sample[(t - 1) * P:t * P]

        proj = [(0, "q", t) for t in range(TILES)] + [(1, "k", t) for t in range(TILES)] \
            + [(2, "v", t) for t in range(TILES)] + [(4, "gv", t) for t in range(TILES)] \
            + [(3, "gu", (g, w)) for g in range(GROUPS) for w in (CTX, LAT)]
        rows = [n for n, p in enumerate(proj) if p[1] in ("q", "k", "gv")]
        row_no = {n: i for i, n in enumerate(rows)}

        def positions(ap, t):
            if t == 0:
                return ap[:, :, 0:P].rearrange("p k (r c) -> p k r c", r=2)
            v = ap[:, :, P:].rearrange("p k (c r) -> p k r c", r=GRID_H)
            return v[:, :, 2 * (t - 1):2 * t, :]

        steps = [(t, h) for t in range(TILES) for h in range(HEADS)]

        ada_parts = [(j, k) for j in range(4, 12) for k in range(KD)]
        ada_of = [[a for i, a in enumerate(ada_parts) if i * (len(steps) - HEADS) // len(ada_parts) == n]
                  for n in range(len(steps))]
        ada_ends = {n: [j for j, k in parts if k == KD - 1] for n, parts in enumerate(ada_of)}
        row_at = {}
        for n, ends in ada_ends.items():
            for j in ends:
                if j % 2:
                    row_at[min(n + 2, len(steps) - 1)] = j // 2

        def span(t):
            i = t - 1
            lo, hi = max(i - 1, 0), min(i + 1, 3)
            return lo, hi - lo + 1, (LEFT_EDGE if i == 0 else RIGHT_EDGE if i == 3 else INNER)

        def key_tiles(t):
            return 1 if t == 0 else span(t)[1] + 2

        def used(key):
            kind, j = key
            if kind == "ada":
                return ada_done, j + 1
            if kind == "in":
                return proj_done, max(n for n, p in enumerate(proj) if p[0] == j) + 1
            return wout_done, 2 * TILES - 1 + j

        TE = TILES * EXPERTS
        scores_s = rcut(TE)
        sel, msel, tmp, rank = [rcut(TE) for _ in range(4)]
        hot12, tmp12 = rcut(2 * TE), rcut(2 * TE)
        hot1, hot2 = hot12[:, 0:TE], hot12[:, TE:]
        pair = rcut(TILES * EG * 6)
        gsc, ghot, gtmp, gdesc = [rcut(TILES * EG) for _ in range(4)]
        desc = rcut(EXPERTS)
        t5a, t5b = rcut(TILES), rcut(TILES)
        gate_s = rcut(10)
        nb, bend, bskip = [rcut(EXPERTS) for _ in range(3)]
        first_slot, next_blk = rcut(EXPERTS), rcut(EXPERTS)
        slotf = rcut(10)
        place_u, blk_u = rcut(10).bitcast(U32), rcut(10).bitcast(U32)
        iota_b = rcut(28)
        iota_p = rcut(P)
        ebf = rcut(28)
        cmp_e = rcut(12 * EXPERTS)
        hot_b = rcut(5 * 28).bitcast(F16)
        hot_bt = rcut(5 * 28).bitcast(F16)
        assert r_at[0] <= 6 * 512
        hot_s = rs[:, 0:5 * P].bitcast(F16)

        block = ctx.enter_context(nc.Block())

        @block.sync
        def _(sp):
            for n, (kind, j) in enumerate(chunks):
                if n >= RING:
                    sp.wait_ge(*used(chunks[n - RING]))
                src = {"ada": ada_v, "in": in_v, "out": out_v}[kind]
                sp.dma_start(ring[n % RING], src[:, :, 512 * j:512 * (j + 1)]).then_inc(ring_in[n % RING], 16)
            sp.wait_ge(ada_done, 12)
            sp.wait_ge(bc_in, 96)
            for p in range(2):
                for src, off in ((w1, 0), (w3, DE)):
                    sp.dma_start(w13[p][:, :, off:off + DE],
                                 src[p].rearrange("(p k) f -> p k f", k=KD)).then_inc(w13_in[p], 16)
            sp.wait_ge(zero_ready, 1)
            fill = slot_out[EXPERTS * P:].rearrange("(p b) (v n) -> p (b v) n", p=P, n=256)
            sp.dma_start(fill, zero[:].unsqueeze(1).to_broadcast((P, fill.shape[1], 256))).then_inc(slots_zeroed, 16)
            for t in range(TILES):
                sp.wait_ge(h2_ready, t + 1)
                sp.dma_start(h2_rows[t * P:(t + 1) * P], h2[t % 2]).then_inc(h2_out[t % 2], 16)
            sp.wait_ge(wout_done, 2 * TILES)
            for p in range(2):
                sp.dma_start(w2s[p], w2[p].rearrange("(p k) n -> p k n", k=2)).then_inc(w2_in[p], 16)
            sp.wait_ge(table_ready, 1)
            more = sp.value_load(ebi[0:1, 27:28], min_val=SHARED, max_val=MAX_BLOCKS // 2 - 1)

            def load(p, b):
                e = sp.value_load(ebi[0:1, bass.ds(b, 1)], min_val=0, max_val=EXPERTS - 1)
                for src, off in ((w1, 0), (w3, DE)):
                    sp.dma_start(w13[p][:, :, off:off + DE], src[bass.ds(e, 1)].rearrange(
                        "e (p k) f -> p (e k) f", k=KD)).then_inc(w13_in[p], 16)
                return e

            def load2(p, e):
                sp.dma_start(w2s[p], w2[bass.ds(e, 1)].rearrange("e (p k) n -> p (e k) n", k=2)).then_inc(w2_in[p], 16)

            with sp.Fori(0, more) as i:
                for p in range(2):
                    sp.wait_ge(w13_done, 2 * i + p + 1)
                    e = load(p, 2 * i + p + 2)
                    sp.wait_ge(y_done, 2 * i + p + 1)
                    load2(p, e)

        @block.gpsimd
        def _(pool):
            steps_done = [0]

            def link(ins):
                steps_done[0] += 1
                ins.then_inc(pool_step, 1)
                pool.wait_ge(pool_step, steps_done[0])

            with nc.allow_non_contiguous_dma(reason="columns of the conditioning"):
                pool.dma_start(cond[:, 0, :], c_ctx.rearrange("(p k) -> p k", k=KD)).then_inc(cond_in, 16)
                pool.dma_start(cond[:, 1, :], c.rearrange("(p k) -> p k", k=KD)).then_inc(cond_in, 16)
                pool.dma_start(x_sb[:, 0, :], x_prompt).then_inc(x_in, 16)
                pool.dma_start(x_sb[:, 1:, :], x_sample.rearrange("(t p) d -> p t d", p=P)).then_inc(x_in, 16)
                pool.dma_start(bcol, b_ada[0:2 * D].rearrange("(v p k) -> p v k", p=P, k=KD)).then_inc(small_in, 16)
                pool.dma_start(n1w, norm1_w.rearrange("(p k) -> p k", k=KD)).then_inc(small_in, 16)
            nc.gpsimd.memset(zero[:], 0.0).then_inc(zero_ready, 1)
            nc.gpsimd.memset(ones[:], 1.0).then_inc(ones_ready, 1)
            nc.gpsimd.memset(ones_b[:], 1.0).then_inc(ones_ready, 1)
            nc.gpsimd.memset(both, 0.0).then_inc(ones_ready, 1)
            pool.wait_ge(ones_ready, 3)
            nc.gpsimd.memset(mhalf, -0.5).then_inc(consts_ready, 1)
            nc.gpsimd.affine_select(out=ident[:], in_=ones[:], pattern=[[-1, P]], compare_op=ALU.is_equal,
                                    fill=0.0, base=0, channel_multiplier=1).then_inc(consts_ready, 1)
            nc.gpsimd.affine_select(out=before[:], in_=ones_b[:], pattern=[[1, P]], compare_op=ALU.is_gt,
                                    fill=0.0, base=0, channel_multiplier=-1).then_inc(consts_ready, 1)
            pool.wait_ge(zero_ready, 1)

            def mask(name, rel, side, src):
                first = GRID_H * COLS * rel
                link(nc.gpsimd.affine_select(
                    out=masks[name], in_=src, pattern=[[side * GRID_H, COLS], [0, GRID_H]],
                    compare_op=ALU.is_ge, fill=NEG,
                    base=(first + GRID_H * HALF_W + GRID_H - 1) if side > 0 else GRID_H * (HALF_W - 1) - first,
                    channel_multiplier=-side))

            mask("left", -1, 1, zero[:, 0:P])
            mask("right", 1, -1, zero[:, 0:P])
            mask("from", 0, 1, zero[:, 0:P])
            mask("upto", 0, -1, zero[:, 0:P])
            mask("both", 0, -1, masks["from"])
            pool.wait_ge(consts_ready, 3)
            pool.wait_ge(ms_ready, 1)
            nc.gpsimd.tensor_tensor(xr, xms, mhalf[:, 0:5], ALU.pow).then_inc(rstd_ready, 1)
            pool.dma_start(qw.rearrange("p (h d) -> p h d", h=HEADS),
                           q_norm_w.partition_broadcast(P).unsqueeze(1).to_broadcast((P, HEADS, HD))).then_inc(norms_in, 16)
            pool.dma_start(kw.rearrange("p (h d) -> p h d", h=HEADS),
                           k_norm_w.partition_broadcast(P).unsqueeze(1).to_broadcast((P, HEADS, HD))).then_inc(norms_in, 16)
            pool.dma_start(lnw, ln_w.partition_broadcast(P)).then_inc(norms_in, 16)
            pool.dma_start(lnb, ln_b.partition_broadcast(P)).then_inc(norms_in, 16)
            pool.dma_start(bsg, b_sgu.partition_broadcast(P)).then_inc(norms_in, 16)
            pool.dma_start(wsT, w_sgu_t).then_inc(norms_in, 16)
            pool.dma_start(ckT, cache_kt).then_inc(cache_in, 16)
            pool.dma_start(cv, cache_v.rearrange("(t p) d -> p t d", p=P)).then_inc(cache_in, 16)
            pool.dma_start(wr_sb[:], w_router.rearrange("(p k) n -> p k n", k=KD)).then_inc(cache_in, 16)
            pool.dma_start(brt, b_router.partition_broadcast(P)).then_inc(cache_in, 16)
            for half in range(2):
                ks = slice(4 * half, 4 * half + 4)
                pool.wait_ge(hT_ready, 12 + 4 * half)
                nc.gpsimd.tensor_copy(hT_rows[:, ks, :].rearrange("p k (r c) -> p k r c", c=GRID_W),
                                      hT[:, ks, P:].rearrange("p k (c r) -> p k r c", r=GRID_H)).then_inc(by_row, 1)
            for i, n in enumerate(rows):
                w = 4 if proj[n][1] == "gv" else HEADS
                pool.wait_ge(normed_ms, i + 1)
                nc.gpsimd.tensor_tensor(rsq[i % 2][:, 0:w], msq[i % 2][:, 0:w], mhalf[:, 0:w],
                                        ALU.pow).then_inc(norm_rstd_ready, 1)
            pool.wait_ge(sgu_done, TILES)
            pool.dma_start(slab, rpb_runs).then_inc(slab_in, 16)
            pool.wait_ge(slab_in, 16)
            pool.wait_ge(sgu_out, TILES)
            pool.dma_start(bias_row, b_ada[2 * D:3 * D].partition_broadcast(2)).then_inc(row_in, 16)
            pool.dma_start(n2_row, norm2_w.partition_broadcast(2)).then_inc(n2_in, 16)
            for piece, rel, name in (
                    (LEFT_EDGE, 0, "from"), (LEFT_EDGE + 1, 1, "right"), (INNER, -1, "left"), (INNER + 1, 0, "both"),
                    (INNER + 2, 1, "right"), (RIGHT_EDGE, -1, "left"), (RIGHT_EDGE + 1, 0, "upto")):
                keys = bass.AP(slab.tensor, slab.offset + COLS * (rel + 1),
                               [slab.ap[0], slab.ap[1], (1, COLS), (RPB_W, GRID_H)])
                nc.gpsimd.tensor_tensor(
                    bm[:, :, piece, :].rearrange("p h (c r) -> p h c r", r=GRID_H), keys,
                    masks[name].rearrange("p (c r) -> p c r", r=GRID_H).unsqueeze(1).to_broadcast(
                        (P, HEADS, COLS, GRID_H)), ALU.add).then_inc(bias_ready, 1)
            for v in range(3, 6):
                pool.wait_ge(ada_copied, 2 * v)
                pool.dma_start(bias_row, b_ada[v * D:(v + 1) * D].partition_broadcast(2)).then_inc(row_in, 16)
            for out, step, base, per_row in ((desc, -1, EXPERTS, 0), (iota_b, 1, 0, 0), (iota_p, 1, 0, 0),
                                             (first_slot, P, 0, 0), (next_blk, -P, P * (EXPERTS - 1), 0),
                                             (tokid, P, 0, 1)):
                nc.gpsimd.iota(out, pattern=[[step, out.shape[1]]], base=base, channel_multiplier=per_row,
                               allow_small_or_imprecise_dtypes=True).then_inc(bm_ready, 1)
            pool.wait_ge(row_out, 16 * 4)
            pool.wait_ge(scored, len(steps))
            pool.wait_ge(pv_done, len(steps))
            for cnd in range(2):
                pool.dma_start(g1b[:, cnd, :], ada_rows[2, cnd].partition_broadcast(P)).then_inc(g1_in, 16)
            for t in range(TILES):
                pool.dma_start(x_sb[:, t, :], tile_rows(x_prompt, x_sample, t)).then_inc(x_again, 16)
            pool.wait_ge(win_ready, len(steps) - HEADS)
            for cnd in range(2):
                for v in range(3):
                    pool.dma_start(bc[:, v, cnd, :], ada_rows[3 + v, cnd].partition_broadcast(P)).then_inc(bc_in, 16)
            for t in range(TILES):
                pool.wait_ge(ms2_ready, t + 1)
                nc.gpsimd.tensor_tensor(xr[:, t:t + 1], xms[:, t:t + 1], mhalf[:, 0:1], ALU.pow).then_inc(n_rstd2, 1)
            pool.wait_ge(hot_b_ready, 1)
            nc.gpsimd.tensor_tensor(hot_bt.rearrange("p (t b) -> p t b", t=TILES),
                                    hot_b.rearrange("p (t b) -> p t b", t=TILES),
                                    tokid.unsqueeze(2).to_broadcast((P, TILES, 56)), ALU.mult).then_inc(hot_b_ready, 1)
            pool.wait_ge(h2_out[0], 16 * 3)
            pool.wait_ge(h2_out[1], 16 * 2)
            pool.wait_ge(table_ready, 1)
            more = pool.value_load(ebi[0:1, 27:28], min_val=SHARED, max_val=MAX_BLOCKS // 2 - 1)

            def hold(i):
                nc.gpsimd.tensor_tensor(held[:, i:i + 1], mhalf[:, 0:1], mhalf[:, 0:1], ALU.mult)

            def gather(b, p):
                nc.gpsimd.tensor_copy(idx1[p], gidx[:, bass.ds(b, 1)]).then_inc(idx_ready, 1)
                pool.wait_ge(idx_ready, b + 1)
                hold(p)
                nc.gpsimd.indirect_dma_start(out=hg[p], out_offset=None, in_=h2_rows,
                                             in_offset=bass.IndirectOffsetOnAxis(ap=idx1[p], axis=0)
                                             ).then_inc(hg_in[p], 16)

            gather(0, 0)
            gather(1, 1)
            with pool.Fori(0, more) as i:
                for p in range(2):
                    pool.wait_ge(hgT_done, 2 * i + p + 1)
                    gather(2 * i + p + 2, p)
            pool.wait_ge(y_stored, 32 * more + 48)
            hold(2)
            for t in range(TILES):
                if t >= 2:
                    pool.wait_ge(fin_mid, t - 1)
                for j in range(2):
                    nc.gpsimd.indirect_dma_start(
                        out=y_in[t % 2][j], out_offset=None, in_=slot_out,
                        in_offset=bass.IndirectOffsetOnAxis(ap=slot_u[:, 2 * t + j:2 * t + j + 1], axis=0)
                    ).then_inc(back_in[t % 2], 16)

        @block.scalar
        def _(act):
            act.wait_ge(cond_in, 32)
            act.wait_ge(consts_ready, 3)
            nc.scalar.activation(silT.rearrange("p k c -> p c k"), cond, ACT.Silu).then_inc(silu_ready, 1)
            act.wait_ge(x_in, 32)
            for t in range(TILES):
                if t:
                    act.wait_ge(ss_ready, t)
                nc.scalar.activation(junk, x_sb[:, t, :], ACT.Square, accum_out=xss[:, t:t + 1]).then_inc(ss_ready, 1)
            act.wait_ge(cols_ready, 2)
            for half in range(2):
                act.wait_ge(xT_done, half + 1)
                for k in range(4 * half, 4 * half + 4):
                    nc.scalar.activation(hT[:, k, 0:P], banks[half][:, (k % 4) * P:(k % 4 + 1) * P], ACT.Identity,
                                         scale=colA[:, k, CTX:CTX + 1], bias=colB[:, k, CTX:CTX + 1]).then_inc(hT_ready, 1)
            for k in range(KD):
                act.wait_ge(xT_done, k + 3)
                nc.scalar.activation(hT[:, k, P:], banks[(k + 2) % 4][:], ACT.Identity,
                                     scale=colA[:, k, LAT:LAT + 1], bias=colB[:, k, LAT:LAT + 1]).then_inc(hT_ready, 1)
            for n, (_, kind, t) in enumerate(proj):
                out = banks[n % 4]
                act.wait_ge(proj_done, n + 1)
                i = row_no.get(n)
                if i is not None and i >= 2:
                    act.wait_ge(raw_normed, i - 1)
                    if proj[rows[i - 2]][1] in ("q", "k"):
                        act.wait_ge(nT_done, i - 1)
                    if proj[rows[i - 2]] == (1, "k", 0):
                        act.wait_ge(new_out, 16)
                if kind in ("q", "k"):
                    nc.scalar.activation(sq[i % 2], out[:], ACT.Square).then_inc(raw_ready, 1)
                    nc.scalar.activation(raw[i % 2], out[:], ACT.Copy).then_inc(proj_out, 1)
                elif kind == "v":
                    nc.scalar.activation(v_sb[:, t, :], out[:], ACT.Copy).then_inc(proj_out, 1)
                elif kind == "gv":
                    nc.scalar.activation(raw[i % 2], out[:], ACT.Gelu_apprx_tanh).then_inc(proj_out, 1)
                else:
                    g, w = t
                    lo, hi = (0, P) if w == CTX else (P, TOK)
                    nc.scalar.activation(uT[:, g, lo:hi], out[:, 0:hi - lo], ACT.Gelu_apprx_tanh).then_inc(proj_out, 1)
                if kind == "k" and t == 1:
                    act.wait_ge(raw_normed, TILES + 1)
                    act.dma_start(new_k, raw[TILES % 2]).then_inc(new_out, 16)
                if kind == "v" and t == 0:
                    act.wait_ge(proj_out, n + 1)
                    act.dma_start(new_v, v_sb[:, 0, :]).then_inc(new_out, 16)
            def softmax(n):
                t, h = steps[n]
                bank = 2 * (n % 2)
                nk = key_tiles(t)
                act.wait_ge(nmax_ready, n + 1)
                if n >= 2:
                    act.wait_ge(pT_done, n - 1)
                if h == 0 and t >= 2:
                    act.wait_ge(o_ready, t - 1)
                row = row_at.get(n)
                if row is not None:
                    act.wait_ge(ada_copied, 2 * row + 2)
                    if row == 4:
                        act.wait_ge(row_ready, 1)
                    act.dma_start(ada_rows[row], ada_row[:, :]).then_inc(row_out, 16)
                w = 0
                if t:
                    w = span(t)[1] * P
                    nc.scalar.activation(probs[n % 2][:, 0:w], win[n % 2][:, 0:w], ACT.Exp, bias=nmax[:, n % 2:n % 2 + 1],
                                         accum_out=sums[:, t % 2, h, 0:1]).then_inc(act_step, 1)
                    src = banks[bank + 1][:, 0:CACHE]
                else:
                    src = banks[bank + 1][:, 0:P]
                nc.scalar.activation(probs[n % 2][:, w:nk * P], src, ACT.Exp, bias=nmax[:, n % 2:n % 2 + 1],
                                     accum_out=sums[:, t % 2, h, 1:2]).then_inc(exp_done, 1)

            def copy_pT(n):
                t, h = steps[n]
                k4 = min(key_tiles(t), 3)
                act.wait_ge(pT_done, n + 1)
                if n >= 2:
                    act.wait_ge(pv_done, n - 1)
                nc.scalar.activation(pT[n % 2][:, 0:k4, :], banks[4][:, 0:k4 * P].rearrange("p (j n) -> p j n", n=P),
                                     ACT.Copy).then_inc(pT_act, 1)

            def copy_aT(t):
                act.wait_ge(aT_done, t + 1)
                nc.scalar.activation(catT[:, 0:4, t * P:(t + 1) * P],
                                     banks[4][:].rearrange("p (j n) -> p j n", n=P), ACT.Copy).then_inc(aT_copied, 1)

            for n in range(len(steps) + 2):
                if n < len(steps):
                    softmax(n)
                if 1 <= n <= len(steps):
                    copy_pT(n - 1)
                if n >= 2 and steps[n - 2][1] == HEADS - 1:
                    copy_aT(steps[n - 2][0])
            nc.scalar.activation(warm[:, 0:1], mhalf[:, 0:1], ACT.Sigmoid)
            for t in range(TILES):
                act.wait_ge(x1_ready, 2 * (t + 1))
                nc.scalar.activation(junk, x_sb[:, t, :], ACT.Square, accum_out=xss[:, t:t + 1]).then_inc(ss2_ready, 1)
                act.wait_ge(ss2_ready, t + 1)
                act.wait_ge(h2T_done, t + 1)
                if t:
                    act.wait_ge(z_done, t)
                nc.scalar.activation(h2T[:, 0:4, :], banks[4][:].rearrange("p (j n) -> p j n", n=P),
                                     ACT.Copy).then_inc(h2T_act, 1)
            act.wait_ge(z_done, TILES)
            nc.scalar.activation(scores_s, banks[6][:, 0:TILES * EXPERTS], ACT.Sigmoid).then_inc(s_ready, 1)
            nc.scalar.activation(warm[:, 1:2], mhalf[:, 0:1], ACT.Silu)
            act.wait_ge(table_ready, 1)
            more = act.value_load(ebi[0:1, 27:28], min_val=SHARED, max_val=MAX_BLOCKS // 2 - 1)

            def copy_hgT(b):
                act.wait_ge(hgT_done, b + 1)
                act.wait_ge(w13_done, b)
                nc.scalar.activation(hgT[:, 0:4, :], banks[4][:].rearrange("p (j n) -> p j n", n=P),
                                     ACT.Copy).then_inc(hgT_act, 1)

            def silu(b, p):
                act.wait_ge(w13_done, b + 1)
                act.wait_ge(hid_ready, b + 1)
                nc.scalar.activation(sil, banks[6 + p][:, 0:DE], ACT.Silu).then_inc(silu_done, 1)

            def store(b):
                act.wait_ge(y_done, b + 1)
                act.wait_ge(y_stored, 16 * (b + 1))
                nc.scalar.activation(y_sb[:, 0:512], banks[0][:], ACT.Copy).then_inc(y_act, 1)
                act.wait_ge(y_act, b + 1)
                act.wait_ge(y_dve, b + 1)
                act.dma_start(slot_out[bass.ds(b * P, P)], y_sb).then_inc(y_stored, 16)

            act.nop().then_inc(y_stored, 16)
            act.wait_ge(slots_zeroed, 16)
            act.wait_ge(hgT_done, 1)
            nc.scalar.activation(hgT[:, 0:4, :], banks[4][:].rearrange("p (j n) -> p j n", n=P),
                                 ACT.Copy).then_inc(hgT_act, 1)
            act.wait_ge(w13_done, 1)
            nc.scalar.activation(sil, banks[6][:, 0:DE], ACT.Silu).then_inc(silu_done, 1)
            copy_hgT(1)
            with act.Fori(0, more) as i:
                for p in (1, 0):
                    b = 2 * i + 2 - p
                    silu(b, p)
                    copy_hgT(b + 1)
                    store(2 * i + 1 - p)
            silu(2 * more + 1, 1)
            store(2 * more)
            store(2 * more + 1)
            for t in range(TILES):
                act.wait_ge(fin_ready, t + 1)
                act.dma_start(tile_rows(y_prompt, y_sample, t), y_fin[t % 2]).then_inc(fin_out[t % 2], 16)
            act.wait_ge(fin_out[0], 16 * 3)
            act.wait_ge(fin_out[1], 16 * 2)
            act.wait_ge(new_out, 32)

        @block.vector
        def _(dve):
            done = [0]

            def link(ins):
                done[0] += 1
                ins.then_inc(dve_step, 1)
                dve.wait_ge(dve_step, done[0])

            V = nc.vector
            dve.wait_ge(ss_ready, TILES)
            V.tensor_scalar(xms, xss, 1.0 / D, EPS, ALU.mult, ALU.add).then_inc(ms_ready, 1)
            dve.wait_ge(rstd_ready, 1)
            for t in range(TILES):
                V.tensor_scalar(x_sb[:, t, :], x_sb[:, t, :], xr[:, t:t + 1], None, ALU.mult).then_inc(xn_ready, 1)
            dve.wait_ge(small_in, 32)
            for v in range(2):
                for half in range(2):
                    dve.wait_ge(ada_done, 2 * v + half + 1)
                    if v and not half:
                        dve.wait_ge(col_done, v)
                    V.tensor_copy(ada_row[:, half * 512:(half + 1) * 512],
                                  banks[6 + half][0:2, :]).then_inc(ada_copied, 1)
                dve.wait_ge(col_done, v + 1)
                col = banks[5][:, 0:16].rearrange("p (k c) -> p k c", c=2)
                b = bcol[:, v, :].unsqueeze(2).to_broadcast((P, KD, 2))
                if v == 0:
                    V.tensor_tensor(colB, col, b, ALU.add).then_inc(cols_ready, 1)
                else:
                    link(V.tensor_tensor(colA, col, b, ALU.add))
                    link(V.tensor_scalar(colA, colA, 1.0, None, ALU.add))
                    V.tensor_tensor(colA, colA, n1w.unsqueeze(2).to_broadcast((P, KD, 2)), ALU.mult).then_inc(cols_ready, 1)
            dve.wait_ge(norms_in, 96)
            link(V.tensor_scalar(qw, qw, HD ** -0.5, None, ALU.mult))

            def norm_head(i):
                n = rows[i]
                kind = proj[n][1]
                r = raw[i % 2]
                dve.wait_ge(proj_out, n + 1)
                if kind == "gv":
                    g = r.rearrange("p (g n) -> p g n", g=GROUPS)
                    s = sq[i % 2].rearrange("p (g n) -> p g n", g=GROUPS)
                    link(V.tensor_reduce(mean, g, X, ALU.add))
                    link(V.tensor_scalar(mean, mean, -1.0 / P, None, ALU.mult))
                    link(V.tensor_tensor(g, g, mean.unsqueeze(2).to_broadcast((P, GROUPS, P)), ALU.add))
                    link(V.tensor_tensor(s, g, g, ALU.mult))
                    link(V.tensor_reduce(ssq[i % 2][:, 0:4], s, X, ALU.add))
                    V.tensor_scalar(msq[i % 2][:, 0:4], ssq[i % 2][:, 0:4], 1.0 / P, EPS, ALU.mult,
                                    ALU.add).then_inc(normed_ms, 1)
                else:
                    dve.wait_ge(raw_ready, i + 1)
                    link(V.tensor_reduce(ssq[i % 2], sq[i % 2].rearrange("p (h d) -> p h d", h=HEADS), X, ALU.add))
                    V.tensor_scalar(msq[i % 2], ssq[i % 2], 1.0 / HD, EPS, ALU.mult, ALU.add).then_inc(normed_ms, 1)

            def norm_tail(i):
                n = rows[i]
                _, kind, t = proj[n]
                r = raw[i % 2]
                dve.wait_ge(norm_rstd_ready, i + 1)
                g = GROUPS if kind == "gv" else HEADS
                rv = r.rearrange("p (g n) -> p g n", g=g)
                link(V.tensor_tensor(rv, rv, rsq[i % 2][:, 0:g].unsqueeze(2).to_broadcast((P, g, 512 // g)), ALU.mult))
                if kind == "gv":
                    link(V.tensor_tensor(r, r, lnw, ALU.mult))
                    V.tensor_tensor(vv[:, t, :], r, lnb, ALU.add).then_inc(raw_normed, 1)
                else:
                    V.tensor_tensor(r, r, qw if kind == "q" else kw, ALU.mult).then_inc(raw_normed, 1)

            def copy_nT(i):
                _, kind, t = proj[rows[i]]
                dve.wait_ge(nT_done, i + 1)
                V.tensor_copy((qT if kind == "q" else kT)[:, :, t * P:(t + 1) * P],
                              banks[4 + i % 2][:].rearrange("p (j n) -> p j n", n=P)).then_inc(nT_copied, 1)

            for i in range(len(rows)):
                norm_head(i)
                norm_tail(i)
                if 1 <= i <= 2 * TILES:
                    copy_nT(i - 1)
            dve.wait_ge(proj_out, len(proj))
            for t in range(TILES):
                dve.wait_ge(sgu_done, t + 1)
                s = sq[t % 2].rearrange("p (g n) -> p g n", g=GROUPS)
                link(V.tensor_tensor(s, banks[4 + t % 2][:].rearrange("p (g n) -> p g n", g=GROUPS),
                                     bsg.rearrange("p (g n) -> p g n", g=GROUPS), ALU.add))
                u = positions(uT, t)
                o = positions(catT[:, 4:8, :], t)
                for g in range(GROUPS):
                    ins = V.tensor_tensor(o[:, g], s[:, g].rearrange("p (r c) -> p r c", r=2), u[:, g], ALU.mult)
                ins.then_inc(sgu_out, 1)
            def ada_half(j):
                v, half = j // 2, j % 2
                if half == 0:
                    dve.wait_ge(row_in, 16 * (v - 1))
                    dve.wait_ge(n2_in, 16)
                    if v > 2:
                        dve.wait_ge(row_out, 16 * (v - 2))
                s = slice(half * 512, (half + 1) * 512)
                dve.wait_ge(ada_done, j + 1)
                V.tensor_tensor(ada_row[:, s], banks[7][0:2, :], bias_row[:, s], ALU.add).then_inc(ada_copied, 1)
                if j == 9:
                    dve.wait_ge(ada_copied, 10)
                    link(V.tensor_scalar(ada_row[:, :], ada_row[:, :], 1.0, None, ALU.add))
                    V.tensor_tensor(ada_row[:, :], ada_row[:, :], n2_row, ALU.mult).then_inc(row_ready, 1)

            def largest(n):
                t, h = steps[n]
                bank = 2 * (n % 2)
                p = n % 2
                dve.wait_ge(scored, n + 1)
                if t == 0:
                    link(V.tensor_reduce(m_ctx[:, p:p + 1], banks[bank + 1][:, 0:P], X, ALU.max))
                    V.tensor_scalar(nmax[:, p:p + 1], m_ctx[:, p:p + 1], -1.0, None, ALU.mult).then_inc(nmax_ready, 1)
                    return
                _, nt, piece = span(t)
                dve.wait_ge(bias_ready, {1: 2, 4: 7}.get(t, 5))
                V.tensor_tensor_reduce(out=win[p][:, 0:nt * P], in0=banks[bank][:, 0:nt * P],
                                       in1=bm[:, h, piece:piece + nt, :].rearrange("p v n -> p (v n)"),
                                       scale=1.0, scalar=-3e38, op0=ALU.add, op1=ALU.max,
                                       accum_out=m_win[:, p:p + 1]).then_inc(win_ready, 1)
                link(V.tensor_reduce(m_ctx[:, p:p + 1], banks[bank + 1][:, 0:CACHE], X, ALU.max))
                dve.wait_ge(win_ready, n - HEADS + 1)
                V.tensor_scalar(nmax[:, p:p + 1], m_ctx[:, p:p + 1], m_win[:, p:p + 1], -1.0, ALU.max,
                                ALU.mult).then_inc(nmax_ready, 1)

            def copy_pT(n):
                t, h = steps[n]
                nk = key_tiles(t)
                dve.wait_ge(pT_done, n + 1)
                if nk > 3:
                    if n >= 2:
                        dve.wait_ge(pv_done, n - 1)
                    V.tensor_copy(pT[n % 2][:, 3:nk, :], banks[5][:, 0:(nk - 3) * P].rearrange(
                        "p (j n) -> p j n", n=P)).then_inc(pT_dve, 1)

            def normalise(t):
                dve.wait_ge(exp_done, HEADS * (t + 1))
                if t:
                    dve.wait_ge(act_step, HEADS * t)
                    link(V.tensor_tensor(rsum, sums[:, t % 2, :, 0], sums[:, t % 2, :, 1], ALU.add))
                    link(V.reciprocal(rsum, rsum))
                else:
                    link(V.reciprocal(rsum, sums[:, 0, :, 1]))
                dve.wait_ge(pv_done, HEADS * (t + 1))
                if t:
                    dve.wait_ge(aT_done, t)
                V.tensor_tensor(o_row.rearrange("p (h d) -> p h d", h=HEADS),
                                banks[6][:].rearrange("p (h d) -> p h d", h=HEADS),
                                rsum.unsqueeze(2).to_broadcast((P, HEADS, HD)), ALU.mult).then_inc(o_ready, 1)

            for n in range(len(steps) + 2):
                if n < len(steps):
                    largest(n)
                if 1 <= n <= len(steps):
                    copy_pT(n - 1)
                for j in ada_ends.get(n - 1, ()):
                    ada_half(j)
                if n >= 2 and steps[n - 2][1] == HEADS - 1:
                    normalise(steps[n - 2][0])
            dve.wait_ge(g1_in, 32)
            dve.wait_ge(new_out, 32)

            def second_norm(t):
                cnd = LAT if t else CTX
                dve.wait_ge(ss2_ready, t + 1)
                V.tensor_scalar(xms[:, t:t + 1], xss[:, t:t + 1], 1.0 / D, EPS, ALU.mult, ALU.add).then_inc(ms2_ready, 1)
                dve.wait_ge(n_rstd2, t + 1)
                if t >= 2:
                    dve.wait_ge(h2T_done, t - 1)
                    dve.wait_ge(h2_out[t % 2], 16 * (t // 2))
                link(V.scalar_tensor_tensor(h2[t % 2], x_sb[:, t, :], xr[:, t:t + 1], bc[:, 1, cnd, :],
                                            ALU.mult, ALU.mult))
                V.tensor_tensor(h2[t % 2], h2[t % 2], bc[:, 0, cnd, :], ALU.add).then_inc(h2_ready, 1)
                dve.wait_ge(h2T_done, t + 1)
                if t:
                    dve.wait_ge(z_done, t)
                V.tensor_copy(h2T[:, 4:8, :], banks[5][:].rearrange("p (j n) -> p j n", n=P)).then_inc(h2T_dve, 1)

            for t in range(TILES):
                cnd = LAT if t else CTX
                dve.wait_ge(x_again, 16 * TILES)
                for half in range(2):
                    s = slice(half * 512, (half + 1) * 512)
                    dve.wait_ge(wout_done, 2 * t + half + 1)
                    link(V.tensor_tensor(sq[half], banks[(2 * t + half) % 4][:], g1b[:, cnd, s], ALU.mult))
                    V.tensor_tensor(x_sb[:, t, s], x_sb[:, t, s], sq[half], ALU.add).then_inc(x1_ready, 1)
                if t == 0:
                    dve.wait_ge(bc_in, 96)
                second_norm(t)

            def b3(a, n, w):
                return a.rearrange("p (t e) -> p t e", t=n)

            def wide(a, n, w):
                return a.unsqueeze(2).to_broadcast((P, n, w))

            dve.wait_ge(s_ready, 1)
            dve.wait_ge(bm_ready, 6)
            link(V.tensor_tensor(b3(sel, TILES, 16), b3(scores_s, TILES, 16),
                                 brt.unsqueeze(1).to_broadcast((P, TILES, EXPERTS)), ALU.add))
            s4 = sel.rearrange("p (g e) -> p g e", e=EPG)
            p6 = pair.rearrange("p (g e) -> p g e", e=6)
            V.tensor_tensor(p6[:, :, 0:3], s4[:, :, 0:3], s4[:, :, 1:4], ALU.add)
            V.tensor_tensor(p6[:, :, 3:5], s4[:, :, 0:2], s4[:, :, 2:4], ALU.add)
            link(V.tensor_tensor(p6[:, :, 5:6], s4[:, :, 0:1], s4[:, :, 3:4], ALU.add))
            link(V.tensor_reduce(gsc, p6, X, ALU.max))

            def first_largest(hot, val, n, t1, best, order):
                v3, h3, o3 = b3(val, TILES, n), b3(hot, TILES, n), b3(t1, TILES, n)
                link(V.tensor_reduce(best, v3, X, ALU.max))
                link(V.tensor_tensor(o3, v3, wide(best, TILES, n), ALU.is_ge))
                link(V.tensor_tensor(o3, o3, order.unsqueeze(1).to_broadcast((P, TILES, n)), ALU.mult))
                link(V.tensor_reduce(best, o3, X, ALU.max))
                link(V.tensor_tensor(h3, o3, wide(best, TILES, n), ALU.is_equal))

            first_largest(ghot, gsc, EG, gtmp, t5a, desc[:, EXPERTS - EG:])
            m4 = msel.rearrange("p (g e) -> p g e", e=EPG)
            link(V.tensor_tensor(m4, s4, wide(ghot, TILES * EG, EPG), ALU.mult))
            link(V.tensor_scalar(gtmp, ghot, 1.0, -NEG, ALU.subtract, ALU.mult))
            link(V.tensor_tensor(m4, m4, wide(gtmp, TILES * EG, EPG), ALU.add))
            first_largest(hot1, msel, EXPERTS, tmp, t5a, desc)
            link(V.scalar_tensor_tensor(msel, hot1, 3 * NEG, msel, ALU.mult, ALU.add))
            first_largest(hot2, msel, EXPERTS, tmp, t5a, desc)
            V.tensor_tensor(both[:, 0:TE], hot1, hot2, ALU.add).then_inc(m_ready, 1)
            dve.wait_ge(ranks_done, 1)
            count = banks[7][:, TE:TE + EXPERTS]
            link(V.tensor_scalar(nb, count, float(P), None, ALU.is_gt))
            for j in range(2, TILES):
                link(V.scalar_tensor_tensor(nb, count, float(j * P), nb, ALU.is_gt, ALU.add))
            link(V.tensor_tensor_scan(bend, ones[:, 0:EXPERTS], nb, 0.0, ALU.mult, ALU.add))
            link(V.tensor_tensor(bskip, bend, nb, ALU.subtract))
            link(V.scalar_tensor_tensor(bskip, bskip, float(P), next_blk, ALU.mult, ALU.add))
            ranks = b3(banks[7][:, 0:TE], TILES, 16)
            link(V.scalar_tensor_tensor(b3(rank, TILES, 16), ranks, P - 0.5,
                                        bskip.unsqueeze(1).to_broadcast((P, TILES, EXPERTS)), ALU.is_gt, ALU.mult))
            link(V.tensor_tensor(b3(rank, TILES, 16), b3(rank, TILES, 16), ranks, ALU.add))
            link(V.tensor_tensor(b3(rank, TILES, 16), b3(rank, TILES, 16),
                                 first_slot.unsqueeze(1).to_broadcast((P, TILES, EXPERTS)), ALU.add))
            link(V.tensor_tensor(tmp12.rearrange("p (k n) -> p k n", k=2), hot12.rearrange("p (k n) -> p k n", k=2),
                                 rank.unsqueeze(1).to_broadcast((P, 2, TE)), ALU.mult))
            link(V.tensor_reduce(slotf.rearrange("p (t k) -> p k t", k=2),
                                 tmp12.rearrange("p (k t e) -> p k t e", k=2, e=EXPERTS), X, ALU.add))
            link(V.tensor_copy(slot_u, slotf))
            link(V.tensor_scalar(blk_u, slot_u, 7, None, ALU.logical_shift_right))
            V.tensor_tensor(hot_b.rearrange("p (s b) -> p s b", s=10), wide(blk_u, 10, 28),
                            iota_b.unsqueeze(1).to_broadcast((P, 10, 28)), ALU.is_equal).then_inc(hot_b_ready, 1)
            link(V.tensor_scalar(place_u, slot_u, P - 1, None, ALU.bitwise_and))
            for half in range(2):
                ss = slice(5 * half, 5 * half + 5)
                V.tensor_tensor(hot_s.rearrange("p (s n) -> p s n", s=10)[:, ss], wide(place_u[:, ss], 5, P),
                                iota_p.unsqueeze(1).to_broadcast((P, 5, P)), ALU.is_equal).then_inc(hot_ready, 1)
            link(V.tensor_tensor(cmp_e.rearrange("p (b e) -> p b e", e=EXPERTS), wide(iota_b[:, 0:12], 12, EXPERTS),
                                 bend.unsqueeze(1).to_broadcast((P, 12, EXPERTS)), ALU.is_ge))
            link(V.tensor_reduce(ebf[:, EXPERTS:28], cmp_e.rearrange("p (b e) -> p b e", e=EXPERTS), X, ALU.add))
            link(V.tensor_scalar(ebf[:, EXPERTS:28], ebf[:, EXPERTS:28], float(EXPERTS - 1), None, ALU.min))
            link(V.tensor_copy(ebf[:, 0:EXPERTS], iota_b[:, 0:EXPERTS]))
            link(V.tensor_tensor(cmp_e[:, 0:5], iota_b[:, 0:10].rearrange("p (i k) -> p i k", k=2)[:, :, 0],
                                 bend[:, 15:16].to_broadcast((P, 5)), ALU.is_lt))
            link(V.tensor_reduce(ebf[:, 27:28], cmp_e[:, 0:5], X, ALU.add))
            link(V.tensor_scalar(ebf[:, 27:28], ebf[:, 27:28], float(SHARED), None, ALU.add))
            link(V.tensor_copy(ebi, ebf))
            dve.wait_ge(inv_done, 1)
            V.tensor_copy(gidx, banks[7][:, 128:156]).then_inc(table_ready, 1)
            for j, hot in enumerate((hot1, hot2)):
                link(V.tensor_tensor(tmp, scores_s, hot, ALU.mult))
                link(V.tensor_reduce(gate_s[:, 5 * j:5 * j + 5], b3(tmp, TILES, 16), X, ALU.add))
            link(V.tensor_tensor(t5a, gate_s[:, 0:5], gate_s[:, 5:10], ALU.add))
            link(V.reciprocal(t5b, t5a))
            link(V.tensor_tensor(gates, gate_s.rearrange("p (k t) -> p k t", k=2),
                                 t5b.unsqueeze(1).to_broadcast((P, 2, TILES)), ALU.mult))
            dve.wait_ge(table_ready, 1)
            more = dve.value_load(ebi[0:1, 27:28], min_val=SHARED, max_val=MAX_BLOCKS // 2 - 1)

            def copy_hgT(b):
                dve.wait_ge(hgT_done, b + 1)
                if not (isinstance(b, int) and b == 0):
                    dve.wait_ge(w13_done, b)
                V.tensor_copy(hgT[:, 4:8, :], banks[5][:].rearrange("p (j n) -> p j n", n=P)).then_inc(hgT_dve, 1)

            def hidden(b, p):
                dve.wait_ge(silu_done, b + 1)
                V.tensor_tensor(hid[p], banks[6 + p][:, DE:2 * DE], sil, ALU.mult).then_inc(hid_ready, 1)

            def copy_hidT(b):
                dve.wait_ge(hidT_done, b + 1)
                V.tensor_copy(hidT, banks[3][:, 0:2 * P].rearrange("p (j n) -> p j n", n=P)).then_inc(hidT_ready, 1)

            def copy_y(b):
                dve.wait_ge(y_done, b + 1)
                dve.wait_ge(y_stored, 16 * (b + 1))
                V.tensor_copy(y_sb[:, 512:1024], banks[1][:]).then_inc(y_dve, 1)

            V.engine_nop().then_inc(hid_ready, 1)
            copy_hgT(0)
            hidden(0, 0)
            copy_hgT(1)
            with dve.Fori(0, more) as i:
                for p in (1, 0):
                    b = 2 * i + 2 - p
                    hidden(b, p)
                    copy_hgT(b + 1)
                    copy_hidT(2 * i + 1 - p)
                    copy_y(2 * i + 1 - p)
            hidden(2 * more + 1, 1)
            for b in (2 * more, 2 * more + 1):
                copy_hidT(b)
                copy_y(b)
            for t in range(TILES):
                cnd = LAT if t else CTX
                a, b = y_in[t % 2]
                f = y_fin[t % 2]
                dve.wait_ge(back_in[t % 2], 32 * (t // 2 + 1))
                if t >= 2:
                    dve.wait_ge(fin_out[t % 2], 16 * (t // 2))
                link(V.tensor_scalar(f, a, gates[:, 0, t:t + 1], None, ALU.mult))
                ins = V.scalar_tensor_tensor(f, b, gates[:, 1, t:t + 1], f, ALU.mult, ALU.add)
                ins.then_inc(fin_mid, 1)
                dve.wait_ge(fin_mid, t + 1)
                link(V.tensor_tensor(f, f, bc[:, 2, cnd, :], ALU.mult))
                V.tensor_tensor(f, f, x_sb[:, t, :], ALU.add).then_inc(fin_ready, 1)

        @block.tensor
        def _(pe):
            T = nc.tensor

            def arrived(key):
                n = chunk_at[key]
                pe.wait_ge(ring_in[n % RING], 16 * (n // RING + 1))
                return ring[n % RING]

            def ada(j, s):
                w = arrived(("ada", j))
                bank = banks[6 + j % 2]
                if j >= 2:
                    pe.wait_ge(ada_copied, j - 1)
                for k in range(KD):
                    ins = T.matmul(bank[0:2, :], s[:, k, :], w[:, k, :], start=(k == 0), stop=(k == KD - 1))
                ins.then_inc(ada_done, 1)

            pe.wait_ge(consts_ready, 3)
            pe.wait_ge(ones_ready, 3)
            pe.wait_ge(silu_ready, 1)
            for v in range(2):
                for half in range(2):
                    ada(2 * v + half, silT)
                pe.wait_ge(ada_copied, 2 * v + 2)
                if v:
                    pe.wait_ge(cols_ready, v)
                for k in range(KD):
                    ins = T.transpose(banks[5][:, 2 * k:2 * k + 2], ada_row[:, :].rearrange(
                        "c (p k) -> c k p", k=KD)[:, k, :], ident[0:2, 0:2])
                ins.then_inc(col_done, 1)
            pe.wait_ge(xn_ready, TILES)
            xv = x_sb.rearrange("p t (c k) -> p t k c", k=KD)
            for half in range(2):
                for k in range(4 * half, 4 * half + 4):
                    ins = T.transpose(banks[half][:, (k % 4) * P:(k % 4 + 1) * P], xv[:, 0, k, :], ident[:])
                ins.then_inc(xT_done, 1)
            for k in range(KD):
                if k >= 2:
                    pe.wait_ge(hT_ready, 4 * (k - 1) if k < 4 else 8 + k - 3)
                for t in range(1, TILES):
                    ins = T.transpose(banks[(k + 2) % 4][:, (t - 1) * P:t * P], xv[:, t, k, :], ident[:])
                ins.then_inc(xT_done, 1)
            def norm_T(i):
                pe.wait_ge(raw_normed, i + 1)
                if i >= 2:
                    pe.wait_ge(nT_copied, i - 1)
                for j in range(4):
                    ins = T.transpose(banks[4 + i % 2][:, j * P:(j + 1) * P], raw[i % 2][:, j * P:(j + 1) * P], ident[:])
                ins.then_inc(nT_done, 1)

            pe.wait_ge(hT_ready, 16)
            for n, (col, kind, t) in enumerate(proj):
                w = arrived(("in", col))
                bank = banks[n % 4]
                if n >= 4:
                    pe.wait_ge(proj_out, n - 3)
                if kind == "gv" and t == 1:
                    pe.wait_ge(by_row, 2)
                for k in range(KD):
                    if kind == "gu":
                        g, part = t
                        lo, hi = (0, P) if part == CTX else (P, TOK)
                        ins = T.matmul(bank[:, 0:hi - lo], w[:, k, g * P:(g + 1) * P], hT[:, k, lo:hi],
                                       start=(k == 0), stop=(k == KD - 1))
                    else:
                        if kind == "gv" and t:
                            lhs = hT_rows[:, k, (t - 1) * P:t * P]
                        else:
                            lhs = hT[:, k, t * P:(t + 1) * P]
                        ins = T.matmul(bank[:], lhs, w[:, k, :], start=(k == 0), stop=(k == KD - 1))
                ins.then_inc(proj_done, 1)
                if 1 <= n <= 2 * TILES:
                    norm_T(n - 1)
            pe.wait_ge(raw_normed, 3 * TILES)
            pe.wait_ge(norms_in, 96)
            pe.wait_ge(nT_copied, 2 * TILES)
            for t in range(TILES):
                if t >= 2:
                    pe.wait_ge(sgu_out, t - 1)
                for g in range(GROUPS):
                    ins = T.matmul(banks[4 + t % 2][:, g * P:(g + 1) * P], vv[:, t, g * P:(g + 1) * P],
                                   wsT[:, g * P:(g + 1) * P], start=True, stop=True)
                ins.then_inc(sgu_done, 1)
            def ada_part(j, k):
                if k == 0:
                    pe.wait_ge(ada_copied, j)
                w = arrived(("ada", j))
                ins = T.matmul(banks[7][0:2, :], silT[:, k, :], w[:, k, :], start=(k == 0), stop=(k == KD - 1))
                if k == KD - 1:
                    ins.then_inc(ada_done, 1)

            def scores(n):
                t, h = steps[n]
                hp, lo = h // 2, HD * (h % 2)
                bank = 2 * (n % 2)
                if n >= 2:
                    pe.wait_ge(exp_done, n - 1)
                q = qT[lo:lo + HD, hp, t * P:(t + 1) * P]
                if t == 0:
                    T.matmul(banks[bank + 1][:, 0:P], q, kT[lo:lo + HD, hp, 0:P], start=True,
                             stop=True).then_inc(scored, 1)
                    return
                first, nt, _ = span(t)
                T.matmul(banks[bank][:, 0:nt * P], q, kT[lo:lo + HD, hp, (1 + first) * P:(1 + first + nt) * P],
                         start=True, stop=True)
                T.matmul(banks[bank + 1][:, 0:CACHE], q, ckT[lo:lo + HD, hp, :], start=True,
                         stop=True).then_inc(scored, 1)

            def prob_T(n):
                t, h = steps[n]
                pe.wait_ge(exp_done, n + 1)
                if t:
                    pe.wait_ge(act_step, n - HEADS + 1)
                if n >= 1:
                    pe.wait_ge(pT_act, n)
                    if dve_copies(n - 1):
                        pe.wait_ge(pT_dve, dve_copies(n - 1))
                if n >= 2 and steps[n - 2][1] == HEADS - 1:
                    att_T(steps[n - 2][0])
                    pe.wait_ge(aT_copied, steps[n - 2][0] + 1)
                for j in range(key_tiles(t)):
                    bank, at_ = (4, j) if j < 3 else (5, j - 3)
                    ins = T.transpose(banks[bank][:, at_ * P:(at_ + 1) * P], probs[n % 2][:, j * P:(j + 1) * P], ident[:])
                ins.then_inc(pT_done, 1)

            def dve_copies(n):
                return sum(key_tiles(steps[m][0]) > 3 for m in range(n + 1))

            def values(n):
                t, h = steps[n]
                pe.wait_ge(pT_act, n + 1)
                if dve_copies(n):
                    pe.wait_ge(pT_dve, dve_copies(n))
                if h == 0 and t:
                    pe.wait_ge(o_ready, t)
                lo = h * HD
                nk = key_tiles(t)
                for j in range(nk):
                    if t == 0:
                        v = v_sb[:, 0, lo:lo + HD]
                    elif j < nk - 2:
                        v = v_sb[:, 1 + span(t)[0] + j, lo:lo + HD]
                    else:
                        v = cv[:, j - (nk - 2), lo:lo + HD]
                    ins = T.matmul(banks[6][:, lo:lo + HD], pT[n % 2][:, j, :], v, start=(j == 0),
                                   stop=(j == nk - 1))
                ins.then_inc(pv_done, 1)

            def att_T(t):
                pe.wait_ge(o_ready, t + 1)
                for j in range(4):
                    ins = T.transpose(banks[4][:, j * P:(j + 1) * P], o_row[:, j * P:(j + 1) * P], ident[:])
                ins.then_inc(aT_done, 1)

            pe.wait_ge(cache_in, 64)
            pe.wait_ge(sgu_out, TILES)
            scores(0)
            for n in range(len(steps)):
                if n + 1 < len(steps):
                    scores(n + 1)
                for part in ada_of[n][:1]:
                    ada_part(*part)
                prob_T(n)
                for part in ada_of[n][1:]:
                    ada_part(*part)
                if n:
                    values(n - 1)
            values(len(steps) - 1)
            att_T(TILES - 1)
            pe.wait_ge(exp_done, len(steps))
            pe.wait_ge(aT_copied, TILES)

            def router(t):
                pe.wait_ge(h2_ready, t + 1)
                if t:
                    pe.wait_ge(h2T_act, t)
                    pe.wait_ge(h2T_dve, t)
                hrow = h2[t % 2].rearrange("p (c k) -> p k c", k=KD)
                for k in range(KD):
                    ins = T.transpose(banks[4 + k // 4][:, (k % 4) * P:(k % 4 + 1) * P], hrow[:, k, :], ident[:])
                ins.then_inc(h2T_done, 1)
                pe.wait_ge(h2T_act, t + 1)
                pe.wait_ge(h2T_dve, t + 1)
                for k in range(KD):
                    ins = T.matmul(banks[6][:, t * EXPERTS:(t + 1) * EXPERTS], h2T[:, k, :], wr_sb[:, k, :],
                                   start=(k == 0), stop=(k == KD - 1))
                ins.then_inc(z_done, 1)

            arrived(("out", 0))
            arrived(("out", 1))
            for t in range(TILES):
                for half in range(2):
                    n = 2 * t + half
                    w = arrived(("out", half))
                    if n >= 4:
                        pe.wait_ge(x1_ready, n - 3)
                    for k in range(KD):
                        ins = T.matmul(banks[n % 4][:], catT[:, k, t * P:(t + 1) * P], w[:, k, :],
                                       start=(k == 0), stop=(k == KD - 1))
                    ins.then_inc(wout_done, 1)
                if t:
                    router(t - 1)
            router(TILES - 1)
            pe.wait_ge(m_ready, 1)
            T.matmul(banks[7][:, 0:TE + EXPERTS], before[:], both, start=True, stop=False)
            for u in range(TILES):
                ins = T.matmul(banks[7][:, (u + 1) * EXPERTS:TE + EXPERTS].rearrange("p (t e) -> p t e", e=EXPERTS),
                               ones_b[:], both[:, u * EXPERTS:(u + 1) * EXPERTS].unsqueeze(1).to_broadcast(
                                   (P, TILES - u, EXPERTS)), start=False, stop=(u == TILES - 1))
            ins.then_inc(ranks_done, 1)
            pe.wait_ge(hot_b_ready, 2)
            for s in range(10):
                if s % 5 == 0:
                    pe.wait_ge(hot_ready, s // 5 + 1)
                ins = T.matmul(banks[7][:, 128:156], hot_s[:, s * P:(s + 1) * P], hot_bt[:, s * 28:(s + 1) * 28],
                               start=(s == 0), stop=(s == 9))
            ins.then_inc(inv_done, 1)
            pe.wait_ge(table_ready, 1)
            more = pe.value_load(ebi[0:1, 27:28], min_val=SHARED, max_val=MAX_BLOCKS // 2 - 1)

            def token_T(b, p, half):
                pe.wait_ge(hg_in[p], 16 * (half + 1))
                if not (isinstance(b, int) and b == 0):
                    pe.wait_ge(hgT_act, b)
                    pe.wait_ge(hgT_dve, b)
                hrow = hg[p].rearrange("p (c k) -> p k c", k=KD)
                for k in range(KD):
                    ins = T.transpose(banks[4 + k // 4][:, (k % 4) * P:(k % 4 + 1) * P], hrow[:, k, :], ident[:])
                ins.then_inc(hgT_done, 1)

            def up(b, p, half):
                pe.wait_ge(hgT_act, b + 1)
                pe.wait_ge(hgT_dve, b + 1)
                pe.wait_ge(w13_in[p], 32 * (half + 1))
                if not (isinstance(b, int) and b == 0):
                    pe.wait_ge(hid_ready, b)
                for k in range(KD):
                    ins = T.matmul(banks[6 + p][:], hgT[:, k, :], w13[p][:, k, :], start=(k == 0), stop=(k == KD - 1))
                ins.then_inc(w13_done, 1)

            def down(b, p, half):
                pe.wait_ge(hid_ready, b + 2)
                hrow = hid[p].rearrange("p (c k) -> p k c", k=2)
                for k in range(2):
                    ins = T.transpose(banks[3][:, k * P:(k + 1) * P], hrow[:, k, :], ident[:])
                ins.then_inc(hidT_done, 1)
                pe.wait_ge(hidT_ready, b + 1)
                pe.wait_ge(w2_in[p], 16 * (half + 1))
                if not (isinstance(b, int) and b == 0):
                    pe.wait_ge(y_act, b)
                    pe.wait_ge(y_dve, b)
                for n in range(2):
                    for k in range(2):
                        ins = T.matmul(banks[n][:], hidT[:, k, :], w2s[p][:, k, n * 512:(n + 1) * 512],
                                       start=(k == 0), stop=(k == 1))
                ins.then_inc(y_done, 1)

            token_T(0, 0, 0)
            up(0, 0, 0)
            token_T(1, 1, 0)
            with pe.Fori(0, more) as i:
                up(2 * i + 1, 1, i)
                token_T(2 * i + 2, 0, i + 1)
                down(2 * i, 0, i)
                up(2 * i + 2, 0, i + 1)
                token_T(2 * i + 3, 1, i + 1)
                down(2 * i + 1, 1, i)
            up(2 * more + 1, 1, more)
            down(2 * more, 0, more)
            down(2 * more + 1, 1, more)


_INS = ("x_prompt", "x_sample", "cache_kt", "cache_v", "c", "c_ctx", "w_ada", "b_ada", "norm1_w", "norm2_w", "w_in",
        "q_norm_w", "k_norm_w", "rpb_runs", "w_sgu_t", "b_sgu", "ln_w", "ln_b", "w_out", "w_router", "b_router", "w1",
        "w3", "w2")
_OUTS = (("y_prompt", (P, D)), ("y_sample", (4 * P, D)), ("new_k", (P, AW)), ("new_v", (P, AW)))


def kernel(x_prompt, x_sample, cache_k, cache_v, c, c_ctx, w_ada, b_ada, norm1_w, norm2_w, w_in, q_norm_w, k_norm_w,
           rpb, w_sgu, b_sgu, sgu_ln_w, sgu_ln_b, w_out, w_router, b_router, w1, w3, w2):
    import concourse.bacc as bacc
    import numpy as np
    from concourse.bass_utils import run_bass_kernel_spmd

    def a(x, *shape):
        return np.ascontiguousarray(np.asarray(x).reshape(shape))

    rpb_flat = np.zeros(2 * RPB_PAD + np.asarray(rpb).size, np.asarray(rpb).dtype)
    rpb_flat[RPB_PAD:-RPB_PAD] = np.asarray(rpb).ravel()
    rpb_runs = np.empty((P, HEADS, RUN), rpb_flat.dtype)
    for p in range(P):
        for h in range(HEADS):
            at = RPB_PAD + (h * RPB_H + GRID_H - 1 - p % GRID_H) * RPB_W - p // GRID_H - 1
            rpb_runs[p, h] = rpb_flat[at:at + RUN]
    arrays = {
        "x_prompt": a(x_prompt, P, D),
        "x_sample": np.ascontiguousarray(a(x_sample, GRID_H, GRID_W, D).transpose(1, 0, 2)).reshape(4 * P, D),
        "cache_kt": np.ascontiguousarray(a(cache_k, CACHE, 4, P).transpose(2, 1, 0)),
        "cache_v": a(cache_v, CACHE, AW), "c": a(c, D), "c_ctx": a(c_ctx, D), "w_ada": a(w_ada, D, 6 * D),
        "b_ada": a(b_ada, 6 * D), "norm1_w": a(norm1_w, D), "norm2_w": a(norm2_w, D), "w_in": a(w_in, D, 5 * AW),
        "q_norm_w": a(q_norm_w, HD), "k_norm_w": a(k_norm_w, HD), "rpb_runs": rpb_runs,
        "w_sgu_t": np.ascontiguousarray(a(w_sgu, GROUPS, P, P).transpose(2, 0, 1)).reshape(P, GROUPS * P),
        "b_sgu": a(b_sgu, GROUPS * P), "ln_w": a(sgu_ln_w, AW), "ln_b": a(sgu_ln_b, AW), "w_out": a(w_out, D, D),
        "w_router": a(w_router, D, EXPERTS), "b_router": a(b_router, EXPERTS), "w1": a(w1, EXPERTS, D, DE),
        "w3": a(w3, EXPERTS, D, DE), "w2": a(w2, EXPERTS, DE, D),
    }
    nc = bacc.Bacc("TRN2", target_bir_lowering=False, num_devices=1)
    ins = [nc.dram_tensor(n, arrays[n].shape, mybir.dt.from_np(arrays[n].dtype), kind="ExternalInput").ap()
           for n in _INS]
    outs = [nc.dram_tensor(n, shape, F32, kind="ExternalOutput").ap() for n, shape in _OUTS]
    build(nc, ins, outs)
    r = run_bass_kernel_spmd(nc, [arrays], core_ids=[0]).results[0]
    y_sample = r["y_sample"].reshape(GRID_W, GRID_H, D).transpose(1, 0, 2).reshape(1, 4 * P, D)
    return (r["y_prompt"].reshape(1, P, D), np.ascontiguousarray(y_sample), r["new_k"].reshape(1, 1, P, HEADS, HD),
            r["new_v"].reshape(1, 1, P, HEADS, HD))
```

```python
from contextlib import ExitStack

import concourse.bass as bass
from concourse import mybir

F32 = mybir.dt.float32
F32R = mybir.dt.float32r
BF16 = mybir.dt.bfloat16
F16 = mybir.dt.float16
U32 = mybir.dt.uint32
I32 = mybir.dt.int32
ALU = mybir.AluOpType
ACT = mybir.ActivationFunctionType
X = mybir.AxisListType.X

P = 128
D = 1024
KD = D // P
GRID_W, GRID_H = 64, 8
HEADS, HD = 8, 64
AW = HEADS * HD
GROUPS = 4
TILES = 5
TOK = TILES * P
CTX, LAT = 0, 1
COLS = P // GRID_H
CACHE = 256
WIN_W, HALF_W = 16, 8
RPB_W = 2 * WIN_W - 1
RPB_H = 2 * GRID_H - 1
RPB_PAD = 16
RUN = (GRID_H - 1) * RPB_W + 3 * COLS
EXPERTS, EG, EPG = 16, 4, 4
DE = 256
MAX_BLOCKS = EXPERTS + 10
SHARED = EXPERTS // 2 - 1
POOL_TILES = 3
NEG = -1e30
EPS = 1e-6
CHUNK = KD * 512
RING = 4
LAT_DVE = 6

INNER, LEFT_EDGE, RIGHT_EDGE = 0, 3, 5


def build(nc, t_in, t_out):
    (x_prompt, x_sample, cache_kt, cache_v, c, c_ctx, w_ada, b_ada, norm1_w, norm2_w, w_in, q_norm_w,
     k_norm_w, rpb_runs, w_sgu_t, b_sgu, ln_w, ln_b, w_out, w_router, b_router, w1, w3, w2) = t_in
    y_prompt, y_sample, new_k, new_v = t_out
    ctx = ExitStack()
    with ctx:
        def sb(name, shape, dt=F32):
            return ctx.enter_context(nc.sbuf_tensor(name, shape, dt))

        def sb_both(name, n):
            with nc.sbuf_tensor(name, [P, n], F32) as plain:
                pass
            return plain, sb(name + "_r", [P, n], F32R)

        def sem(name):
            return ctx.enter_context(nc.semaphore(name))

        ada_rows = nc.dram_tensor("ada_rows", (6, 2, D), F32, kind="Internal").ap()
        h2_rows = nc.dram_tensor("h2_rows", (TOK, D), F32, kind="Internal").ap()
        slot_out = nc.dram_tensor("slot_out", (MAX_BLOCKS * P, D), F32, kind="Internal").ap()

        big = sb("big", [P, RING * CHUNK + KD * TOK])
        ring = [big[:, s * CHUNK:(s + 1) * CHUNK].rearrange("p (k n) -> p k n", k=KD) for s in range(RING)]
        catT = big[:, RING * CHUNK:].rearrange("p (k n) -> p k n", k=KD)
        hT_rows = catT[:, :, 0:4 * P]
        w13 = [ring[3], ring[0]]
        w2s = [big[:, (CHUNK + s * 2 * D):(CHUNK + (s + 1) * 2 * D)].rearrange("p (k n) -> p k n", k=2)
               for s in range(2)]
        y_in = [[big[:, (2 * t + j) * D:(2 * t + j + 1) * D] for j in range(2)] for t in range(TILES)]
        y_fin = [big[:, (2 * TILES + t) * D:(2 * TILES + t + 1) * D] for t in range(TILES)]

        hu = sb("hu", [P, KD * TOK + GROUPS * TOK])
        hT = hu[:, 0:KD * TOK].rearrange("p (k n) -> p k n", k=KD)
        uT = hu[:, KD * TOK:].rearrange("p (g n) -> p g n", g=GROUPS)
        bm = hu[:, 0:HEADS * 7 * P].rearrange("p (h v n) -> p h v n", h=HEADS, v=7)
        bc = hu[:, 0:6 * D].rearrange("p (v c n) -> p v c n", v=3, c=2)

        vvr = sb("vvr", [P, TILES * AW])
        vv = vvr[:, :].rearrange("p (t n) -> p t n", t=TILES)
        slab = vvr[:, 0:HEADS * RUN].rearrange("p (h n) -> p h n", h=HEADS)
        hg = [vvr[:, s * D:(s + 1) * D] for s in range(2)]

        qk = sb("qk", [P, 5 * D])
        x_sb = qk[:, :].rearrange("p (t n) -> p t n", t=TILES)
        qT = qk[:, 0:4 * TOK].rearrange("p (k n) -> p k n", k=4)
        kT = qk[:, 4 * TOK:8 * TOK].rearrange("p (k n) -> p k n", k=4)

        vr = sb("vr", [P, TILES * AW])
        v_sb = vr[:, :].rearrange("p (t n) -> p t n", t=TILES)
        h2 = [vr[:, s * D:(s + 1) * D] for s in range(2)]
        hgT = vr[:, 0:D].rearrange("p (k n) -> p k n", k=KD)
        sil = vr[:, D:D + DE]
        hid = [vr[:, D + (1 + s) * DE:D + (2 + s) * DE] for s in range(2)]
        hidT = vr[:, D + 3 * DE:D + 4 * DE].rearrange("p (k n) -> p k n", k=2)

        cc = sb("cc", [P, 4 * CACHE + 2 * AW])
        ckT = cc[:, 0:4 * CACHE].rearrange("p (k n) -> p k n", k=4)
        cv = cc[:, 4 * CACHE:].rearrange("p (t n) -> p t n", t=2)
        g1b = cc[:, :].rearrange("p (c n) -> p c n", c=2)

        xt = sb("xt", [P, 2 * D])
        junk = xt[:, 0:D]
        probs = [xt[:, s * 640:(s + 1) * 640] for s in range(2)]
        win = [xt[:, 1280 + s * 384:1280 + (s + 1) * 384] for s in range(2)]

        po, po_r = sb_both("po", 2 * D)
        pT = [po[:, s * 640:(s + 1) * 640].rearrange("p (j n) -> p j n", j=5) for s in range(2)]
        o_row = po[:, 1280:1280 + AW]
        masks = {m: catT[:, i, 4 * P:] for i, m in enumerate(("left", "right", "from", "upto"))}
        masks["both"] = sb("mask_both", [P, P])[:, :]
        h2T = po[:, 0:D].rearrange("p (k n) -> p k n", k=KD)

        rs, rs_r = sb_both("rs", 4 * 512)
        raw = [rs[:, s * 512:(s + 1) * 512] for s in range(2)]
        sq = [rs[:, (2 + s) * 512:(3 + s) * 512] for s in range(2)]
        y_sb = rs[:, 0:D]
        wr_sb = sb("wr_sb", [P, KD, EXPERTS])
        ada_row = sb("ada_row", [2, D])
        norms = sb("norms", [P, 6 * 512])
        bias_row = norms[0:2, 0:D]
        n2_row = norms[0:2, D:2 * D]
        qw, kw, lnw, lnb, bsg, wsT = [norms[:, s * 512:(s + 1) * 512] for s in range(6)]
        ident = sb("ident", [P, P])
        ones = sb("ones", [P, P])
        before = sb("before", [P, P], BF16)
        ones_b = sb("ones_b", [P, P], BF16)
        zero = sb("zero", [P, 256])
        small = sb("small", [P, 400])
        at = [0]

        def cut(n, shape=None, dt=F32):
            a = small[:, at[0]:at[0] + n]
            at[0] += n
            a = a if dt == F32 else a.bitcast(dt)
            return a if shape is None else a.rearrange(shape[0], **shape[1])

        cond = cut(16, ("p (c k) -> p c k", dict(c=2)))
        silT = cut(16, ("p (k c) -> p k c", dict(c=2)))
        bcol = cut(16, ("p (v k) -> p v k", dict(v=2)))
        n1w = cut(8)
        colB = cut(16, ("p (k c) -> p k c", dict(c=2)))
        colA = cut(16, ("p (k c) -> p k c", dict(c=2)))
        xss, xms, xr = cut(5), cut(5), cut(5)
        mean, ssq, msq, rsq = cut(4), [cut(8) for _ in range(2)], [cut(8) for _ in range(2)], [cut(8) for _ in range(2)]
        mhalf = cut(8)
        m_win, m_ctx, nmax = [cut(2) for _ in range(3)]
        sums = cut(32, ("p (b h c) -> p b h c", dict(b=2, c=2)))
        rsum = cut(8)
        tokid = cut(5)
        brt = cut(16)
        gates = cut(10, ("p (k t) -> p k t", dict(k=2)))
        slot_u = cut(10, None, U32)
        gidx = cut(28, None, U32)
        ebi = cut(28, None, I32)
        held = cut(3)
        warm = cut(2)
        both = cut((TILES + 1) * EXPERTS // 2).bitcast(BF16)
        idx1 = [cut(1, None, U32) for _ in range(2)]
        r_at = [0]

        def rcut(n):
            a = norms[:, r_at[0]:r_at[0] + n]
            r_at[0] += n
            return a

        sil_r = sb("sil_r", [P, 4 * KD], F32R)[:, :].rearrange("p (k s c) -> p k s c", s=2, c=2)

        part_bufs = [(buf[:, i * 512:(i + 1) * 512], buf[:, (i + 1) * 512:(i + 2) * 512])
                     for buf in (rs_r, po_r) for i in (0, 2)]

        def parts(q):
            return part_bufs[q % len(part_bufs)]

        banks = [ctx.enter_context(nc.psum_tensor(f"bank{i}", [P, 512], F32)) for i in range(8)]

        cond_in, small_in, norms_in, cache_in, slab_in = [sem(n) for n in (
            "cond_in", "small_in", "norms_in", "cache_in", "slab_in")]
        x_in = [sem(f"x_in{t}") for t in range(TILES)]
        ring_in = [sem(f"ring_in{s}") for s in range(RING)]
        zero_ready, slots_zeroed, bias_ready = sem("zero_ready"), sem("slots_zeroed"), sem("bias_ready")
        by_row, ones_ready, n2_in, consts_ready, rstd_ready, norm_rstd_ready, n_rstd2 = [sem(n) for n in (
            "by_row", "ones_ready", "n2_in", "consts_ready", "rstd_ready", "norm_rstd_ready", "n_rstd2")]
        sil_hi, sil_lo, hi_ready, lo_ready, part_used = [sem(n) for n in (
            "sil_hi", "sil_lo", "hi_ready", "lo_ready", "part_used")]
        silu_ready, ada_done, ada_copied, col_done, cols_ready = [sem(n) for n in (
            "silu_ready", "ada_done", "ada_copied", "col_done", "cols_ready")]
        ss_ready, ms_ready, xn_ready, xT_done, xT_act, xT_dve, hT_act, hT_dve = [sem(n) for n in (
            "ss_ready", "ms_ready", "xn_ready", "xT_done", "xT_act", "xT_dve", "hT_act", "hT_dve")]
        proj_done, proj_out, raw_ready, raw_normed, nT_done, nT_copied, normed_ms = [sem(n) for n in (
            "proj_done", "proj_out", "raw_ready", "raw_normed", "nT_done", "nT_copied", "normed_ms")]
        new_out, sgu_done, sgu_out, row_in, row_ready, row_out = [sem(n) for n in (
            "new_out", "sgu_done", "sgu_out", "row_in", "row_ready", "row_out")]
        bm_ready, scored, win_ready, nmax_ready, exp_done, pT_done, pT_dve, pT_act = [sem(n) for n in (
            "bm_ready", "scored", "win_ready", "nmax_ready", "exp_done", "pT_done", "pT_dve", "pT_act")]
        pv_done, o_ready, aT_done, aT_copied = [sem(n) for n in ("pv_done", "o_ready", "aT_done", "aT_copied")]
        x_again, g1_in, bc_in, wout_done, x1_ready, ss2_ready, ms2_ready, h2_ready, h2_stored = [sem(n) for n in (
            "x_again", "g1_in", "bc_in", "wout_done", "x1_ready", "ss2_ready", "ms2_ready", "h2_ready", "h2_stored")]
        h2_out = [sem(f"h2_out{s}") for s in range(2)]
        h2T_done, h2T_act, h2T_dve, z_done, s_ready, m_ready, ranks_done, hot_ready, inv_done, table_ready = [
            sem(n) for n in ("h2T_done", "h2T_act", "h2T_dve", "z_done", "s_ready", "m_ready", "ranks_done",
                             "hot_ready", "inv_done", "table_ready")]
        hot_b_ready, gates_ready = sem("hot_b_ready"), sem("gates_ready")
        w13_in = [sem(f"w13_in{s}") for s in range(2)]
        w2_in = [sem(f"w2_in{s}") for s in range(2)]
        hg_in = [sem(f"hg_in{s}") for s in range(2)]
        hgT_done, hgT_act, hgT_dve, w13_done, silu_done, hid_ready, hidT_done, hidT_ready = [sem(n) for n in (
            "hgT_done", "hgT_act", "hgT_dve", "w13_done", "silu_done", "hid_ready", "hidT_done", "hidT_ready")]
        y_done, y_act, y_dve, y_stored, idx_ready = [sem(n) for n in (
            "y_done", "y_act", "y_dve", "y_stored", "idx_ready")]
        back_in = [sem(f"back_in{t}") for t in range(TILES)]
        fin_first, fin_moe, fin_ready, fin_last, fin_out = [sem(n) for n in (
            "fin_first", "fin_moe", "fin_ready", "fin_last", "fin_out")]
        dve_step, pool_step, act_step = [sem(n) for n in ("dve_step", "pool_step", "act_step")]

        chunks = [("ada", j) for j in range(4)] + [("in", j) for j in (0, 1, 2, 4, 3)] \
            + [("ada", j) for j in range(4, 12)] + [("out", j) for j in range(2)]
        chunk_at = {key: n for n, key in enumerate(chunks)}
        ada_v = w_ada.rearrange("(p k) n -> p k n", k=KD)
        in_v = w_in.rearrange("(p k) n -> p k n", k=KD)
        out_v = w_out.rearrange("(k p) n -> p k n", k=KD)

        def tile_rows(prompt, sample, t):
            return prompt if t == 0 else sample[(t - 1) * P:t * P]

        proj = [(0, "q", t) for t in range(TILES)] + [(1, "k", t) for t in range(TILES)] \
            + [(2, "v", t) for t in range(TILES)] + [(4, "gv", t) for t in range(TILES)] \
            + [(3, "gu", (g, w)) for g in range(GROUPS) for w in (CTX, LAT)]
        rows = [n for n, p in enumerate(proj) if p[1] in ("q", "k", "gv")]
        row_no = {n: i for i, n in enumerate(rows)}

        def positions(ap, t):
            if t == 0:
                return ap[:, :, 0:P].rearrange("p k (r c) -> p k r c", r=2)
            v = ap[:, :, P:].rearrange("p k (c r) -> p k r c", r=GRID_H)
            return v[:, :, 2 * (t - 1):2 * t, :]

        steps = [(t, h) for t in range(TILES) for h in range(HEADS)]

        ada_parts = [(j, k) for j in range(4, 12) for k in range(KD)]
        ada_of = [[a for i, a in enumerate(ada_parts) if i * (len(steps) - HEADS) // len(ada_parts) == n]
                  for n in range(len(steps))]
        ada_ends = {n: [j for j, k in parts if k == KD - 1] for n, parts in enumerate(ada_of)}
        row_at = {}
        for n, ends in ada_ends.items():
            for j in ends:
                if j % 2:
                    row_at[min(n + 2, len(steps) - 1)] = j // 2

        def slice_at(q):
            n = chunk_at[("ada", q // KD)]
            return ring[n % RING][:, q % KD, :], (ring_in[n % RING], 16 * (n // RING + 1))

        def span(t):
            i = t - 1
            lo, hi = max(i - 1, 0), min(i + 1, 3)
            return lo, hi - lo + 1, (LEFT_EDGE if i == 0 else RIGHT_EDGE if i == 3 else INNER)

        def key_tiles(t):
            return 1 if t == 0 else span(t)[1] + 2

        def used(key):
            kind, j = key
            if kind == "ada":
                return (part_used, KD * (j + 1)) if j < 4 else (ada_done, j - 3)
            if kind == "in":
                return proj_done, max(n for n, p in enumerate(proj) if p[0] == j) + 1
            return wout_done, 2 * TILES - 1 + j

        TE = TILES * EXPERTS
        scores_s = rcut(TE)
        sel, msel, tmp, rank = [rcut(TE) for _ in range(4)]
        hot12, tmp12 = rcut(2 * TE), rcut(2 * TE)
        hot1, hot2 = hot12[:, 0:TE], hot12[:, TE:]
        pair = rcut(TILES * EG * 6)
        gsc, ghot, gtmp, gdesc = [rcut(TILES * EG) for _ in range(4)]
        desc = rcut(EXPERTS)
        t5a, t5b = rcut(TILES), rcut(TILES)
        gate_s = rcut(10)
        nb, bend, bskip = [rcut(EXPERTS) for _ in range(3)]
        first_slot, next_blk = rcut(EXPERTS), rcut(EXPERTS)
        slotf = rcut(10)
        place_u, blk_u = rcut(10).bitcast(U32), rcut(10).bitcast(U32)
        iota_b = rcut(28)
        iota_p = rcut(P)
        ebf = rcut(28)
        cmp_e = rcut(12 * EXPERTS)
        hot_b = rcut(5 * 28).bitcast(F16)
        hot_bt = rcut(5 * 28).bitcast(F16)
        assert r_at[0] <= 6 * 512
        hot_s = rs[:, 0:5 * P].bitcast(F16)

        block = ctx.enter_context(nc.Block())

        @block.sync
        def _(sp):
            for t in range(TILES):
                sp.dma_start(x_sb[:, t, :], tile_rows(x_prompt, x_sample, t)).then_inc(x_in[t], 16)
            for n, (kind, j) in enumerate(chunks):
                if (kind, j) == ("ada", 4):
                    sp.wait_ge(zero_ready, 1)
                    fill = slot_out[EXPERTS * P:].rearrange("(p b) (v n) -> p (b v) n", p=P, n=256)
                    sp.dma_start(fill, zero[:].unsqueeze(1).to_broadcast((P, fill.shape[1], 256))).then_inc(
                        slots_zeroed, 16)
                if n >= RING:
                    sp.wait_ge(*used(chunks[n - RING]))
                src = {"ada": ada_v, "in": in_v, "out": out_v}[kind]
                sp.dma_start(ring[n % RING], src[:, :, 512 * j:512 * (j + 1)]).then_inc(ring_in[n % RING], 16)
            sp.wait_ge(ada_done, 8)
            sp.wait_ge(bc_in, 96)
            for p in range(2):
                for src, off in ((w1, 0), (w3, DE)):
                    sp.dma_start(w13[p][:, :, off:off + DE],
                                 src[p].rearrange("(p k) f -> p k f", k=KD)).then_inc(w13_in[p], 16)
            for t in range(TILES):
                sp.wait_ge(h2_ready, t + 1)
                sp.dma_start(h2_rows[t * P:(t + 1) * P], h2[t % 2]).then_inc(h2_out[t % 2], 16)
            sp.wait_ge(wout_done, 2 * TILES)
            for p in range(2):
                sp.dma_start(w2s[p], w2[p].rearrange("(p k) n -> p k n", k=2)).then_inc(w2_in[p], 16)
            sp.wait_ge(table_ready, 1)
            more = sp.value_load(ebi[0:1, 27:28], min_val=SHARED, max_val=MAX_BLOCKS // 2 - 1)

            def load(p, b):
                e = sp.value_load(ebi[0:1, bass.ds(b, 1)], min_val=0, max_val=EXPERTS - 1)
                for src, off in ((w1, 0), (w3, DE)):
                    sp.dma_start(w13[p][:, :, off:off + DE], src[bass.ds(e, 1)].rearrange(
                        "e (p k) f -> p (e k) f", k=KD)).then_inc(w13_in[p], 16)
                return e

            def load2(p, e):
                sp.dma_start(w2s[p], w2[bass.ds(e, 1)].rearrange("e (p k) n -> p (e k) n", k=2)).then_inc(w2_in[p], 16)

            with sp.Fori(0, more) as i:
                for p in range(2):
                    sp.wait_ge(w13_done, 2 * i + p + 1)
                    e = load(p, 2 * i + p + 2)
                    sp.wait_ge(y_done, 2 * i + p + 1)
                    load2(p, e)
            for t in range(TILES):
                if t < POOL_TILES:
                    sp.wait_ge(fin_ready, t + 1)
                else:
                    sp.wait_ge(fin_last, t - POOL_TILES + 1)
                sp.dma_start(tile_rows(y_prompt, y_sample, t), y_fin[t]).then_inc(fin_out, 16)
            sp.wait_ge(fin_out, 16 * TILES)

        @block.gpsimd
        def _(pool):
            steps_done = [0]

            def link(ins):
                steps_done[0] += 1
                ins.then_inc(pool_step, 1)
                pool.wait_ge(pool_step, steps_done[0])

            nc.gpsimd.memset(zero[:], 0.0).then_inc(zero_ready, 1)
            nc.gpsimd.memset(ones[:], 1.0).then_inc(ones_ready, 1)
            nc.gpsimd.memset(ones_b[:], 1.0).then_inc(ones_ready, 1)
            nc.gpsimd.memset(both, 0.0).then_inc(ones_ready, 1)
            pool.wait_ge(ones_ready, 3)
            nc.gpsimd.memset(mhalf, -0.5).then_inc(consts_ready, 1)
            nc.gpsimd.affine_select(out=ident[:], in_=ones[:], pattern=[[-1, P]], compare_op=ALU.is_equal,
                                    fill=0.0, base=0, channel_multiplier=1).then_inc(consts_ready, 1)
            nc.gpsimd.affine_select(out=before[:], in_=ones_b[:], pattern=[[1, P]], compare_op=ALU.is_gt,
                                    fill=0.0, base=0, channel_multiplier=-1).then_inc(consts_ready, 1)
            pool.wait_ge(consts_ready, 3)
            for t in range(TILES):
                pool.wait_ge(ms_ready, t + 1)
                nc.gpsimd.tensor_tensor(xr[:, t:t + 1], xms[:, t:t + 1], mhalf[:, 0:1], ALU.pow).then_inc(rstd_ready, 1)
            pool.wait_ge(zero_ready, 1)

            def mask(name, rel, side, src):
                first = GRID_H * COLS * rel
                link(nc.gpsimd.affine_select(
                    out=masks[name], in_=src, pattern=[[side * GRID_H, COLS], [0, GRID_H]],
                    compare_op=ALU.is_ge, fill=NEG,
                    base=(first + GRID_H * HALF_W + GRID_H - 1) if side > 0 else GRID_H * (HALF_W - 1) - first,
                    channel_multiplier=-side))

            mask("left", -1, 1, zero[:, 0:P])
            mask("right", 1, -1, zero[:, 0:P])
            mask("from", 0, 1, zero[:, 0:P])
            mask("upto", 0, -1, zero[:, 0:P])
            mask("both", 0, -1, masks["from"])
            pool.wait_ge(part_used, 3 * KD)
            pool.dma_start(qw.rearrange("p (h d) -> p h d", h=HEADS),
                           q_norm_w.partition_broadcast(P).unsqueeze(1).to_broadcast((P, HEADS, HD))).then_inc(norms_in, 16)
            pool.dma_start(kw.rearrange("p (h d) -> p h d", h=HEADS),
                           k_norm_w.partition_broadcast(P).unsqueeze(1).to_broadcast((P, HEADS, HD))).then_inc(norms_in, 16)
            pool.dma_start(lnw, ln_w.partition_broadcast(P)).then_inc(norms_in, 16)
            pool.dma_start(lnb, ln_b.partition_broadcast(P)).then_inc(norms_in, 16)
            pool.dma_start(bsg, b_sgu.partition_broadcast(P)).then_inc(norms_in, 16)
            pool.dma_start(wsT, w_sgu_t).then_inc(norms_in, 16)
            pool.dma_start(ckT, cache_kt).then_inc(cache_in, 16)
            pool.dma_start(cv, cache_v.rearrange("(t p) d -> p t d", p=P)).then_inc(cache_in, 16)
            pool.dma_start(wr_sb[:], w_router.rearrange("(p k) n -> p k n", k=KD)).then_inc(cache_in, 16)
            pool.dma_start(brt, b_router.partition_broadcast(P)).then_inc(cache_in, 16)
            for i, n in enumerate(rows):
                w = 4 if proj[n][1] == "gv" else HEADS
                pool.wait_ge(normed_ms, i + 1)
                nc.gpsimd.tensor_tensor(rsq[i % 2][:, 0:w], msq[i % 2][:, 0:w], mhalf[:, 0:w],
                                        ALU.pow).then_inc(norm_rstd_ready, 1)
                if 1 <= i <= KD:
                    if i == 1:
                        pool.wait_ge(hT_dve, KD + LAT_DVE)
                        pool.wait_ge(hT_act, KD - LAT_DVE)
                    k = i - 1
                    nc.gpsimd.tensor_copy(hT_rows[:, k, :].rearrange("p (r c) -> p r c", c=GRID_W),
                                          hT[:, k, P:].rearrange("p (c r) -> p r c", r=GRID_H)).then_inc(by_row, 1)
            pool.wait_ge(sgu_done, TILES)
            pool.dma_start(slab, rpb_runs).then_inc(slab_in, 16)
            pool.wait_ge(slab_in, 16)
            pool.wait_ge(sgu_out, TILES)
            pool.dma_start(bias_row, b_ada[2 * D:3 * D].partition_broadcast(2)).then_inc(row_in, 16)
            pool.dma_start(n2_row, norm2_w.partition_broadcast(2)).then_inc(n2_in, 16)
            for piece, rel, name in (
                    (LEFT_EDGE, 0, "from"), (LEFT_EDGE + 1, 1, "right"), (INNER, -1, "left"), (INNER + 1, 0, "both"),
                    (INNER + 2, 1, "right"), (RIGHT_EDGE, -1, "left"), (RIGHT_EDGE + 1, 0, "upto")):
                keys = bass.AP(slab.tensor, slab.offset + COLS * (rel + 1),
                               [slab.ap[0], slab.ap[1], (1, COLS), (RPB_W, GRID_H)])
                nc.gpsimd.tensor_tensor(
                    bm[:, :, piece, :].rearrange("p h (c r) -> p h c r", r=GRID_H), keys,
                    masks[name].rearrange("p (c r) -> p c r", r=GRID_H).unsqueeze(1).to_broadcast(
                        (P, HEADS, COLS, GRID_H)), ALU.add).then_inc(bias_ready, 1)
            for v in range(3, 6):
                pool.wait_ge(ada_copied, 2 * v)
                pool.dma_start(bias_row, b_ada[v * D:(v + 1) * D].partition_broadcast(2)).then_inc(row_in, 16)
            pool.wait_ge(row_out, 16 * 4)
            pool.wait_ge(scored, len(steps))
            pool.wait_ge(pv_done, len(steps))
            for cnd in range(2):
                pool.dma_start(g1b[:, cnd, :], ada_rows[2, cnd].partition_broadcast(P)).then_inc(g1_in, 16)
            for t in range(TILES):
                pool.dma_start(x_sb[:, t, :], tile_rows(x_prompt, x_sample, t)).then_inc(x_again, 16)
            pool.wait_ge(win_ready, len(steps) - HEADS)
            for cnd in range(2):
                for v in range(3):
                    pool.dma_start(bc[:, v, cnd, :], ada_rows[3 + v, cnd].partition_broadcast(P)).then_inc(bc_in, 16)
            for out, step, base, per_row in ((desc, -1, EXPERTS, 0), (iota_b, 1, 0, 0), (iota_p, 1, 0, 0),
                                             (first_slot, P, 0, 0), (next_blk, -P, P * (EXPERTS - 1), 0),
                                             (tokid, P, 0, 1)):
                nc.gpsimd.iota(out, pattern=[[step, out.shape[1]]], base=base, channel_multiplier=per_row,
                               allow_small_or_imprecise_dtypes=True).then_inc(bm_ready, 1)
            for t in range(TILES):
                pool.wait_ge(ms2_ready, t + 1)
                nc.gpsimd.tensor_tensor(xr[:, t:t + 1], xms[:, t:t + 1], mhalf[:, 0:1], ALU.pow).then_inc(n_rstd2, 1)
            pool.wait_ge(hot_b_ready, 1)
            nc.gpsimd.tensor_tensor(hot_bt.rearrange("p (t b) -> p t b", t=TILES),
                                    hot_b.rearrange("p (t b) -> p t b", t=TILES),
                                    tokid.unsqueeze(2).to_broadcast((P, TILES, 56)), ALU.mult).then_inc(hot_b_ready, 1)
            pool.wait_ge(h2_out[0], 16 * 3)
            pool.wait_ge(h2_out[1], 16 * 2)
            pool.wait_ge(table_ready, 1)
            more = pool.value_load(ebi[0:1, 27:28], min_val=SHARED, max_val=MAX_BLOCKS // 2 - 1)

            def hold(i):
                nc.gpsimd.tensor_tensor(held[:, i:i + 1], mhalf[:, 0:1], mhalf[:, 0:1], ALU.mult)

            def gather(b, p):
                nc.gpsimd.tensor_copy(idx1[p], gidx[:, bass.ds(b, 1)]).then_inc(idx_ready, 1)
                pool.wait_ge(idx_ready, b + 1)
                hold(p)
                nc.gpsimd.indirect_dma_start(out=hg[p], out_offset=None, in_=h2_rows,
                                             in_offset=bass.IndirectOffsetOnAxis(ap=idx1[p], axis=0)
                                             ).then_inc(hg_in[p], 16)

            gather(0, 0)
            gather(1, 1)
            with pool.Fori(0, more) as i:
                for p in range(2):
                    pool.wait_ge(hgT_done, 2 * i + p + 1)
                    gather(2 * i + p + 2, p)
            pool.wait_ge(y_stored, 32 * more + 48)
            hold(2)
            for t in range(TILES):
                for j in range(2):
                    nc.gpsimd.indirect_dma_start(
                        out=y_in[t][j], out_offset=None, in_=slot_out,
                        in_offset=bass.IndirectOffsetOnAxis(ap=slot_u[:, 2 * t + j:2 * t + j + 1], axis=0)
                    ).then_inc(back_in[t], 16)
            for t in range(POOL_TILES):
                pool.wait_ge(fin_moe, t + 1)
                nc.gpsimd.tensor_tensor(y_fin[t], y_fin[t], x_sb[:, t, :], ALU.add).then_inc(fin_ready, 1)

        @block.scalar
        def _(act):
            with nc.allow_non_contiguous_dma(reason="columns of the conditioning"):
                act.dma_start(cond[:, 0, :], c_ctx.rearrange("(p k) -> p k", k=KD)).then_inc(cond_in, 16)
                act.dma_start(cond[:, 1, :], c.rearrange("(p k) -> p k", k=KD)).then_inc(cond_in, 16)
                act.dma_start(bcol, b_ada[0:2 * D].rearrange("(v p k) -> p v k", p=P, k=KD)).then_inc(small_in, 16)
                act.dma_start(n1w, norm1_w.rearrange("(p k) -> p k", k=KD)).then_inc(small_in, 16)
            act.wait_ge(cond_in, 32)
            act.wait_ge(consts_ready, 3)
            nc.scalar.activation(silT.rearrange("p k c -> p c k"), cond, ACT.Silu).then_inc(silu_ready, 1)
            act.wait_ge(silu_ready, 1)
            nc.scalar.activation(sil_r[:, :, 0, :], silT, ACT.Copy).then_inc(sil_hi, 1)

            def split_hi(q):
                hi, _ = parts(q)
                w, arrival = slice_at(q)
                act.wait_ge(*arrival)
                if q >= len(part_bufs):
                    act.wait_ge(part_used, q - len(part_bufs) + 1)
                nc.scalar.activation(hi, w, ACT.Copy).then_inc(hi_ready, 1)

            def copy_xT(t):
                act.wait_ge(xT_done, t + 1)
                nc.scalar.activation(hT[:, 0:4, t * P:(t + 1) * P], banks[2 * (t % 3)][:].rearrange(
                    "p (k n) -> p k n", n=P), ACT.Copy).then_inc(xT_act, 1)

            for t in range(TILES):
                act.wait_ge(x_in[t], 16)
                if t:
                    act.wait_ge(ss_ready, t)
                nc.scalar.activation(junk, x_sb[:, t, :], ACT.Square, accum_out=xss[:, t:t + 1]).then_inc(ss_ready, 1)
            for t in range(TILES):
                copy_xT(t)
            for q in range(4 * KD):
                split_hi(q)
            act.wait_ge(cols_ready, 2)
            act.wait_ge(xT_dve, TILES)
            for k in range(LAT_DVE, KD):
                nc.scalar.activation(hT[:, k, P:], hT[:, k, P:], ACT.Identity, scale=colA[:, k, LAT:LAT + 1],
                                     bias=colB[:, k, LAT:LAT + 1]).then_inc(hT_act, 1)
            for n, (_, kind, t) in enumerate(proj):
                out = banks[n % 4]
                act.wait_ge(proj_done, n + 1)
                i = row_no.get(n)
                if i is not None and i >= 2:
                    act.wait_ge(raw_normed, i - 1)
                    if proj[rows[i - 2]][1] in ("q", "k"):
                        act.wait_ge(nT_done, i - 1)
                    if proj[rows[i - 2]] == (1, "k", 0):
                        act.wait_ge(new_out, 16)
                if kind in ("q", "k"):
                    nc.scalar.activation(sq[i % 2], out[:], ACT.Square).then_inc(raw_ready, 1)
                    nc.scalar.activation(raw[i % 2], out[:], ACT.Copy).then_inc(proj_out, 1)
                elif kind == "v":
                    nc.scalar.activation(v_sb[:, t, :], out[:], ACT.Copy).then_inc(proj_out, 1)
                elif kind == "gv":
                    nc.scalar.activation(raw[i % 2], out[:], ACT.Gelu_apprx_tanh).then_inc(proj_out, 1)
                else:
                    g, w = t
                    lo, hi = (0, P) if w == CTX else (P, TOK)
                    nc.scalar.activation(uT[:, g, lo:hi], out[:, 0:hi - lo], ACT.Gelu_apprx_tanh).then_inc(proj_out, 1)
                if kind == "k" and t == 1:
                    act.wait_ge(raw_normed, TILES + 1)
                    act.dma_start(new_k, raw[TILES % 2]).then_inc(new_out, 16)
                if kind == "v" and t == 0:
                    act.wait_ge(proj_out, n + 1)
                    act.dma_start(new_v, v_sb[:, 0, :]).then_inc(new_out, 16)
            def softmax(n):
                t, h = steps[n]
                bank = 2 * (n % 2)
                nk = key_tiles(t)
                act.wait_ge(nmax_ready, n + 1)
                if n >= 2:
                    act.wait_ge(pT_done, n - 1)
                if h == 0 and t >= 2:
                    act.wait_ge(o_ready, t - 1)
                row = row_at.get(n)
                if row is not None:
                    act.wait_ge(ada_copied, 2 * row + 2)
                    if row == 4:
                        act.wait_ge(row_ready, 1)
                    act.dma_start(ada_rows[row], ada_row[:, :]).then_inc(row_out, 16)
                w = 0
                if t:
                    w = span(t)[1] * P
                    nc.scalar.activation(probs[n % 2][:, 0:w], win[n % 2][:, 0:w], ACT.Exp, bias=nmax[:, n % 2:n % 2 + 1],
                                         accum_out=sums[:, t % 2, h, 0:1]).then_inc(act_step, 1)
                    src = banks[bank + 1][:, 0:CACHE]
                else:
                    src = banks[bank + 1][:, 0:P]
                nc.scalar.activation(probs[n % 2][:, w:nk * P], src, ACT.Exp, bias=nmax[:, n % 2:n % 2 + 1],
                                     accum_out=sums[:, t % 2, h, 1:2]).then_inc(exp_done, 1)

            def copy_pT(n):
                t, h = steps[n]
                k4 = min(key_tiles(t), 3)
                act.wait_ge(pT_done, n + 1)
                if n >= 2:
                    act.wait_ge(pv_done, n - 1)
                nc.scalar.activation(pT[n % 2][:, 0:k4, :], banks[4][:, 0:k4 * P].rearrange("p (j n) -> p j n", n=P),
                                     ACT.Copy).then_inc(pT_act, 1)

            def copy_aT(t):
                act.wait_ge(aT_done, t + 1)
                nc.scalar.activation(catT[:, 0:4, t * P:(t + 1) * P],
                                     banks[4][:].rearrange("p (j n) -> p j n", n=P), ACT.Copy).then_inc(aT_copied, 1)

            for n in range(len(steps) + 2):
                if n < len(steps):
                    softmax(n)
                if 1 <= n <= len(steps):
                    copy_pT(n - 1)
                if n >= 2 and steps[n - 2][1] == HEADS - 1:
                    copy_aT(steps[n - 2][0])
            nc.scalar.activation(warm[:, 0:1], mhalf[:, 0:1], ACT.Sigmoid)
            for t in range(TILES):
                act.wait_ge(x1_ready, 2 * (t + 1))
                nc.scalar.activation(junk, x_sb[:, t, :], ACT.Square, accum_out=xss[:, t:t + 1]).then_inc(ss2_ready, 1)
                act.wait_ge(ss2_ready, t + 1)
                act.wait_ge(h2T_done, t + 1)
                if t:
                    act.wait_ge(z_done, t)
                nc.scalar.activation(h2T[:, 0:4, :], banks[4][:].rearrange("p (j n) -> p j n", n=P),
                                     ACT.Copy).then_inc(h2T_act, 1)
            act.wait_ge(z_done, TILES)
            nc.scalar.activation(scores_s, banks[6][:, 0:TILES * EXPERTS], ACT.Sigmoid).then_inc(s_ready, 1)
            nc.scalar.activation(warm[:, 1:2], mhalf[:, 0:1], ACT.Silu)
            act.wait_ge(table_ready, 1)
            more = act.value_load(ebi[0:1, 27:28], min_val=SHARED, max_val=MAX_BLOCKS // 2 - 1)

            def copy_hgT(b):
                act.wait_ge(hgT_done, b + 1)
                act.wait_ge(w13_done, b)
                nc.scalar.activation(hgT[:, 0:4, :], banks[4][:].rearrange("p (j n) -> p j n", n=P),
                                     ACT.Copy).then_inc(hgT_act, 1)

            def silu(b, p):
                act.wait_ge(w13_done, b + 1)
                act.wait_ge(hid_ready, b + 1)
                nc.scalar.activation(sil, banks[6 + p][:, 0:DE], ACT.Silu).then_inc(silu_done, 1)

            def store(b):
                act.wait_ge(y_done, b + 1)
                act.wait_ge(y_stored, 16 * (b + 1))
                nc.scalar.activation(y_sb[:, 0:512], banks[0][:], ACT.Copy).then_inc(y_act, 1)
                act.wait_ge(y_act, b + 1)
                act.wait_ge(y_dve, b + 1)
                act.dma_start(slot_out[bass.ds(b * P, P)], y_sb).then_inc(y_stored, 16)

            act.nop().then_inc(y_stored, 16)
            act.wait_ge(slots_zeroed, 16)
            act.wait_ge(hgT_done, 1)
            nc.scalar.activation(hgT[:, 0:4, :], banks[4][:].rearrange("p (j n) -> p j n", n=P),
                                 ACT.Copy).then_inc(hgT_act, 1)
            act.wait_ge(w13_done, 1)
            nc.scalar.activation(sil, banks[6][:, 0:DE], ACT.Silu).then_inc(silu_done, 1)
            copy_hgT(1)
            with act.Fori(0, more) as i:
                for p in (1, 0):
                    b = 2 * i + 2 - p
                    silu(b, p)
                    copy_hgT(b + 1)
                    store(2 * i + 1 - p)
            silu(2 * more + 1, 1)
            store(2 * more)
            store(2 * more + 1)
            act.wait_ge(gates_ready, 1)
            for t in range(TILES):
                act.wait_ge(back_in[t], 32)
                nc.scalar.activation(y_fin[t], y_in[t][0], ACT.Copy, scale=gates[:, 0, t:t + 1]).then_inc(fin_first, 1)
            act.wait_ge(new_out, 32)

        @block.vector
        def _(dve):
            done = [0]

            def link(ins):
                done[0] += 1
                ins.then_inc(dve_step, 1)
                dve.wait_ge(dve_step, done[0])

            V = nc.vector
            def split_lo(q):
                hi, lo = parts(q)
                w, arrival = slice_at(q)
                dve.wait_ge(*arrival)
                dve.wait_ge(hi_ready, q + 1)
                if q >= len(part_bufs):
                    dve.wait_ge(part_used, q - len(part_bufs) + 1)
                V.tensor_tensor(lo, w, hi.bitcast(F32), ALU.subtract).then_inc(lo_ready, 1)

            def copy_xT(t):
                dve.wait_ge(xT_done, t + 1)
                V.tensor_copy(hT[:, 4:8, t * P:(t + 1) * P], banks[2 * (t % 3) + 1][:].rearrange(
                    "p (k n) -> p k n", n=P)).then_inc(xT_dve, 1)

            dve.wait_ge(sil_hi, 1)
            V.tensor_tensor(sil_r[:, :, 1, :], silT, sil_r[:, :, 0, :].bitcast(F32), ALU.subtract).then_inc(sil_lo, 1)
            for t in range(TILES):
                dve.wait_ge(ss_ready, t + 1)
                V.tensor_scalar(xms[:, t:t + 1], xss[:, t:t + 1], 1.0 / D, EPS, ALU.mult, ALU.add).then_inc(ms_ready, 1)
                dve.wait_ge(rstd_ready, t + 1)
                V.tensor_scalar(x_sb[:, t, :], x_sb[:, t, :], xr[:, t:t + 1], None, ALU.mult).then_inc(xn_ready, 1)
                if t >= 2:
                    copy_xT(t - 2)
            copy_xT(TILES - 2)
            copy_xT(TILES - 1)
            dve.wait_ge(small_in, 32)
            for v in range(2):
                for half in range(2):
                    for k in range(KD):
                        split_lo((2 * v + half) * KD + k)
                    dve.wait_ge(part_used, (2 * v + half + 1) * KD)
                    if v and not half:
                        dve.wait_ge(col_done, v)
                    V.tensor_copy(ada_row[:, half * 512:(half + 1) * 512],
                                  banks[6 + half][0:2, :]).then_inc(ada_copied, 1)
                dve.wait_ge(col_done, v + 1)
                col = banks[5][:, 0:16].rearrange("p (k c) -> p k c", c=2)
                b = bcol[:, v, :].unsqueeze(2).to_broadcast((P, KD, 2))
                if v == 0:
                    V.tensor_tensor(colB, col, b, ALU.add).then_inc(cols_ready, 1)
                else:
                    link(V.tensor_tensor(colA, col, b, ALU.add))
                    link(V.tensor_scalar(colA, colA, 1.0, None, ALU.add))
                    V.tensor_tensor(colA, colA, n1w.unsqueeze(2).to_broadcast((P, KD, 2)), ALU.mult).then_inc(cols_ready, 1)
            dve.wait_ge(cols_ready, 2)
            dve.wait_ge(xT_act, TILES)
            dve.wait_ge(xT_dve, TILES)
            for cnd, ks in ((CTX, KD), (LAT, LAT_DVE)):
                ts = slice(0, P) if cnd == CTX else slice(P, TOK)
                for k in range(ks):
                    V.tensor_scalar(hT[:, k, ts], hT[:, k, ts], colA[:, k, cnd:cnd + 1], colB[:, k, cnd:cnd + 1],
                                    ALU.mult, ALU.add).then_inc(hT_dve, 1)
            dve.wait_ge(norms_in, 96)
            link(V.tensor_scalar(qw, qw, HD ** -0.5, None, ALU.mult))

            def norm_head(i):
                n = rows[i]
                kind = proj[n][1]
                r = raw[i % 2]
                dve.wait_ge(proj_out, n + 1)
                if kind == "gv":
                    g = r.rearrange("p (g n) -> p g n", g=GROUPS)
                    s = sq[i % 2].rearrange("p (g n) -> p g n", g=GROUPS)
                    link(V.tensor_reduce(mean, g, X, ALU.add))
                    link(V.tensor_scalar(mean, mean, -1.0 / P, None, ALU.mult))
                    link(V.tensor_tensor(g, g, mean.unsqueeze(2).to_broadcast((P, GROUPS, P)), ALU.add))
                    link(V.tensor_tensor(s, g, g, ALU.mult))
                    link(V.tensor_reduce(ssq[i % 2][:, 0:4], s, X, ALU.add))
                    V.tensor_scalar(msq[i % 2][:, 0:4], ssq[i % 2][:, 0:4], 1.0 / P, EPS, ALU.mult,
                                    ALU.add).then_inc(normed_ms, 1)
                else:
                    dve.wait_ge(raw_ready, i + 1)
                    link(V.tensor_reduce(ssq[i % 2], sq[i % 2].rearrange("p (h d) -> p h d", h=HEADS), X, ALU.add))
                    V.tensor_scalar(msq[i % 2], ssq[i % 2], 1.0 / HD, EPS, ALU.mult, ALU.add).then_inc(normed_ms, 1)

            def norm_tail(i):
                n = rows[i]
                _, kind, t = proj[n]
                r = raw[i % 2]
                dve.wait_ge(norm_rstd_ready, i + 1)
                g = GROUPS if kind == "gv" else HEADS
                rv = r.rearrange("p (g n) -> p g n", g=g)
                link(V.tensor_tensor(rv, rv, rsq[i % 2][:, 0:g].unsqueeze(2).to_broadcast((P, g, 512 // g)), ALU.mult))
                if kind == "gv":
                    link(V.tensor_tensor(r, r, lnw, ALU.mult))
                    V.tensor_tensor(vv[:, t, :], r, lnb, ALU.add).then_inc(raw_normed, 1)
                else:
                    V.tensor_tensor(r, r, qw if kind == "q" else kw, ALU.mult).then_inc(raw_normed, 1)

            def copy_nT(i):
                _, kind, t = proj[rows[i]]
                dve.wait_ge(nT_done, i + 1)
                V.tensor_copy((qT if kind == "q" else kT)[:, :, t * P:(t + 1) * P],
                              banks[4 + i % 2][:].rearrange("p (j n) -> p j n", n=P)).then_inc(nT_copied, 1)

            for i in range(len(rows)):
                norm_head(i)
                norm_tail(i)
                if 1 <= i <= 2 * TILES:
                    copy_nT(i - 1)
            dve.wait_ge(proj_out, len(proj))
            for t in range(TILES):
                dve.wait_ge(sgu_done, t + 1)
                s = sq[t % 2].rearrange("p (g n) -> p g n", g=GROUPS)
                link(V.tensor_tensor(s, banks[4 + t % 2][:].rearrange("p (g n) -> p g n", g=GROUPS),
                                     bsg.rearrange("p (g n) -> p g n", g=GROUPS), ALU.add))
                u = positions(uT, t)
                o = positions(catT[:, 4:8, :], t)
                for g in range(GROUPS):
                    ins = V.tensor_tensor(o[:, g], s[:, g].rearrange("p (r c) -> p r c", r=2), u[:, g], ALU.mult)
                ins.then_inc(sgu_out, 1)
            def ada_half(j):
                v, half = j // 2, j % 2
                if half == 0:
                    dve.wait_ge(row_in, 16 * (v - 1))
                    dve.wait_ge(n2_in, 16)
                    if v > 2:
                        dve.wait_ge(row_out, 16 * (v - 2))
                s = slice(half * 512, (half + 1) * 512)
                dve.wait_ge(ada_done, j - 3)
                V.tensor_tensor(ada_row[:, s], banks[7][0:2, :], bias_row[:, s], ALU.add).then_inc(ada_copied, 1)
                if j == 9:
                    dve.wait_ge(ada_copied, 10)
                    link(V.tensor_scalar(ada_row[:, :], ada_row[:, :], 1.0, None, ALU.add))
                    V.tensor_tensor(ada_row[:, :], ada_row[:, :], n2_row, ALU.mult).then_inc(row_ready, 1)

            def largest(n):
                t, h = steps[n]
                bank = 2 * (n % 2)
                p = n % 2
                dve.wait_ge(scored, n + 1)
                if t == 0:
                    link(V.tensor_reduce(m_ctx[:, p:p + 1], banks[bank + 1][:, 0:P], X, ALU.max))
                    V.tensor_scalar(nmax[:, p:p + 1], m_ctx[:, p:p + 1], -1.0, None, ALU.mult).then_inc(nmax_ready, 1)
                    return
                _, nt, piece = span(t)
                dve.wait_ge(bias_ready, {1: 2, 4: 7}.get(t, 5))
                V.tensor_tensor_reduce(out=win[p][:, 0:nt * P], in0=banks[bank][:, 0:nt * P],
                                       in1=bm[:, h, piece:piece + nt, :].rearrange("p v n -> p (v n)"),
                                       scale=1.0, scalar=-3e38, op0=ALU.add, op1=ALU.max,
                                       accum_out=m_win[:, p:p + 1]).then_inc(win_ready, 1)
                link(V.tensor_reduce(m_ctx[:, p:p + 1], banks[bank + 1][:, 0:CACHE], X, ALU.max))
                dve.wait_ge(win_ready, n - HEADS + 1)
                V.tensor_scalar(nmax[:, p:p + 1], m_ctx[:, p:p + 1], m_win[:, p:p + 1], -1.0, ALU.max,
                                ALU.mult).then_inc(nmax_ready, 1)

            def copy_pT(n):
                t, h = steps[n]
                nk = key_tiles(t)
                dve.wait_ge(pT_done, n + 1)
                if nk > 3:
                    if n >= 2:
                        dve.wait_ge(pv_done, n - 1)
                    V.tensor_copy(pT[n % 2][:, 3:nk, :], banks[5][:, 0:(nk - 3) * P].rearrange(
                        "p (j n) -> p j n", n=P)).then_inc(pT_dve, 1)

            def normalise(t):
                dve.wait_ge(exp_done, HEADS * (t + 1))
                if t:
                    dve.wait_ge(act_step, HEADS * t)
                    link(V.tensor_tensor(rsum, sums[:, t % 2, :, 0], sums[:, t % 2, :, 1], ALU.add))
                    link(V.reciprocal(rsum, rsum))
                else:
                    link(V.reciprocal(rsum, sums[:, 0, :, 1]))
                dve.wait_ge(pv_done, HEADS * (t + 1))
                if t:
                    dve.wait_ge(aT_done, t)
                V.tensor_tensor(o_row.rearrange("p (h d) -> p h d", h=HEADS),
                                banks[6][:].rearrange("p (h d) -> p h d", h=HEADS),
                                rsum.unsqueeze(2).to_broadcast((P, HEADS, HD)), ALU.mult).then_inc(o_ready, 1)

            for n in range(len(steps) + 2):
                if n < len(steps):
                    largest(n)
                if 1 <= n <= len(steps):
                    copy_pT(n - 1)
                for j in ada_ends.get(n - 1, ()):
                    ada_half(j)
                if n >= 2 and steps[n - 2][1] == HEADS - 1:
                    normalise(steps[n - 2][0])
            dve.wait_ge(g1_in, 32)
            dve.wait_ge(new_out, 32)

            def second_norm(t):
                cnd = LAT if t else CTX
                dve.wait_ge(ss2_ready, t + 1)
                V.tensor_scalar(xms[:, t:t + 1], xss[:, t:t + 1], 1.0 / D, EPS, ALU.mult, ALU.add).then_inc(ms2_ready, 1)
                dve.wait_ge(n_rstd2, t + 1)
                if t >= 2:
                    dve.wait_ge(h2T_done, t - 1)
                    dve.wait_ge(h2_out[t % 2], 16 * (t // 2))
                link(V.scalar_tensor_tensor(h2[t % 2], x_sb[:, t, :], xr[:, t:t + 1], bc[:, 1, cnd, :],
                                            ALU.mult, ALU.mult))
                V.tensor_tensor(h2[t % 2], h2[t % 2], bc[:, 0, cnd, :], ALU.add).then_inc(h2_ready, 1)
                dve.wait_ge(h2T_done, t + 1)
                if t:
                    dve.wait_ge(z_done, t)
                V.tensor_copy(h2T[:, 4:8, :], banks[5][:].rearrange("p (j n) -> p j n", n=P)).then_inc(h2T_dve, 1)

            for t in range(TILES):
                cnd = LAT if t else CTX
                dve.wait_ge(x_again, 16 * TILES)
                for half in range(2):
                    s = slice(half * 512, (half + 1) * 512)
                    dve.wait_ge(wout_done, 2 * t + half + 1)
                    link(V.tensor_tensor(sq[half], banks[(2 * t + half) % 4][:], g1b[:, cnd, s], ALU.mult))
                    V.tensor_tensor(x_sb[:, t, s], x_sb[:, t, s], sq[half], ALU.add).then_inc(x1_ready, 1)
                if t == 0:
                    dve.wait_ge(bc_in, 96)
                second_norm(t)

            def b3(a, n, w):
                return a.rearrange("p (t e) -> p t e", t=n)

            def wide(a, n, w):
                return a.unsqueeze(2).to_broadcast((P, n, w))

            dve.wait_ge(s_ready, 1)
            dve.wait_ge(bm_ready, 6)
            link(V.tensor_tensor(b3(sel, TILES, 16), b3(scores_s, TILES, 16),
                                 brt.unsqueeze(1).to_broadcast((P, TILES, EXPERTS)), ALU.add))
            s4 = sel.rearrange("p (g e) -> p g e", e=EPG)
            p6 = pair.rearrange("p (g e) -> p g e", e=6)
            V.tensor_tensor(p6[:, :, 0:3], s4[:, :, 0:3], s4[:, :, 1:4], ALU.add)
            V.tensor_tensor(p6[:, :, 3:5], s4[:, :, 0:2], s4[:, :, 2:4], ALU.add)
            link(V.tensor_tensor(p6[:, :, 5:6], s4[:, :, 0:1], s4[:, :, 3:4], ALU.add))
            link(V.tensor_reduce(gsc, p6, X, ALU.max))

            def first_largest(hot, val, n, t1, best, order):
                v3, h3, o3 = b3(val, TILES, n), b3(hot, TILES, n), b3(t1, TILES, n)
                link(V.tensor_reduce(best, v3, X, ALU.max))
                link(V.tensor_tensor(o3, v3, wide(best, TILES, n), ALU.is_ge))
                link(V.tensor_tensor(o3, o3, order.unsqueeze(1).to_broadcast((P, TILES, n)), ALU.mult))
                link(V.tensor_reduce(best, o3, X, ALU.max))
                link(V.tensor_tensor(h3, o3, wide(best, TILES, n), ALU.is_equal))

            first_largest(ghot, gsc, EG, gtmp, t5a, desc[:, EXPERTS - EG:])
            m4 = msel.rearrange("p (g e) -> p g e", e=EPG)
            link(V.tensor_tensor(m4, s4, wide(ghot, TILES * EG, EPG), ALU.mult))
            link(V.tensor_scalar(gtmp, ghot, 1.0, -NEG, ALU.subtract, ALU.mult))
            link(V.tensor_tensor(m4, m4, wide(gtmp, TILES * EG, EPG), ALU.add))
            first_largest(hot1, msel, EXPERTS, tmp, t5a, desc)
            link(V.scalar_tensor_tensor(msel, hot1, 3 * NEG, msel, ALU.mult, ALU.add))
            first_largest(hot2, msel, EXPERTS, tmp, t5a, desc)
            V.tensor_tensor(both[:, 0:TE], hot1, hot2, ALU.add).then_inc(m_ready, 1)
            dve.wait_ge(ranks_done, 1)
            count = banks[7][:, TE:TE + EXPERTS]
            link(V.tensor_scalar(nb, count, float(P), None, ALU.is_gt))
            for j in range(2, TILES):
                link(V.scalar_tensor_tensor(nb, count, float(j * P), nb, ALU.is_gt, ALU.add))
            link(V.tensor_tensor_scan(bend, ones[:, 0:EXPERTS], nb, 0.0, ALU.mult, ALU.add))
            link(V.tensor_tensor(bskip, bend, nb, ALU.subtract))
            link(V.scalar_tensor_tensor(bskip, bskip, float(P), next_blk, ALU.mult, ALU.add))
            ranks = b3(banks[7][:, 0:TE], TILES, 16)
            link(V.scalar_tensor_tensor(b3(rank, TILES, 16), ranks, P - 0.5,
                                        bskip.unsqueeze(1).to_broadcast((P, TILES, EXPERTS)), ALU.is_gt, ALU.mult))
            link(V.tensor_tensor(b3(rank, TILES, 16), b3(rank, TILES, 16), ranks, ALU.add))
            link(V.tensor_tensor(b3(rank, TILES, 16), b3(rank, TILES, 16),
                                 first_slot.unsqueeze(1).to_broadcast((P, TILES, EXPERTS)), ALU.add))
            link(V.tensor_tensor(tmp12.rearrange("p (k n) -> p k n", k=2), hot12.rearrange("p (k n) -> p k n", k=2),
                                 rank.unsqueeze(1).to_broadcast((P, 2, TE)), ALU.mult))
            link(V.tensor_reduce(slotf.rearrange("p (t k) -> p k t", k=2),
                                 tmp12.rearrange("p (k t e) -> p k t e", k=2, e=EXPERTS), X, ALU.add))
            link(V.tensor_copy(slot_u, slotf))
            link(V.tensor_scalar(blk_u, slot_u, 7, None, ALU.logical_shift_right))
            V.tensor_tensor(hot_b.rearrange("p (s b) -> p s b", s=10), wide(blk_u, 10, 28),
                            iota_b.unsqueeze(1).to_broadcast((P, 10, 28)), ALU.is_equal).then_inc(hot_b_ready, 1)
            link(V.tensor_scalar(place_u, slot_u, P - 1, None, ALU.bitwise_and))
            for half in range(2):
                ss = slice(5 * half, 5 * half + 5)
                V.tensor_tensor(hot_s.rearrange("p (s n) -> p s n", s=10)[:, ss], wide(place_u[:, ss], 5, P),
                                iota_p.unsqueeze(1).to_broadcast((P, 5, P)), ALU.is_equal).then_inc(hot_ready, 1)
            link(V.tensor_tensor(cmp_e.rearrange("p (b e) -> p b e", e=EXPERTS), wide(iota_b[:, 0:12], 12, EXPERTS),
                                 bend.unsqueeze(1).to_broadcast((P, 12, EXPERTS)), ALU.is_ge))
            link(V.tensor_reduce(ebf[:, EXPERTS:28], cmp_e.rearrange("p (b e) -> p b e", e=EXPERTS), X, ALU.add))
            link(V.tensor_scalar(ebf[:, EXPERTS:28], ebf[:, EXPERTS:28], float(EXPERTS - 1), None, ALU.min))
            link(V.tensor_copy(ebf[:, 0:EXPERTS], iota_b[:, 0:EXPERTS]))
            link(V.tensor_tensor(cmp_e[:, 0:5], iota_b[:, 0:10].rearrange("p (i k) -> p i k", k=2)[:, :, 0],
                                 bend[:, 15:16].to_broadcast((P, 5)), ALU.is_lt))
            link(V.tensor_reduce(ebf[:, 27:28], cmp_e[:, 0:5], X, ALU.add))
            link(V.tensor_scalar(ebf[:, 27:28], ebf[:, 27:28], float(SHARED), None, ALU.add))
            link(V.tensor_copy(ebi, ebf))
            dve.wait_ge(inv_done, 1)
            V.tensor_copy(gidx, banks[7][:, 128:156]).then_inc(table_ready, 1)
            for j, hot in enumerate((hot1, hot2)):
                link(V.tensor_tensor(tmp, scores_s, hot, ALU.mult))
                link(V.tensor_reduce(gate_s[:, 5 * j:5 * j + 5], b3(tmp, TILES, 16), X, ALU.add))
            link(V.tensor_tensor(t5a, gate_s[:, 0:5], gate_s[:, 5:10], ALU.add))
            link(V.reciprocal(t5b, t5a))
            link(V.tensor_tensor(gates, gate_s.rearrange("p (k t) -> p k t", k=2),
                                 t5b.unsqueeze(1).to_broadcast((P, 2, TILES)), ALU.mult))
            V.engine_nop().then_inc(gates_ready, 1)
            dve.wait_ge(table_ready, 1)
            more = dve.value_load(ebi[0:1, 27:28], min_val=SHARED, max_val=MAX_BLOCKS // 2 - 1)

            def copy_hgT(b):
                dve.wait_ge(hgT_done, b + 1)
                if not (isinstance(b, int) and b == 0):
                    dve.wait_ge(w13_done, b)
                V.tensor_copy(hgT[:, 4:8, :], banks[5][:].rearrange("p (j n) -> p j n", n=P)).then_inc(hgT_dve, 1)

            def hidden(b, p):
                dve.wait_ge(silu_done, b + 1)
                V.tensor_tensor(hid[p], banks[6 + p][:, DE:2 * DE], sil, ALU.mult).then_inc(hid_ready, 1)

            def copy_hidT(b):
                dve.wait_ge(hidT_done, b + 1)
                V.tensor_copy(hidT, banks[3][:, 0:2 * P].rearrange("p (j n) -> p j n", n=P)).then_inc(hidT_ready, 1)

            def copy_y(b):
                dve.wait_ge(y_done, b + 1)
                dve.wait_ge(y_stored, 16 * (b + 1))
                V.tensor_copy(y_sb[:, 512:1024], banks[1][:]).then_inc(y_dve, 1)

            V.engine_nop().then_inc(hid_ready, 1)
            copy_hgT(0)
            hidden(0, 0)
            copy_hgT(1)
            with dve.Fori(0, more) as i:
                for p in (1, 0):
                    b = 2 * i + 2 - p
                    hidden(b, p)
                    copy_hgT(b + 1)
                    copy_hidT(2 * i + 1 - p)
                    copy_y(2 * i + 1 - p)
            hidden(2 * more + 1, 1)
            for b in (2 * more, 2 * more + 1):
                copy_hidT(b)
                copy_y(b)
            for t in range(TILES):
                f = y_fin[t]
                dve.wait_ge(back_in[t], 32)
                dve.wait_ge(fin_first, t + 1)
                link(V.scalar_tensor_tensor(f, y_in[t][1], gates[:, 1, t:t + 1], f, ALU.mult, ALU.add))
                V.tensor_tensor(f, f, bc[:, 2, LAT if t else CTX, :], ALU.mult).then_inc(fin_moe, 1)
                if t >= POOL_TILES:
                    dve.wait_ge(fin_moe, t + 1)
                    V.tensor_tensor(f, f, x_sb[:, t, :], ALU.add).then_inc(fin_last, 1)

        @block.tensor
        def _(pe):
            T = nc.tensor

            def arrived(key):
                n = chunk_at[key]
                pe.wait_ge(ring_in[n % RING], 16 * (n // RING + 1))
                return ring[n % RING]

            def ada_slice(q, bank):
                k = q % KD
                hi, lo = parts(q)
                pe.wait_ge(hi_ready, q + 1)
                T.matmul(bank[0:2, :], sil_r[:, k, 0, :], hi, start=(k == 0), stop=False)
                T.matmul(bank[0:2, :], sil_r[:, k, 1, :], hi, start=False, stop=False)
                pe.wait_ge(lo_ready, q + 1)
                T.matmul(bank[0:2, :], sil_r[:, k, 0, :], lo, start=False, stop=(k == KD - 1)).then_inc(part_used, 1)

            def ada(j):
                if j >= 2:
                    pe.wait_ge(ada_copied, j - 1)
                for k in range(KD):
                    ada_slice(j * KD + k, banks[6 + j % 2])

            pe.wait_ge(consts_ready, 3)
            pe.wait_ge(ones_ready, 3)
            for t in range(TILES):
                pe.wait_ge(xn_ready, t + 1)
                if t >= 3:
                    pe.wait_ge(xT_act, t - 2)
                    pe.wait_ge(xT_dve, t - 2)
                xrow = x_sb[:, t, :].rearrange("p (c k) -> p k c", k=KD)
                for k in range(KD):
                    ins = T.transpose(banks[2 * (t % 3) + k // 4][:, (k % 4) * P:(k % 4 + 1) * P], xrow[:, k, :],
                                      ident[:])
                ins.then_inc(xT_done, 1)
            pe.wait_ge(sil_lo, 1)
            for v in range(2):
                for half in range(2):
                    ada(2 * v + half)
                pe.wait_ge(ada_copied, 2 * v + 2)
                if v:
                    pe.wait_ge(cols_ready, v)
                for k in range(KD):
                    ins = T.transpose(banks[5][:, 2 * k:2 * k + 2], ada_row[:, :].rearrange(
                        "c (p k) -> c k p", k=KD)[:, k, :], ident[0:2, 0:2])
                ins.then_inc(col_done, 1)
            def norm_T(i):
                pe.wait_ge(raw_normed, i + 1)
                if i >= 2:
                    pe.wait_ge(nT_copied, i - 1)
                for j in range(4):
                    ins = T.transpose(banks[4 + i % 2][:, j * P:(j + 1) * P], raw[i % 2][:, j * P:(j + 1) * P], ident[:])
                ins.then_inc(nT_done, 1)

            for n, (col, kind, t) in enumerate(proj):
                w = arrived(("in", col))
                if n == 0:
                    pe.wait_ge(hT_dve, KD)
                if n == 1:
                    pe.wait_ge(hT_dve, KD + LAT_DVE)
                    pe.wait_ge(hT_act, KD - LAT_DVE)
                bank = banks[n % 4]
                if n >= 4:
                    pe.wait_ge(proj_out, n - 3)
                if kind == "gv" and t == 1:
                    pe.wait_ge(by_row, KD)
                for k in range(KD):
                    if kind == "gu":
                        g, part = t
                        lo, hi = (0, P) if part == CTX else (P, TOK)
                        ins = T.matmul(bank[:, 0:hi - lo], w[:, k, g * P:(g + 1) * P], hT[:, k, lo:hi],
                                       start=(k == 0), stop=(k == KD - 1))
                    else:
                        if kind == "gv" and t:
                            lhs = hT_rows[:, k, (t - 1) * P:t * P]
                        else:
                            lhs = hT[:, k, t * P:(t + 1) * P]
                        ins = T.matmul(bank[:], lhs, w[:, k, :], start=(k == 0), stop=(k == KD - 1))
                ins.then_inc(proj_done, 1)
                if 1 <= n <= 2 * TILES:
                    norm_T(n - 1)
            pe.wait_ge(raw_normed, 3 * TILES)
            pe.wait_ge(norms_in, 96)
            pe.wait_ge(nT_copied, 2 * TILES)
            for t in range(TILES):
                if t >= 2:
                    pe.wait_ge(sgu_out, t - 1)
                for g in range(GROUPS):
                    ins = T.matmul(banks[4 + t % 2][:, g * P:(g + 1) * P], vv[:, t, g * P:(g + 1) * P],
                                   wsT[:, g * P:(g + 1) * P], start=True, stop=True)
                ins.then_inc(sgu_done, 1)
            def ada_part(j, k):
                if k == 0:
                    pe.wait_ge(ada_copied, j)
                w = arrived(("ada", j))
                ins = T.matmul(banks[7][0:2, :], silT[:, k, :], w[:, k, :], start=(k == 0), stop=(k == KD - 1))
                if k == KD - 1:
                    ins.then_inc(ada_done, 1)

            def scores(n):
                t, h = steps[n]
                hp, lo = h // 2, HD * (h % 2)
                bank = 2 * (n % 2)
                if n >= 2:
                    pe.wait_ge(exp_done, n - 1)
                q = qT[lo:lo + HD, hp, t * P:(t + 1) * P]
                if t == 0:
                    T.matmul(banks[bank + 1][:, 0:P], q, kT[lo:lo + HD, hp, 0:P], start=True,
                             stop=True).then_inc(scored, 1)
                    return
                first, nt, _ = span(t)
                T.matmul(banks[bank][:, 0:nt * P], q, kT[lo:lo + HD, hp, (1 + first) * P:(1 + first + nt) * P],
                         start=True, stop=True)
                T.matmul(banks[bank + 1][:, 0:CACHE], q, ckT[lo:lo + HD, hp, :], start=True,
                         stop=True).then_inc(scored, 1)

            def prob_T(n):
                t, h = steps[n]
                pe.wait_ge(exp_done, n + 1)
                if t:
                    pe.wait_ge(act_step, n - HEADS + 1)
                if n >= 1:
                    pe.wait_ge(pT_act, n)
                    if dve_copies(n - 1):
                        pe.wait_ge(pT_dve, dve_copies(n - 1))
                if n >= 2 and steps[n - 2][1] == HEADS - 1:
                    att_T(steps[n - 2][0])
                    pe.wait_ge(aT_copied, steps[n - 2][0] + 1)
                for j in range(key_tiles(t)):
                    bank, at_ = (4, j) if j < 3 else (5, j - 3)
                    ins = T.transpose(banks[bank][:, at_ * P:(at_ + 1) * P], probs[n % 2][:, j * P:(j + 1) * P], ident[:])
                ins.then_inc(pT_done, 1)

            def dve_copies(n):
                return sum(key_tiles(steps[m][0]) > 3 for m in range(n + 1))

            def values(n):
                t, h = steps[n]
                pe.wait_ge(pT_act, n + 1)
                if dve_copies(n):
                    pe.wait_ge(pT_dve, dve_copies(n))
                if h == 0 and t:
                    pe.wait_ge(o_ready, t)
                lo = h * HD
                nk = key_tiles(t)
                for j in range(nk):
                    if t == 0:
                        v = v_sb[:, 0, lo:lo + HD]
                    elif j < nk - 2:
                        v = v_sb[:, 1 + span(t)[0] + j, lo:lo + HD]
                    else:
                        v = cv[:, j - (nk - 2), lo:lo + HD]
                    ins = T.matmul(banks[6][:, lo:lo + HD], pT[n % 2][:, j, :], v, start=(j == 0),
                                   stop=(j == nk - 1))
                ins.then_inc(pv_done, 1)

            def att_T(t):
                pe.wait_ge(o_ready, t + 1)
                for j in range(4):
                    ins = T.transpose(banks[4][:, j * P:(j + 1) * P], o_row[:, j * P:(j + 1) * P], ident[:])
                ins.then_inc(aT_done, 1)

            pe.wait_ge(cache_in, 64)
            pe.wait_ge(sgu_out, TILES)
            scores(0)
            for n in range(len(steps)):
                if n + 1 < len(steps):
                    scores(n + 1)
                for part in ada_of[n][:1]:
                    ada_part(*part)
                prob_T(n)
                for part in ada_of[n][1:]:
                    ada_part(*part)
                if n:
                    values(n - 1)
            values(len(steps) - 1)
            att_T(TILES - 1)
            pe.wait_ge(exp_done, len(steps))
            pe.wait_ge(aT_copied, TILES)

            def router(t):
                pe.wait_ge(h2_ready, t + 1)
                if t:
                    pe.wait_ge(h2T_act, t)
                    pe.wait_ge(h2T_dve, t)
                hrow = h2[t % 2].rearrange("p (c k) -> p k c", k=KD)
                for k in range(KD):
                    ins = T.transpose(banks[4 + k // 4][:, (k % 4) * P:(k % 4 + 1) * P], hrow[:, k, :], ident[:])
                ins.then_inc(h2T_done, 1)
                pe.wait_ge(h2T_act, t + 1)
                pe.wait_ge(h2T_dve, t + 1)
                for k in range(KD):
                    ins = T.matmul(banks[6][:, t * EXPERTS:(t + 1) * EXPERTS], h2T[:, k, :], wr_sb[:, k, :],
                                   start=(k == 0), stop=(k == KD - 1))
                ins.then_inc(z_done, 1)

            arrived(("out", 0))
            arrived(("out", 1))
            for t in range(TILES):
                for half in range(2):
                    n = 2 * t + half
                    w = arrived(("out", half))
                    if n >= 4:
                        pe.wait_ge(x1_ready, n - 3)
                    for k in range(KD):
                        ins = T.matmul(banks[n % 4][:], catT[:, k, t * P:(t + 1) * P], w[:, k, :],
                                       start=(k == 0), stop=(k == KD - 1))
                    ins.then_inc(wout_done, 1)
                if t:
                    router(t - 1)
            router(TILES - 1)
            pe.wait_ge(m_ready, 1)
            T.matmul(banks[7][:, 0:TE + EXPERTS], before[:], both, start=True, stop=False)
            for u in range(TILES):
                ins = T.matmul(banks[7][:, (u + 1) * EXPERTS:TE + EXPERTS].rearrange("p (t e) -> p t e", e=EXPERTS),
                               ones_b[:], both[:, u * EXPERTS:(u + 1) * EXPERTS].unsqueeze(1).to_broadcast(
                                   (P, TILES - u, EXPERTS)), start=False, stop=(u == TILES - 1))
            ins.then_inc(ranks_done, 1)
            pe.wait_ge(hot_b_ready, 2)
            for s in range(10):
                if s % 5 == 0:
                    pe.wait_ge(hot_ready, s // 5 + 1)
                ins = T.matmul(banks[7][:, 128:156], hot_s[:, s * P:(s + 1) * P], hot_bt[:, s * 28:(s + 1) * 28],
                               start=(s == 0), stop=(s == 9))
            ins.then_inc(inv_done, 1)
            pe.wait_ge(table_ready, 1)
            more = pe.value_load(ebi[0:1, 27:28], min_val=SHARED, max_val=MAX_BLOCKS // 2 - 1)

            def token_T(b, p, half):
                pe.wait_ge(hg_in[p], 16 * (half + 1))
                if not (isinstance(b, int) and b == 0):
                    pe.wait_ge(hgT_act, b)
                    pe.wait_ge(hgT_dve, b)
                hrow = hg[p].rearrange("p (c k) -> p k c", k=KD)
                for k in range(KD):
                    ins = T.transpose(banks[4 + k // 4][:, (k % 4) * P:(k % 4 + 1) * P], hrow[:, k, :], ident[:])
                ins.then_inc(hgT_done, 1)

            def up(b, p, half):
                pe.wait_ge(hgT_act, b + 1)
                pe.wait_ge(hgT_dve, b + 1)
                pe.wait_ge(w13_in[p], 32 * (half + 1))
                if not (isinstance(b, int) and b == 0):
                    pe.wait_ge(hid_ready, b)
                for k in range(KD):
                    ins = T.matmul(banks[6 + p][:], hgT[:, k, :], w13[p][:, k, :], start=(k == 0), stop=(k == KD - 1))
                ins.then_inc(w13_done, 1)

            def down(b, p, half):
                pe.wait_ge(hid_ready, b + 2)
                hrow = hid[p].rearrange("p (c k) -> p k c", k=2)
                for k in range(2):
                    ins = T.transpose(banks[3][:, k * P:(k + 1) * P], hrow[:, k, :], ident[:])
                ins.then_inc(hidT_done, 1)
                pe.wait_ge(hidT_ready, b + 1)
                pe.wait_ge(w2_in[p], 16 * (half + 1))
                if not (isinstance(b, int) and b == 0):
                    pe.wait_ge(y_act, b)
                    pe.wait_ge(y_dve, b)
                for n in range(2):
                    for k in range(2):
                        ins = T.matmul(banks[n][:], hidT[:, k, :], w2s[p][:, k, n * 512:(n + 1) * 512],
                                       start=(k == 0), stop=(k == 1))
                ins.then_inc(y_done, 1)

            token_T(0, 0, 0)
            up(0, 0, 0)
            token_T(1, 1, 0)
            with pe.Fori(0, more) as i:
                up(2 * i + 1, 1, i)
                token_T(2 * i + 2, 0, i + 1)
                down(2 * i, 0, i)
                up(2 * i + 2, 0, i + 1)
                token_T(2 * i + 3, 1, i + 1)
                down(2 * i + 1, 1, i)
            up(2 * more + 1, 1, more)
            down(2 * more, 0, more)
            down(2 * more + 1, 1, more)


_INS = ("x_prompt", "x_sample", "cache_kt", "cache_v", "c", "c_ctx", "w_ada", "b_ada", "norm1_w", "norm2_w", "w_in",
        "q_norm_w", "k_norm_w", "rpb_runs", "w_sgu_t", "b_sgu", "ln_w", "ln_b", "w_out", "w_router", "b_router", "w1",
        "w3", "w2")
_OUTS = (("y_prompt", (P, D)), ("y_sample", (4 * P, D)), ("new_k", (P, AW)), ("new_v", (P, AW)))


def kernel(x_prompt, x_sample, cache_k, cache_v, c, c_ctx, w_ada, b_ada, norm1_w, norm2_w, w_in, q_norm_w, k_norm_w,
           rpb, w_sgu, b_sgu, sgu_ln_w, sgu_ln_b, w_out, w_router, b_router, w1, w3, w2):
    import concourse.bacc as bacc
    import numpy as np
    from concourse.bass_utils import run_bass_kernel_spmd

    def a(x, *shape):
        return np.ascontiguousarray(np.asarray(x).reshape(shape))

    rpb_flat = np.zeros(2 * RPB_PAD + np.asarray(rpb).size, np.asarray(rpb).dtype)
    rpb_flat[RPB_PAD:-RPB_PAD] = np.asarray(rpb).ravel()
    rpb_runs = np.empty((P, HEADS, RUN), rpb_flat.dtype)
    for p in range(P):
        for h in range(HEADS):
            at = RPB_PAD + (h * RPB_H + GRID_H - 1 - p % GRID_H) * RPB_W - p // GRID_H - 1
            rpb_runs[p, h] = rpb_flat[at:at + RUN]
    arrays = {
        "x_prompt": a(x_prompt, P, D),
        "x_sample": np.ascontiguousarray(a(x_sample, GRID_H, GRID_W, D).transpose(1, 0, 2)).reshape(4 * P, D),
        "cache_kt": np.ascontiguousarray(a(cache_k, CACHE, 4, P).transpose(2, 1, 0)),
        "cache_v": a(cache_v, CACHE, AW), "c": a(c, D), "c_ctx": a(c_ctx, D), "w_ada": a(w_ada, D, 6 * D),
        "b_ada": a(b_ada, 6 * D), "norm1_w": a(norm1_w, D), "norm2_w": a(norm2_w, D), "w_in": a(w_in, D, 5 * AW),
        "q_norm_w": a(q_norm_w, HD), "k_norm_w": a(k_norm_w, HD), "rpb_runs": rpb_runs,
        "w_sgu_t": np.ascontiguousarray(a(w_sgu, GROUPS, P, P).transpose(2, 0, 1)).reshape(P, GROUPS * P),
        "b_sgu": a(b_sgu, GROUPS * P), "ln_w": a(sgu_ln_w, AW), "ln_b": a(sgu_ln_b, AW), "w_out": a(w_out, D, D),
        "w_router": a(w_router, D, EXPERTS), "b_router": a(b_router, EXPERTS), "w1": a(w1, EXPERTS, D, DE),
        "w3": a(w3, EXPERTS, D, DE), "w2": a(w2, EXPERTS, DE, D),
    }
    nc = bacc.Bacc("TRN2", target_bir_lowering=False, num_devices=1)
    ins = [nc.dram_tensor(n, arrays[n].shape, mybir.dt.from_np(arrays[n].dtype), kind="ExternalInput").ap()
           for n in _INS]
    outs = [nc.dram_tensor(n, shape, F32, kind="ExternalOutput").ap() for n, shape in _OUTS]
    build(nc, ins, outs)
    r = run_bass_kernel_spmd(nc, [arrays], core_ids=[0]).results[0]
    y_sample = r["y_sample"].reshape(GRID_W, GRID_H, D).transpose(1, 0, 2).reshape(1, 4 * P, D)
    return (r["y_prompt"].reshape(1, P, D), np.ascontiguousarray(y_sample), r["new_k"].reshape(1, 1, P, HEADS, HD),
            r["new_v"].reshape(1, 1, P, HEADS, HD))
```
